# Optimizing a Trainium2 kernel written in Bass

```python
import math
import jax
import jax.numpy as jnp
from jax import lax
import numpy as np
import jax, jax.numpy as jnp

D_MODEL = 1024
BATCH = 1
SEQ = 512
DEPTH = 1

HEAD_DIM = 64
NSA_HEADS = 8
NSA_KV_GROUPS = 2
SWA_HEADS = 8
SWA_KV_GROUPS = 2
FOX_HEADS = 8
MIX_WIDTH = 8 * HEAD_DIM
N_BRANCH = 3
Q_BLOCK = 128
CMP_LEN = 32
CMP_STRIDE = 16
CMP_HIDDEN = 256
SLC_LEN = 64
SLC_TOPK = 8
NSA_WINDOW = 256
SWA_WINDOW = 128
N_BUCKETS = 32
MAX_DISTANCE = 128
D_FF = 256 * ((8 * D_MODEL // 3 + 255) // 256)
CONV_WIDTH = 3
RMS_EPS = 1e-6
NEG_INF = -1e30
FORCE_SCORE = 1e9
N_QK_GAINS = 6

KV_A = NSA_KV_GROUPS * HEAD_DIM
KV_B = SWA_KV_GROUPS * HEAD_DIM
IN_SPLITS = (
    ('a_q', NSA_HEADS * HEAD_DIM), ('a_kc', KV_A), ('a_vc', KV_A), ('a_ks', KV_A), ('a_vs', KV_A),
    ('a_kw', KV_A), ('a_vw', KV_A), ('a_gate', NSA_HEADS * 3),
    ('b_q', SWA_HEADS * HEAD_DIM), ('b_k', KV_B), ('b_v', KV_B),
    ('c_q', FOX_HEADS * HEAD_DIM), ('c_k', FOX_HEADS * HEAD_DIM), ('c_v', FOX_HEADS * HEAD_DIM),
    ('c_f', FOX_HEADS),
    ('merge', N_BRANCH * D_MODEL),
)
IN_WIDTH = sum(w for _, w in IN_SPLITS)


def rms_norm(x, g):
    xf = x.astype(jnp.float32)
    return (xf * lax.rsqrt(jnp.mean(xf * xf, axis=-1, keepdims=True) + RMS_EPS)).astype(x.dtype) * g

def split_columns(h):
    cols, off = {}, 0
    for name, w in IN_SPLITS:
        cols[name] = h[..., off:off + w]
        off += w
    return cols

def to_heads(z, n_heads):
    b, t, _ = z.shape
    return z.reshape(b, t, n_heads, HEAD_DIM).transpose(0, 2, 1, 3)

def from_heads(z):
    b, h, t, d = z.shape
    return z.transpose(0, 2, 1, 3).reshape(b, t, h * d)

def t5_bucket(dist):
    max_exact = N_BUCKETS // 2
    d = jnp.maximum(dist, 0)
    log_ratio = jnp.log(jnp.maximum(d, 1).astype(jnp.float32) / max_exact) / math.log(MAX_DISTANCE / max_exact)
    large = jnp.minimum(max_exact + (log_ratio * (N_BUCKETS - max_exact)).astype(jnp.int32), N_BUCKETS - 1)
    return jnp.where(d < max_exact, d, large)

def banded_kv(z, n_prev):
    b, g, t, d = z.shape
    nb = t // Q_BLOCK
    zb = jnp.pad(z.reshape(b, g, nb, Q_BLOCK, d), ((0, 0), (0, 0), (n_prev, 0), (0, 0), (0, 0)))
    return jnp.concatenate([zb[:, :, j:j + nb] for j in range(n_prev + 1)], axis=3)

def banded_attention(q, k, v, window, tab, sinks):
    b, g, r, t, d = q.shape
    nb = t // Q_BLOCK
    n_prev = -(-(window - 1) // Q_BLOCK)
    n_keys = (n_prev + 1) * Q_BLOCK
    kb, vb = banded_kv(k, n_prev), banded_kv(v, n_prev)
    qb = q.reshape(b, g, r, nb, Q_BLOCK, d)
    qi = jnp.arange(Q_BLOCK)[:, None]
    ki = jnp.arange(n_keys)[None, :]
    dist = n_prev * Q_BLOCK + qi - ki
    s_pos = (jnp.arange(nb)[:, None, None] - n_prev) * Q_BLOCK + ki[None]
    valid = (dist >= 0) & (dist < window) & (s_pos >= 0)
    bias = jnp.transpose(tab[t5_bucket(dist)], (2, 3, 0, 1))[:, :, None]
    logits = jnp.einsum('bgrnqd,bgnkd->bgrnqk', qb, kb).astype(jnp.float32) * (HEAD_DIM ** -0.5) + bias
    logits = jnp.where(valid, logits, NEG_INF)
    if sinks is None:
        probs = jax.nn.softmax(logits, axis=-1)
    else:
        sink_col = jnp.broadcast_to(sinks.astype(jnp.float32).reshape(g, r, 1, 1, 1), logits.shape[:-1] + (1,))
        probs = jax.nn.softmax(jnp.concatenate([logits, sink_col], axis=-1), axis=-1)[..., :-1]
    out = jnp.einsum('bgrnqk,bgnkd->bgrnqd', probs.astype(v.dtype), vb)
    return out.reshape(b, g, r, t, d)

def nsa_mixer(cols, q_g, k_g, cmp_pos, cmp_w1, cmp_w2, tab_flat):
    b, t, _ = cols['a_q'].shape
    G, R = NSA_KV_GROUPS, NSA_HEADS // NSA_KV_GROUPS
    scale = HEAD_DIM ** -0.5
    tab = tab_flat.reshape(N_BUCKETS, G, R)
    q = rms_norm(to_heads(cols['a_q'], NSA_HEADS), q_g).reshape(b, G, R, t, HEAD_DIM)
    kc, vc = to_heads(cols['a_kc'], G), to_heads(cols['a_vc'], G)
    ks, vs = rms_norm(to_heads(cols['a_ks'], G), k_g), to_heads(cols['a_vs'], G)
    kw, vw = rms_norm(to_heads(cols['a_kw'], G), k_g), to_heads(cols['a_vw'], G)
    pos_t = jnp.arange(t)

    n_cmp = (t - CMP_LEN) // CMP_STRIDE + 1
    win_idx = jnp.arange(n_cmp)[:, None] * CMP_STRIDE + jnp.arange(CMP_LEN)[None, :]

    def compress(z, which):
        blk = z[:, :, win_idx] + cmp_pos[which]
        hid = jax.nn.gelu(blk.reshape(b, G, n_cmp, CMP_LEN * HEAD_DIM) @ cmp_w1[which])
        return hid @ cmp_w2[which]

    k_cmp = rms_norm(compress(kc, 0), k_g)
    v_cmp = compress(vc, 1)
    blk_end = jnp.arange(n_cmp) * CMP_STRIDE + CMP_LEN - 1
    dist_c = pos_t[:, None] - blk_end[None, :]
    valid_c = dist_c >= 0
    bias_c = jnp.transpose(tab[t5_bucket(dist_c)], (2, 3, 0, 1))
    logits_c = jnp.einsum('bgrtd,bgnd->bgrtn', q, k_cmp).astype(jnp.float32) * scale + bias_c
    logits_c = jnp.where(valid_c, logits_c, NEG_INF)
    p_cmp = jax.nn.softmax(logits_c, axis=-1) * jnp.any(valid_c, axis=-1)[:, None]
    o_cmp = jnp.einsum('bgrtn,bgnd->bgrtd', p_cmp.astype(v_cmp.dtype), v_cmp)

    n_slc = t // SLC_LEN
    n_top = min(SLC_TOPK, n_slc)
    c_start = jnp.arange(n_cmp) * CMP_STRIDE
    s_start = jnp.arange(n_slc) * SLC_LEN
    overlap = ((c_start[:, None] < s_start[None, :] + SLC_LEN)
               & (c_start[:, None] + CMP_LEN > s_start[None, :])).astype(jnp.float32)
    importance = jnp.einsum('bgtn,nj->bgtj', p_cmp.sum(axis=2), overlap)
    cur = pos_t // SLC_LEN
    jblk = jnp.arange(n_slc)[None, :]
    valid_s = jblk <= cur[:, None]
    forced = (jblk == 0) | (jblk == cur[:, None]) | (jblk == cur[:, None] - 1)
    score = jnp.where(valid_s, jnp.where(forced, FORCE_SCORE, importance), NEG_INF)
    top_score, top_idx = lax.top_k(score, n_top)
    top_ok = top_score > NEG_INF / 2

    nb = t // Q_BLOCK
    ks_blk = ks.reshape(b, G, n_slc, SLC_LEN, HEAD_DIM)
    vs_blk = vs.reshape(b, G, n_slc, SLC_LEN, HEAD_DIM)
    q_b = jnp.moveaxis(q.reshape(b, G, R, nb, Q_BLOCK, HEAD_DIM), 3, 0)
    idx_b = jnp.moveaxis(top_idx.reshape(b, G, nb, Q_BLOCK, n_top), 2, 0)
    ok_b = jnp.moveaxis(top_ok.reshape(b, G, nb, Q_BLOCK, n_top), 2, 0)
    gather = jax.vmap(jax.vmap(lambda blocks, ix: blocks[ix]))
    bias_lookup = jax.vmap(lambda tb, bk: tb[bk], in_axes=(1, 1), out_axes=1)
    n_sel = n_top * SLC_LEN

    def selected_block(args):
        i, qi, ix, ok = args
        kg = gather(ks_blk, ix).reshape(b, G, Q_BLOCK, n_sel, HEAD_DIM)
        vg = gather(vs_blk, ix).reshape(b, G, Q_BLOCK, n_sel, HEAD_DIM)
        t_pos = i * Q_BLOCK + jnp.arange(Q_BLOCK)
        s_pos = (ix[..., None] * SLC_LEN + jnp.arange(SLC_LEN)).reshape(b, G, Q_BLOCK, n_sel)
        dist = t_pos[:, None] - s_pos
        valid = (dist >= 0) & jnp.repeat(ok, SLC_LEN, axis=-1)
        bias = jnp.moveaxis(bias_lookup(tab, t5_bucket(dist)), -1, 2)
        logits = jnp.einsum('bgrqd,bgqkd->bgrqk', qi, kg).astype(jnp.float32) * scale + bias
        logits = jnp.where(valid[:, :, None], logits, NEG_INF)
        probs = jax.nn.softmax(logits, axis=-1)
        return jnp.einsum('bgrqk,bgqkd->bgrqd', probs.astype(vg.dtype), vg)

    o_slc = lax.map(selected_block, (jnp.arange(nb), q_b, idx_b, ok_b))
    o_slc = jnp.moveaxis(o_slc, 0, 3).reshape(b, G, R, t, HEAD_DIM)

    o_win = banded_attention(q, kw, vw, NSA_WINDOW, tab, None)

    gate = jax.nn.sigmoid(cols['a_gate']).reshape(b, t, NSA_HEADS, 3).transpose(0, 2, 1, 3)
    gate = gate.reshape(b, G, R, t, 3)
    o = gate[..., 0:1] * o_cmp + gate[..., 1:2] * o_slc + gate[..., 2:3] * o_win
    return from_heads(o.reshape(b, NSA_HEADS, t, HEAD_DIM))

def swa_mixer(cols, q_g, k_g, sinks, tab_flat):
    b, t, _ = cols['b_q'].shape
    G, R = SWA_KV_GROUPS, SWA_HEADS // SWA_KV_GROUPS
    q = rms_norm(to_heads(cols['b_q'], SWA_HEADS), q_g).reshape(b, G, R, t, HEAD_DIM)
    k = rms_norm(to_heads(cols['b_k'], G), k_g)
    v = to_heads(cols['b_v'], G)
    o = banded_attention(q, k, v, SWA_WINDOW, tab_flat.reshape(N_BUCKETS, G, R), sinks.reshape(G, R))
    return from_heads(o.reshape(b, SWA_HEADS, t, HEAD_DIM))

def fox_mixer(cols, q_g, k_g, forget_bias):
    b, t, _ = cols['c_q'].shape
    q = rms_norm(to_heads(cols['c_q'], FOX_HEADS), q_g)
    k = rms_norm(to_heads(cols['c_k'], FOX_HEADS), k_g)
    v = to_heads(cols['c_v'], FOX_HEADS)
    log_f = jax.nn.log_sigmoid((cols['c_f'] + forget_bias).astype(jnp.float32))
    c = jnp.cumsum(log_f, axis=1).transpose(0, 2, 1)
    nb = t // Q_BLOCK
    q_b = jnp.moveaxis(q.reshape(b, FOX_HEADS, nb, Q_BLOCK, HEAD_DIM), 2, 0)
    c_b = jnp.moveaxis(c.reshape(b, FOX_HEADS, nb, Q_BLOCK), 2, 0)
    key_pos = jnp.arange(t)

    def query_block(args):
        i, qi, ci = args
        t_pos = i * Q_BLOCK + jnp.arange(Q_BLOCK)
        logits = (jnp.einsum('bhqd,bhsd->bhqs', qi, k).astype(jnp.float32) * (HEAD_DIM ** -0.5)
                  + ci[..., None] - c[:, :, None, :])
        logits = jnp.where(t_pos[:, None] >= key_pos[None, :], logits, NEG_INF)
        probs = jax.nn.softmax(logits, axis=-1)
        return jnp.einsum('bhqs,bhsd->bhqd', probs.astype(v.dtype), v)

    o = lax.map(query_block, (jnp.arange(nb), q_b, c_b))
    o = jnp.moveaxis(o, 0, 2).reshape(b, FOX_HEADS, t, HEAD_DIM)
    return from_heads(o)

def conv_ffn(h, w_gate, w_up, conv_w, conv_b, w_down):
    a = h @ w_gate
    a = lax.conv_general_dilated(a, conv_w[:, None, :], window_strides=(1,),
                                 padding=[(CONV_WIDTH - 1, 0)],
                                 dimension_numbers=('NWC', 'WIO', 'NWC'),
                                 feature_group_count=a.shape[-1]) + conv_b
    return (jax.nn.gelu(a) * (h @ w_up)) @ w_down

def first_inputs(seed: int = 0) -> dict:
    key = jax.random.key(seed)
    ks = jax.random.split(key, 19)
    L, D, F, d = DEPTH, D_MODEL, D_FF, HEAD_DIM
    nrm = jax.random.normal
    return {
        'x': nrm(ks[0], (BATCH, SEQ, D), jnp.float32),
        'rel_bias': 0.5 * nrm(ks[1], (N_BUCKETS, NSA_HEADS + SWA_HEADS), jnp.float32),
        'norm_mix': 1.0 + 0.05 * nrm(ks[2], (L, D), jnp.float32),
        'norm_ffn': 1.0 + 0.05 * nrm(ks[3], (L, D), jnp.float32),
        'w_in': nrm(ks[4], (L, D, IN_WIDTH), jnp.float32) * D ** -0.5,
        'forget_bias': 4.0 + 0.5 * nrm(ks[5], (L, FOX_HEADS), jnp.float32),
        'qk_gain': 1.0 + 0.05 * nrm(ks[6], (L, N_QK_GAINS, d), jnp.float32),
        'cmp_pos': 0.1 * nrm(ks[7], (L, 2, CMP_LEN, d), jnp.float32),
        'cmp_w1': nrm(ks[8], (L, 2, CMP_LEN * d, CMP_HIDDEN), jnp.float32) * (CMP_LEN * d) ** -0.5,
        'cmp_w2': nrm(ks[9], (L, 2, CMP_HIDDEN, d), jnp.float32) * CMP_HIDDEN ** -0.5,
        'sinks': nrm(ks[10], (L, SWA_HEADS), jnp.float32),
        'w_branch': nrm(ks[11], (L, N_BRANCH, MIX_WIDTH, D), jnp.float32) * MIX_WIDTH ** -0.5,
        'w_out': nrm(ks[12], (L, D, D), jnp.float32) * D ** -0.5,
        'w_gate': nrm(ks[13], (L, D, F), jnp.float32) * D ** -0.5,
        'w_up': nrm(ks[14], (L, D, F), jnp.float32) * D ** -0.5,
        'conv_w': nrm(ks[15], (L, CONV_WIDTH, F), jnp.float32) * CONV_WIDTH ** -0.5,
        'conv_b': 0.02 * nrm(ks[16], (L, F), jnp.float32),
        'w_down': nrm(ks[17], (L, F, D), jnp.float32) * F ** -0.5,
    }

def first_block(x, rel_bias, norm_mix, norm_ffn, w_in, forget_bias, qk_gain, cmp_pos, cmp_w1, cmp_w2,
              sinks, w_branch, w_out, w_gate, w_up, conv_w, conv_b, w_down):
    b, t, _ = x.shape
    for l in range(DEPTH):
        h = rms_norm(x, norm_mix[l])
        cols = split_columns(h @ w_in[l])
        o_a = nsa_mixer(cols, qk_gain[l, 0], qk_gain[l, 1], cmp_pos[l], cmp_w1[l], cmp_w2[l],
                        rel_bias[:, :NSA_HEADS])
        o_b = swa_mixer(cols, qk_gain[l, 2], qk_gain[l, 3], sinks[l], rel_bias[:, NSA_HEADS:])
        o_c = fox_mixer(cols, qk_gain[l, 4], qk_gain[l, 5], forget_bias[l])
        branches = jnp.stack([o_a, o_b, o_c], axis=2)
        proj = jnp.einsum('btnm,nmd->btnd', branches, w_branch[l])
        gates = jax.nn.sigmoid(cols['merge']).reshape(b, t, N_BRANCH, D_MODEL)
        x = x + (gates * proj).sum(axis=2) @ w_out[l]
        x = x + conv_ffn(rms_norm(x, norm_ffn[l]), w_gate[l], w_up[l], conv_w[l], conv_b[l], w_down[l])
    return x


DEPTH_2 = 2

GRID_W = 64
N_Q_HEADS = 8
N_KV_HEADS = 2
ROPE_THETA = 10000.0
ATTN_WIDTH = N_Q_HEADS * HEAD_DIM
KV_WIDTH = N_KV_HEADS * HEAD_DIM
SGU_GROUPS = 8
SGU_WIDTH = 512
SGU_GROUP_DIM = SGU_WIDTH // SGU_GROUPS
SGU_CHUNK = 128
Q_END = ATTN_WIDTH
K_END = Q_END + KV_WIDTH
V_END = K_END + KV_WIDTH
Z_END = V_END + 2 * SGU_WIDTH
GA_END = Z_END + D_MODEL
IN_COLS = GA_END + D_MODEL
N_EXPERTS = 64
TOP_K = 8
N_GROUPS = 8
TOPK_GROUPS = 4
EXPERT_FF = 256
SHARED_FF = 256
ROUTED_SCALE = 2.5
MOE_BLOCK = 128
ALPHA = (2 * DEPTH_2) ** 0.25
BETA = (8 * DEPTH_2) ** -0.25


def layer_norm(x, g, b, eps=1e-5):
    xf = x.astype(jnp.float32)
    mu = jnp.mean(xf, -1, keepdims=True)
    var = jnp.mean(jnp.square(xf - mu), -1, keepdims=True)
    return ((xf - mu) * lax.rsqrt(var + eps)).astype(x.dtype) * g + b

def rms_norm_2(x, g, eps=1e-6):
    xf = x.astype(jnp.float32)
    return (xf * lax.rsqrt(jnp.mean(jnp.square(xf), -1, keepdims=True) + eps)).astype(x.dtype) * g

def axial_rope_tables(seq_len, rows):
    t = jnp.arange(seq_len)
    row = (t // GRID_W - rows // 2).astype(jnp.float32)
    col = (t % GRID_W - GRID_W // 2).astype(jnp.float32)
    n_pairs = HEAD_DIM // 4
    inv_freq = ROPE_THETA ** (-jnp.arange(n_pairs, dtype=jnp.float32) / n_pairs)
    ang = jnp.concatenate([row[:, None] * inv_freq, col[:, None] * inv_freq], -1)
    return jnp.cos(ang), jnp.sin(ang)

def apply_rope(x, cos, sin):
    xf = x.astype(jnp.float32).reshape(*x.shape[:-1], HEAD_DIM // 2, 2)
    x0, x1 = xf[..., 0], xf[..., 1]
    c = cos[None, :, None, :]
    s = sin[None, :, None, :]
    out = jnp.stack([x0 * c - x1 * s, x0 * s + x1 * c], -1)
    return out.reshape(x.shape).astype(x.dtype)

def attention_branch(q, k, v, q_scale, k_scale, cos, sin):
    B, S = q.shape[:2]
    grp = N_Q_HEADS // N_KV_HEADS
    q = apply_rope(rms_norm_2(q, q_scale), cos, sin)
    k = apply_rope(rms_norm_2(k, k_scale), cos, sin)
    nqb = S // Q_BLOCK
    qb = q.reshape(B, nqb, Q_BLOCK, N_KV_HEADS, grp, HEAD_DIM).transpose(1, 0, 3, 4, 2, 5)
    kt = k.transpose(0, 2, 1, 3)
    vt = v.transpose(0, 2, 1, 3)
    scale = HEAD_DIM ** -0.5

    def attend(q_blk):
        s = jnp.einsum('bkgqd,bksd->bkgqs', q_blk, kt).astype(jnp.float32) * scale
        p = jax.nn.softmax(s, axis=-1).astype(vt.dtype)
        return jnp.einsum('bkgqs,bksd->bkgqd', p, vt)

    o = lax.map(attend, qb)
    return o.transpose(1, 0, 4, 2, 3, 5).reshape(B, S, ATTN_WIDTH)

def spatial_gating_branch(z, ln_g, ln_b, w_s, b_s):
    B, S, _ = z.shape
    z = jax.nn.gelu(z, approximate=False)
    u, v = z[..., :SGU_WIDTH], z[..., SGU_WIDTH:]
    v = layer_norm(v, ln_g, ln_b)
    vc = v.reshape(B, S // SGU_CHUNK, SGU_CHUNK, SGU_GROUPS, SGU_GROUP_DIM)
    sv = jnp.einsum('gij,bnjgd->bnigd', w_s, vc) + b_s.T[:, :, None]
    return u * sv.reshape(B, S, SGU_WIDTH)

def token_mixer(h, w_in, q_scale, k_scale, sgu_ln_g, sgu_ln_b, w_s, b_s, w_branch_a, w_branch_b, w_out, cos, sin):
    B, S, _ = h.shape
    p = h @ w_in
    q = p[..., :Q_END].reshape(B, S, N_Q_HEADS, HEAD_DIM)
    k = p[..., Q_END:K_END].reshape(B, S, N_KV_HEADS, HEAD_DIM)
    v = p[..., K_END:V_END].reshape(B, S, N_KV_HEADS, HEAD_DIM)
    z = p[..., V_END:Z_END]
    gate_a = p[..., Z_END:GA_END]
    gate_b = p[..., GA_END:]
    o_a = attention_branch(q, k, v, q_scale, k_scale, cos, sin)
    o_b = spatial_gating_branch(z, sgu_ln_g, sgu_ln_b, w_s, b_s)
    y = jax.nn.sigmoid(gate_a) * (o_a @ w_branch_a) + jax.nn.sigmoid(gate_b) * (o_b @ w_branch_b)
    return y @ w_out

def moe_ffn(h, router_w, router_bias, w_gate, w_up, w_down, ws_gate, ws_up, ws_down):
    B, S, D = h.shape
    T = B * S
    xt = h.reshape(T, D)
    scores = jax.nn.sigmoid((xt @ router_w).astype(jnp.float32))
    sel = scores + router_bias.astype(jnp.float32)
    per_group = N_EXPERTS // N_GROUPS
    group_score = lax.top_k(sel.reshape(T, N_GROUPS, per_group), 2)[0].sum(-1)
    _, gidx = lax.top_k(group_score, TOPK_GROUPS)
    gmask = jnp.any(gidx[..., None] == jnp.arange(N_GROUPS), axis=-2)
    emask = jnp.repeat(gmask, per_group, axis=-1)
    _, eidx = lax.top_k(jnp.where(emask, sel, -jnp.inf), TOP_K)
    wts = jnp.take_along_axis(scores, eidx, -1)
    wts = wts / jnp.sum(wts, -1, keepdims=True) * ROUTED_SCALE
    A = T * TOP_K
    e_flat = eidx.reshape(A)
    t_flat = jnp.repeat(jnp.arange(T, dtype=jnp.int32), TOP_K)
    w_flat = wts.reshape(A)
    order = jnp.argsort(e_flat)
    e_s, t_s, w_s = e_flat[order], t_flat[order], w_flat[order]
    counts = jnp.bincount(e_flat, length=N_EXPERTS)
    starts = jnp.cumsum(counts) - counts
    padded = (counts + MOE_BLOCK - 1) // MOE_BLOCK * MOE_BLOCK
    pends = jnp.cumsum(padded)
    pstarts = pends - padded
    dest = pstarts[e_s] + (jnp.arange(A) - starts[e_s])
    n_blocks = A // MOE_BLOCK + N_EXPERTS
    P = n_blocks * MOE_BLOCK
    tok_buf = jnp.full((P,), T, jnp.int32).at[dest].set(t_s.astype(jnp.int32))
    w_buf = jnp.zeros((P,), xt.dtype).at[dest].set(w_s.astype(xt.dtype))
    blk_expert = jnp.minimum(jnp.searchsorted(pends, jnp.arange(n_blocks) * MOE_BLOCK, side='right'), N_EXPERTS - 1)
    x_pad = jnp.concatenate([xt, jnp.zeros((1, D), xt.dtype)], 0)

    def run_block(args):
        e, toks, ws = args
        xb = x_pad[toks]
        hb = jax.nn.silu(xb @ w_gate[e]) * (xb @ w_up[e])
        return (hb @ w_down[e]) * ws[:, None]

    yb = lax.map(run_block, (blk_expert, tok_buf.reshape(n_blocks, MOE_BLOCK), w_buf.reshape(n_blocks, MOE_BLOCK)))
    routed = jax.ops.segment_sum(yb.reshape(P, D), tok_buf, num_segments=T + 1)[:T]
    shared = (jax.nn.silu(xt @ ws_gate) * (xt @ ws_up)) @ ws_down
    return (routed + shared).reshape(B, S, D)

def second_inputs(seed: int = 0) -> dict:
    key = jax.random.key(seed)
    ks = jax.random.split(key, 26)
    L, D, E = DEPTH_2, D_MODEL, N_EXPERTS
    f32 = jnp.float32

    def nrm(k, shape, s):
        return jax.random.normal(k, shape, f32) * s

    def gain(k, shape):
        return 1.0 + 0.02 * jax.random.normal(k, shape, f32)

    w_in = nrm(ks[4], (L, D, IN_COLS), D ** -0.5)
    w_in = w_in.at[:, :, K_END:V_END].multiply(BETA)
    return {
        'x': nrm(ks[0], (BATCH, SEQ, D), 1.0),
        'c': nrm(ks[1], (BATCH, D), 1.0),
        'w_ada': nrm(ks[2], (L, D, 6 * D), 0.5 * D ** -0.5),
        'b_ada': nrm(ks[3], (L, 6 * D), 0.02),
        'w_in': w_in,
        'q_scale': gain(ks[5], (L, HEAD_DIM)),
        'k_scale': gain(ks[6], (L, HEAD_DIM)),
        'sgu_ln_g': gain(ks[7], (L, SGU_WIDTH)),
        'sgu_ln_b': nrm(ks[8], (L, SGU_WIDTH), 0.02),
        'w_spatial': nrm(ks[9], (L, SGU_GROUPS, SGU_CHUNK, SGU_CHUNK), SGU_CHUNK ** -0.5),
        'b_spatial': nrm(ks[10], (L, SGU_GROUPS, SGU_CHUNK), 0.02),
        'w_branch_a': nrm(ks[11], (L, ATTN_WIDTH, D), ATTN_WIDTH ** -0.5),
        'w_branch_b': nrm(ks[12], (L, SGU_WIDTH, D), SGU_WIDTH ** -0.5),
        'w_out': nrm(ks[13], (L, D, D), BETA * D ** -0.5),
        'ln1_g': gain(ks[14], (L, D)),
        'ln1_b': nrm(ks[15], (L, D), 0.02),
        'router_w': nrm(ks[16], (L, D, E), D ** -0.5),
        'router_bias': nrm(ks[17], (L, E), 0.01),
        'w_gate': nrm(ks[18], (L, E, D, EXPERT_FF), D ** -0.5),
        'w_up': nrm(ks[19], (L, E, D, EXPERT_FF), D ** -0.5),
        'w_down': nrm(ks[20], (L, E, EXPERT_FF, D), BETA * EXPERT_FF ** -0.5),
        'ws_gate': nrm(ks[21], (L, D, SHARED_FF), D ** -0.5),
        'ws_up': nrm(ks[22], (L, D, SHARED_FF), D ** -0.5),
        'ws_down': nrm(ks[23], (L, SHARED_FF, D), BETA * SHARED_FF ** -0.5),
        'ln2_g': gain(ks[24], (L, D)),
        'ln2_b': nrm(ks[25], (L, D), 0.02),
    }

def second_block(x, c, w_ada, b_ada, w_in, q_scale, k_scale, sgu_ln_g, sgu_ln_b, w_spatial, b_spatial,
              w_branch_a, w_branch_b, w_out, ln1_g, ln1_b, router_w, router_bias, w_gate, w_up, w_down,
              ws_gate, ws_up, ws_down, ln2_g, ln2_b):
    B, S, D = x.shape
    rows = S // GRID_W
    cos, sin = axial_rope_tables(S, rows)
    cond = jax.nn.silu(c)
    for l in range(DEPTH_2):
        mod = cond @ w_ada[l] + b_ada[l]
        shift1, scale1, gate1, shift2, scale2, gate2 = jnp.split(mod[:, None, :], 6, axis=-1)
        h = x * (1 + scale1) + shift1
        y = token_mixer(h, w_in[l], q_scale[l], k_scale[l], sgu_ln_g[l], sgu_ln_b[l], w_spatial[l], b_spatial[l],
                        w_branch_a[l], w_branch_b[l], w_out[l], cos, sin)
        x = layer_norm(ALPHA * x + gate1 * y, ln1_g[l], ln1_b[l])
        h = x * (1 + scale2) + shift2
        y = moe_ffn(h, router_w[l], router_bias[l], w_gate[l], w_up[l], w_down[l], ws_gate[l], ws_up[l], ws_down[l])
        x = layer_norm(ALPHA * x + gate2 * y, ln2_g[l], ln2_b[l])
    return x


def setup_inputs(seed=0):
    out = dict(first_inputs(seed))
    for name, value in second_inputs(seed + 1).items():
        if name != "x":
            out[name + "_2"] = value
    return out


def reference(
    x, rel_bias, norm_mix, norm_ffn, w_in, forget_bias, qk_gain, cmp_pos, cmp_w1, cmp_w2, sinks,
    w_branch, w_out, w_gate, w_up, conv_w, conv_b, w_down, c_2, w_ada_2, b_ada_2, w_in_2,
    q_scale_2, k_scale_2, sgu_ln_g_2, sgu_ln_b_2, w_spatial_2, b_spatial_2, w_branch_a_2,
    w_branch_b_2, w_out_2, ln1_g_2, ln1_b_2, router_w_2, router_bias_2, w_gate_2, w_up_2,
    w_down_2, ws_gate_2, ws_up_2, ws_down_2, ln2_g_2, ln2_b_2,
):
    x = first_block(
        x, rel_bias, norm_mix, norm_ffn, w_in, forget_bias, qk_gain, cmp_pos, cmp_w1, cmp_w2,
        sinks, w_branch, w_out, w_gate, w_up, conv_w, conv_b, w_down,
    )
    return second_block(
        x, c_2, w_ada_2, b_ada_2, w_in_2, q_scale_2, k_scale_2, sgu_ln_g_2, sgu_ln_b_2,
        w_spatial_2, b_spatial_2, w_branch_a_2, w_branch_b_2, w_out_2, ln1_g_2, ln1_b_2,
        router_w_2, router_bias_2, w_gate_2, w_up_2, w_down_2, ws_gate_2, ws_up_2, ws_down_2,
        ln2_g_2, ln2_b_2,
    )


_drawn_inputs = setup_inputs


def setup_inputs(seed=0):
    import zlib

    import numpy as np

    out = dict(_drawn_inputs(seed))
    spreads = {}
    factors = {'qk_gain': 2.922,
     'sinks': 7.727,
     'conv_b': 3.78,
     'b_ada_2': 2.752,
     'q_scale_2': 8.0,
     'k_scale_2': 8.0,
     'sgu_ln_g_2': 25.069,
     'sgu_ln_b_2': 25.059,
     'b_spatial_2': 25.528,
     'w_branch_a_2': 3.224}
    for name, (base, spread) in spreads.items():
        noise = np.random.default_rng([zlib.crc32(name.encode()), seed]).standard_normal(out[name].shape)
        drawn = base * np.exp(spread * noise) if base else spread * noise
        out[name] = jnp.asarray(drawn.astype(out[name].dtype))
    for name, factor in factors.items():
        out[name] = (out[name] * factor).astype(out[name].dtype)
    return out
```

```python
from contextlib import ExitStack

import numpy as np

import concourse.bass as bass
from concourse import mybir

F32 = mybir.dt.float32
ACT = mybir.ActivationFunctionType
ALU = mybir.AluOpType
AX = mybir.AxisListType

P = 128
T = 512
TT = T // P
D = 1024
DK = D // P
HD = 64
H = 8
MASKED = -1e30
RMS_EPS = 1e-6
F_HID = 2816
FT = F_HID // P
N_CMP = 31
CMP_HID = 256
L_TAB = 384
SLOT = 4608
SLOTS = 4

C_AQ, C_KC, C_KS, C_VS, C_KW, C_VW, C_GATE = 0, 512, 768, 896, 1024, 1152, 1280
C_BQ, C_BK, C_BV = 1304, 1816, 1944
C_CQ, C_CK, C_CV, C_CF, C_MERGE = 2072, 2584, 3096, 3608, 3616


def shape_constants():
    p = np.arange(P)[:, None]
    c = np.arange(P)[None, :]
    ident = np.eye(P, dtype=np.float32)
    block = ((p // HD) == (c // HD)).astype(np.float32)
    win = np.where(p >= c, np.float32(MASKED), np.float32(0)).astype(np.float32)
    causal = np.zeros((P, T), np.float32)
    causal[:, T - P:] = np.where(c > p, MASKED, 0)
    seen = (p >= 31).astype(np.float32)
    foxsel = np.zeros((P, H), np.float32)
    for quarter in range(4):
        foxsel[32 * quarter + np.arange(H), np.arange(H)] = 1
    square = np.concatenate([ident, block, win, causal, seen, foxsel], axis=1).astype(np.float32)

    y = np.arange(L_TAB)
    dist = 255 - y
    d = np.maximum(dist, 1)
    large = np.minimum(16 + (np.log(d / 16.0) / np.log(8.0) * 16 + 1e-9).astype(np.int64), 31)
    bucket = np.where(dist < 16, np.maximum(dist, 0), large)
    rows = []
    for reach in (512, 128):
        hot = np.zeros((33, L_TAB), np.float32)
        hot[np.where((dist >= 0) & (dist < reach), bucket, 32), y] = 1
        rows.append(hot)

    t = np.arange(T)
    freq = (np.float32(10000.0) ** (-np.arange(HD // 4, dtype=np.float32) / np.float32(HD // 4))).astype(np.float32)
    at_row = (t // 64 - (T // 64) // 2).astype(np.float32)
    at_col = (t % 64 - 32).astype(np.float32)
    angle = np.concatenate([at_row[:, None] * freq, at_col[:, None] * freq], axis=1).astype(np.float32)
    angle = np.repeat(angle, 2, axis=1).T
    angle = np.concatenate([angle, angle], axis=0)
    swap = np.zeros((P, P), np.float32)
    even = np.arange(0, P, 2)
    swap[even + 1, even] = -1
    swap[even, even + 1] = 1
    rope = np.concatenate([np.cos(angle), np.sin(angle), swap], axis=1).astype(np.float32)
    pairs = (np.arange(8)[:, None] == (np.arange(512) // HD)[None, :]).astype(np.float32)
    return {"cst_square": square, "cst_buckets": np.concatenate(rows, axis=1), "cst_rope": rope, "cst_pairs": pairs}


IDENT, BLOCK, WIN, CAUSAL, SEEN, FOXSEL = 0, 128, 256, 384, 896, 897
CST_W = 897 + H


class Chain:

    def __init__(self, sem, eng):
        self.sem, self.n, self.eng = sem, 0, eng

    def __call__(self, ins):
        ins.then_inc(self.sem, 1)
        self.n += 1
        self.eng.wait_ge(self.sem, self.n)


class Program:

    def __init__(self, nc, dram):
        self.nc, self.dram, self.previous, self.stages = nc, dram, None, 0

    def sb(self, ctx, name, shape):
        return ctx.enter_context(self.nc.sbuf_tensor(f"{name}_{self.stages}", shape, F32))

    def ps(self, ctx, name, shape):
        return ctx.enter_context(self.nc.psum_tensor(f"{name}_{self.stages}", shape, F32))

    def stage(self, *names):
        return Stage(self, names)

    def finish(self):
        with Stage(self, ()):
            pass
        self.previous = None


class Stage:

    def __init__(self, prog, names):
        self.prog, self.names = prog, names

    def __enter__(self):
        nc = self.prog.nc
        self.holder = ExitStack()
        self.prog.stages += 1
        self.sems = [self.holder.enter_context(nc.semaphore(f"{n}_{self.prog.stages}")) for n in self.names]
        self.block = nc.Block()
        block = self.block.__enter__()
        before = self.prog.previous
        if before is not None and before.sems:
            @block.sync
            def _(sp):
                for sem in before.sems:
                    sp.sem_clear(sem)
        return block, dict(zip(self.names, self.sems))

    def __exit__(self, *exc):
        self.block.__exit__(*exc)
        if exc[0] is None:
            if self.prog.previous is not None:
                self.prog.previous.holder.close()
            self.prog.previous = self


class Ring:

    def __init__(self, prog, ctx, chunks):
        self.nc, self.chunks = prog.nc, chunks
        self.mem = prog.sb(ctx, "weights", [P, SLOTS, SLOT])
        self.loaded = [ctx.enter_context(prog.nc.semaphore(f"weights_loaded_{i}")) for i in range(SLOTS)]
        self.used = ctx.enter_context(prog.nc.semaphore("weights_used"))
        self.plan()

    def plan(self):
        chunks = self.chunks
        self.issued = 0
        total = [0] * SLOTS
        self.need = []
        for c, parts in enumerate(chunks):
            total[c % SLOTS] += 16 * len(parts)
            self.need.append(total[c % SLOTS])

    def slot(self, c, k, n, at=0):
        return self.mem[:, c % SLOTS, at:at + k * n].rearrange("p (k n) -> p k n", k=k)

    def run_ahead(self, sp, end):
        for c in range(self.issued, min(end + SLOTS, len(self.chunks))):
            if c >= SLOTS:
                sp.wait_ge(self.used, c - SLOTS + 1)
            for at, k, n, src in self.chunks[c]:
                sp.dma_start(self.slot(c, k, n, at), src).then_inc(self.loaded[c % SLOTS], 16)
        self.issued = max(self.issued, min(end + SLOTS, len(self.chunks)))

    def wait(self, eng, c):
        eng.wait_ge(self.loaded[c % SLOTS], self.need[c])

    def clear(self, sp):
        for sem in self.loaded + [self.used]:
            sp.sem_clear(sem)


def rows(w, k=DK):
    return w.rearrange("(k p) n -> p k n", p=P)


def norm_model(prog, src, gain, dst):
    nc = prog.nc
    with ExitStack() as ctx:
        sq = prog.sb(ctx, "squares", [P, 2, T])
        root = prog.sb(ctx, "root", [P, T])
        rstd = prog.sb(ctx, "rstd", [P, T])
        total = prog.ps(ctx, "total", [P, T])
        with prog.stage("squared", "summed", "total_ready", "root_ready", "rstd_ready") as (block, s):
            @block.scalar
            def _(act):
                for k in range(DK):
                    if k >= 2:
                        act.wait_ge(s["summed"], k - 1)
                    act.activation(sq[:, k % 2, :], src[:, k, :], ACT.Square).then_inc(s["squared"], 1)
                act.wait_ge(s["summed"], DK)
                act.activation(root[:, :], total[:, :], ACT.Sqrt, bias=prog.eps[:, 0:1],
                               scale=1.0 / D).then_inc(s["root_ready"], 1)

            @block.tensor
            def _(pe):
                for k in range(DK):
                    pe.wait_ge(s["squared"], k + 1)
                    pe.matmul(total[:, :], prog.ones[:, :], sq[:, k % 2, :], start=(k == 0),
                              stop=(k == DK - 1)).then_inc(s["summed"], 1)

            @block.vector
            def _(dve):
                dve.wait_ge(s["root_ready"], 1)
                dve.reciprocal(rstd[:, :], root[:, :]).then_inc(s["rstd_ready"], 1)
                dve.wait_ge(s["rstd_ready"], 1)
                for k in range(DK):
                    dve.scalar_tensor_tensor(out=dst[:, k, :], in0=src[:, k, :], scalar=gain[:, k:k + 1],
                                             in1=rstd[:, :], op0=ALU.mult, op1=ALU.mult)


def norm_heads(prog, tiles):
    nc = prog.nc
    with ExitStack() as ctx:
        sq = prog.sb(ctx, "squares", [P, 2, T])
        root = prog.sb(ctx, "root", [P, 2, T])
        rstd = prog.sb(ctx, "rstd", [P, 2, T])
        total = prog.ps(ctx, "total", [P, 2, T])
        with prog.stage("squared", "summed", "root_ready", "rstd_ready", "normed") as (block, s):
            @block.scalar
            def _(act):
                def roots(i):
                    n = tiles[i][0].shape[-1]
                    act.wait_ge(s["summed"], i + 1)
                    if i >= 2:
                        act.wait_ge(s["rstd_ready"], i - 1)
                    act.activation(root[:, i % 2, 0:n], total[:, i % 2, 0:n], ACT.Sqrt,
                                   bias=prog.eps[:, 0:1], scale=1.0 / HD).then_inc(s["root_ready"], 1)

                for i, (x, g) in enumerate(tiles):
                    if i >= 2:
                        act.wait_ge(s["summed"], i - 1)
                    act.activation(sq[:, i % 2, 0:x.shape[-1]], x, ACT.Square).then_inc(s["squared"], 1)
                    if i >= 1:
                        roots(i - 1)
                roots(len(tiles) - 1)

            @block.tensor
            def _(pe):
                for i, (x, g) in enumerate(tiles):
                    n = x.shape[-1]
                    pe.wait_ge(s["squared"], i + 1)
                    if i >= 2:
                        pe.wait_ge(s["root_ready"], i - 1)
                    pe.matmul(total[:, i % 2, 0:n], prog.block_ones[:, :], sq[:, i % 2, 0:n], start=True,
                              stop=True).then_inc(s["summed"], 1)

            @block.vector
            def _(dve):
                for i, (x, g) in enumerate(tiles):
                    n = x.shape[-1]
                    dve.wait_ge(s["root_ready"], i + 1)
                    if i >= 2:
                        dve.wait_ge(s["normed"], i - 1)
                    dve.reciprocal(rstd[:, i % 2, 0:n], root[:, i % 2, 0:n]).then_inc(s["rstd_ready"], 1)
                    dve.wait_ge(s["rstd_ready"], i + 1)
                    dve.scalar_tensor_tensor(out=x, in0=x, scalar=g, in1=rstd[:, i % 2, 0:n],
                                             op0=ALU.mult, op1=ALU.mult).then_inc(s["normed"], 1)


def transpose_tiles(prog, jobs, pieces=1):
    nc = prog.nc
    with ExitStack() as ctx:
        banks = prog.ps(ctx, "turned", [P, 4, T])
        with prog.stage("turned", "emptied_dve", "emptied_act") as (block, s):
            @block.tensor
            def _(pe):
                for j, (sources, dst) in enumerate(jobs):
                    if j >= 4:
                        pe.wait_ge(s["emptied_dve"] if j % 2 == 0 else s["emptied_act"], (j - 4) // 2 + 1)
                    for i, src in enumerate(sources):
                        last = pe.transpose(banks[:, j % 4, i * P:(i + 1) * P], src, prog.ident[:, :])
                    last.then_inc(s["turned"], 1)

            @block.vector
            def _(dve):
                for j in range(0, len(jobs), 2):
                    dve.wait_ge(s["turned"], j + 1)
                    dst = jobs[j][1]
                    dve.tensor_copy(dst, banks[:, j % 4, 0:P * len(jobs[j][0])]).then_inc(s["emptied_dve"], 1)

            @block.scalar
            def _(act):
                for j in range(1, len(jobs), 2):
                    act.wait_ge(s["turned"], j + 1)
                    dst = jobs[j][1]
                    act.copy(dst, banks[:, j % 4, 0:P * len(jobs[j][0])]).then_inc(s["emptied_act"], 1)


def project(prog, ring, tiles, rhs, first, end, k_tiles=DK):
    nc = prog.nc
    with ExitStack() as ctx:
        banks = prog.ps(ctx, "products", [P, 4, T])
        with prog.stage("product_ready", "emptied_dve", "emptied_act") as (block, s):
            @block.sync
            def _(sp):
                ring.run_ahead(sp, end)

            @block.tensor
            def _(pe):
                seen = first - 1
                for j, (chunk, lhs, right, rows_out, width, parts) in enumerate(tiles):
                    if chunk is not None and chunk > seen:
                        ring.wait(pe, chunk)
                        seen = chunk
                    if j >= 4:
                        pe.wait_ge(s["emptied_dve"] if j % 2 == 0 else s["emptied_act"], (j - 4) // 2 + 1)
                    for k in range(k_tiles):
                        last = pe.matmul(banks[0:rows_out, j % 4, 0:width], lhs(k), right(k), start=(k == 0),
                                         stop=(k == k_tiles - 1))
                    last.then_inc(s["product_ready"], 1)
                    leaves = j + 1 == len(tiles) or tiles[j + 1][0] != chunk
                    if chunk is not None and leaves:
                        pe.wait_ge(s["product_ready"], j + 1)
                        pe.sem_inc(ring.used, 1)

            @block.vector
            def _(dve):
                for j in range(0, len(tiles), 2):
                    dve.wait_ge(s["product_ready"], j + 1)
                    for ps, cols, dst in tiles[j][5]:
                        last = dve.tensor_copy(dst, banks[ps, j % 4, cols])
                    last.then_inc(s["emptied_dve"], 1)

            @block.scalar
            def _(act):
                for j in range(1, len(tiles), 2):
                    act.wait_ge(s["product_ready"], j + 1)
                    for ps, cols, dst in tiles[j][5]:
                        last = act.copy(dst, banks[ps, j % 4, cols])
                    last.then_inc(s["emptied_act"], 1)


def attention(prog, units):
    nc = prog.nc
    with ExitStack() as ctx:
        scores = prog.ps(ctx, "scores", [P, 2, T])
        turned = prog.ps(ctx, "turned", [P, 2, T])
        summed = prog.ps(ctx, "summed", [P, 2, T])
        prob = prog.sb(ctx, "prob", [P, 3, T])
        probT = prog.sb(ctx, "probT", [P, 2, T])
        low = prog.sb(ctx, "low", [P, 4])
        mass = prog.sb(ctx, "mass", [P, 4])
        sinkm = prog.sb(ctx, "sinkm", [P, 4])
        inv = prog.sb(ctx, "inv", [P, 4, 2])
        with prog.stage("scores_ready", "logits_ready", "probs_ready", "turned_ready", "probsT_ready",
                        "summed_ready", "out_ready", "dve_step") as (block, s):
            last_unit = len(units) - 1

            @block.tensor
            def _(pe):
                def make_scores(u):
                    x = units[u]
                    if u >= 2:
                        pe.wait_ge(s["logits_ready"], u - 1)
                    reach = x["extra"][1] if x["extra"] else 0
                    if reach:
                        pe.matmul(scores[:, u % 2, 0:reach], x["q"], x["k"][:, 0:reach], start=True, stop=False)
                        last = pe.matmul(scores[:, u % 2, 0:reach], *x["extra"][0], start=False, stop=True)
                    if reach < x["n"]:
                        last = pe.matmul(scores[:, u % 2, reach:x["n"]], x["q"], x["k"][:, reach:x["n"]], start=True,
                                         stop=True)
                    last.then_inc(s["scores_ready"], 1)

                def turn(u):
                    pe.wait_ge(s["probs_ready"], u + 1)
                    if u >= 2:
                        pe.wait_ge(s["probsT_ready"], u - 1)
                    c = 0
                    for i, (r, v) in enumerate(units[u]["v"]):
                        last = pe.transpose(turned[0:r, u % 2, i * P:(i + 1) * P], prob[:, u % 3, c:c + r],
                                            prog.ident[:, :])
                        c += r
                    last.then_inc(s["turned_ready"], 1)

                def weigh(u):
                    pe.wait_ge(s["probsT_ready"], u + 1)
                    if u >= 2:
                        pe.wait_ge(s["out_ready"], u - 1)
                    vs = units[u]["v"]
                    for i, (r, v) in enumerate(vs):
                        last = pe.matmul(summed[:, u % 2, 0:HD], probT[0:r, u % 2, i * P:(i + 1) * P], v,
                                         start=(i == 0), stop=(i == len(vs) - 1))
                    last.then_inc(s["summed_ready"], 1)

                for i in range(len(units) + 2):
                    if i <= last_unit:
                        make_scores(i)
                    if 1 <= i <= last_unit + 1:
                        turn(i - 1)
                    if i >= 2:
                        weigh(i - 2)

            @block.scalar
            def _(act):
                def exponentials(u):
                    x = units[u]
                    act.wait_ge(s["logits_ready"], u + 1)
                    if u >= 4:
                        act.wait_ge(s["out_ready"], u - 3)
                    if x["sink"] is not None:
                        act.activation(sinkm[:, u % 4:u % 4 + 1], x["sink"], ACT.Exp, bias=low[:, u % 4:u % 4 + 1])
                    act.activation(prob[:, u % 3, 0:x["n"]], prob[:, u % 3, 0:x["n"]], ACT.Exp,
                                   bias=low[:, u % 4:u % 4 + 1], scale=-1.0,
                                   accum_out=mass[:, u % 4:u % 4 + 1]).then_inc(s["probs_ready"], 1)

                def copy_turned(u):
                    act.wait_ge(s["turned_ready"], u + 1)
                    if u >= 2:
                        act.wait_ge(s["summed_ready"], u - 1)
                    vs = units[u]["v"]
                    r = vs[0][0]
                    act.copy(probT[0:r, u % 2, 0:P * len(vs)],
                             turned[0:r, u % 2, 0:P * len(vs)]).then_inc(s["probsT_ready"], 1)

                for i in range(len(units) + 1):
                    if i <= last_unit:
                        exponentials(i)
                    if i >= 1:
                        copy_turned(i - 1)

            @block.vector
            def _(dve):
                link = Chain(s["dve_step"], dve)

                def logits(u):
                    x = units[u]
                    dve.wait_ge(s["scores_ready"], u + 1)
                    if u >= 3:
                        dve.wait_ge(s["turned_ready"], u - 2)
                    sc = scores[:, u % 2, 0:x["n"]]
                    bias = prog.zeros[:, 0:x["n"]] if x["bias"] is None else x["bias"]
                    start = 3e38 if x["sink"] is None else x["minus_sink"]
                    dve.tensor_tensor_reduce(prob[:, u % 3, 0:x["n"]], sc, bias, -1.0, start, ALU.add, ALU.min,
                                             low[:, u % 4:u % 4 + 1]).then_inc(s["logits_ready"], 1)

                def finish(u):
                    x = units[u]
                    a, b = inv[:, u % 4, 0:1], inv[:, u % 4, 1:2]
                    m = mass[:, u % 4:u % 4 + 1]
                    dve.wait_ge(s["summed_ready"], u + 1)
                    if x["sink"] is not None:
                        link(dve.tensor_tensor(b, m, sinkm[:, u % 4:u % 4 + 1], ALU.add))
                        m = b
                    link(dve.reciprocal(a, m))
                    if x["factor"] is not None:
                        link(dve.tensor_tensor(b, a, x["factor"], ALU.mult))
                        a = b
                    if x["adds"]:
                        dve.scalar_tensor_tensor(out=x["out"], in0=summed[:, u % 2, 0:HD], scalar=a, in1=x["out"],
                                                 op0=ALU.mult, op1=ALU.add).then_inc(s["out_ready"], 1)
                    else:
                        dve.tensor_scalar(x["out"], summed[:, u % 2, 0:HD], a, None,
                                          ALU.mult).then_inc(s["out_ready"], 1)

                for i in range(len(units) + 2):
                    if i <= last_unit:
                        logits(i)
                    if i >= 2:
                        finish(i - 2)


def unit(q, k, n, v, out, bias=None, extra=None, sink=None, minus_sink=None, factor=None, adds=False):
    return dict(q=q, k=k, n=n, v=v, out=out, bias=bias, extra=extra, sink=sink, minus_sink=minus_sink,
                factor=factor, adds=adds)


def half(h):
    return slice(HD * (h % 2), HD * (h % 2) + HD)


def rows_of(h):
    return slice(HD * (h % 2), HD * (h % 2) + 32 + H)



def first_chunks(d):
    w = rows(d["w_in"][0])
    w1 = d["cmp_w1"][0]
    wb, wg, wu, wd = d["w_branch"][0], rows(d["w_gate"][0]), rows(d["w_up"][0]), rows(d["w_down"][0], FT)
    wo = rows(d["w_out"][0])
    out = {}
    chunks = []

    def add(name, *parts):
        out.setdefault(name, len(chunks))
        at, listed = 0, []
        for view in parts:
            k, n = view.shape[1], view.shape[2]
            listed.append((at, k, n, view))
            at += k * n
        chunks.append(listed)

    add("a_q", w[:, :, C_AQ:C_AQ + 512])
    add("a_kv", w[:, :, C_KC:C_KC + 512])
    add("a_w", w[:, :, C_KW:C_KW + 280])
    for which in range(2):
        add("cmp_w1", rows(w1[which], 16))
    add("b_q", w[:, :, C_BQ:C_BQ + 512])
    add("b_kv", w[:, :, C_BK:C_BK + 256])
    add("c_q", w[:, :, C_CQ:C_CQ + 512])
    add("c_k", w[:, :, C_CK:C_CK + 512])
    add("c_v", w[:, :, C_CV:C_CV + 512], w[:, :, C_CF:C_CF + H])
    for m in range(DK):
        add("merge", *[w[:, :, C_MERGE + b * D + m * P:C_MERGE + b * D + (m + 1) * P] for b in range(3)],
            *[rows(wb[b], 4)[:, :, m * P:(m + 1) * P] for b in range(3)])
    for m in range(2):
        add("w_out", wo[:, :, m * 512:(m + 1) * 512])
    for m in range(FT // 2):
        add("ffn", wg[:, :, m * 256:(m + 1) * 256], wu[:, :, m * 256:(m + 1) * 256])
    for m in range(DK):
        add("w_down", wd[:, :, m * P:(m + 1) * P])
    return chunks, out


def column(view):
    return view.rearrange("(k p) -> p k", p=P)


def first_block(prog, xT):
    nc, d = prog.nc, prog.dram
    chunks, at = first_chunks(d)
    with ExitStack() as ctx:
        ring = Ring(prog, ctx, chunks)
        gains = prog.sb(ctx, "gains", [P, 6])
        norm_mix = prog.sb(ctx, "norm_mix", [P, DK])
        norm_ffn = prog.sb(ctx, "norm_ffn", [P, DK])
        conv_w = prog.sb(ctx, "conv_w", [P, 3, FT])
        conv_b = prog.sb(ctx, "conv_b", [P, FT])
        with ExitStack() as mixers:
            oT = prog.sb(mixers, "oT", [P, 3, 4, T])
            hT = prog.sb(mixers, "hT", [P, DK, T])
            x_tok = oT[:, 0:2, :, :].rearrange("p a b n -> p (a b n)").rearrange("p (t n) -> p t n", t=TT)
            with prog.stage("loaded", "scaled") as (block, s):
                @block.sync
                def _(sp):
                    for t in range(TT):
                        sp.dma_start(x_tok[:, t, :], d["x"][0, t * P:(t + 1) * P, :]).then_inc(s["loaded"], 16)
                    ring.run_ahead(sp, 0)
                    sp.wait_ge(s["loaded"], 16 * TT)

                @block.scalar
                def _(act):
                    with nc.allow_non_contiguous_dma(reason="small vectors, once"):
                        g = d["qk_gain"][0].rearrange("g d -> d g")
                        act.dma_start(gains[0:HD, :], g).then_inc(s["scaled"], 16)
                        act.dma_start(gains[HD:P, :], g).then_inc(s["scaled"], 16)
                        act.dma_start(norm_mix[:, :], column(d["norm_mix"][0])).then_inc(s["scaled"], 16)
                        act.dma_start(norm_ffn[:, :], column(d["norm_ffn"][0])).then_inc(s["scaled"], 16)
                        act.dma_start(conv_b[:, :], column(d["conv_b"][0])).then_inc(s["scaled"], 16)
                        for i in range(3):
                            act.dma_start(conv_w[:, i, :], column(d["conv_w"][0, i])).then_inc(s["scaled"], 16)
                    act.wait_ge(s["scaled"], 128)

                @block.vector
                def _(dve):
                    dve.wait_ge(s["scaled"], 128)
                    for g in (0, 2, 4):
                        dve.tensor_scalar(gains[:, g:g + 1], gains[:, g:g + 1], HD ** -0.5, None, ALU.mult)
            transpose_tiles(prog, [([x_tok[:, t, m * P:(m + 1) * P] for t in range(TT)], xT[:, m, :])
                                   for m in range(DK)])
            norm_model(prog, xT, norm_mix, hT)
            mixer_a(prog, ring, at, hT, oT, gains)
            mixer_b(prog, ring, at, hT, oT, gains)
            mixer_c(prog, ring, at, hT, oT, gains)
            with ExitStack() as merged:
                yT = prog.sb(merged, "yT", [P, DK, T])
                merge_branches(prog, ring, at["merge"], hT, oT, yT, 3)
                residual_product(prog, ring, at["w_out"], yT, xT)
        with ExitStack() as ffn:
            hT = prog.sb(ffn, "hT_ffn", [P, DK, T])
            norm_model(prog, xT, norm_ffn, hT)
            conv_ffn(prog, ring, at, hT, xT, conv_w, conv_b)
        with prog.stage("none") as (block, s):
            @block.sync
            def _(sp):
                ring.clear(sp)


def bias_tables(prog, tables, group, reach):
    nc, d = prog.nc, prog.dram
    with ExitStack() as ctx:
        tab = prog.sb(ctx, "tab", [33, H])
        tab_wide = prog.sb(ctx, "tab_wide", [33, H, P])
        hot = prog.sb(ctx, "hot", [33, L_TAB])
        line = prog.sb(ctx, "line", [P, H, L_TAB])
        spread = prog.ps(ctx, "spread", [P, 2, T])
        width = tables.shape[2]
        scratch = d["scratch"]
        with prog.stage("loaded", "filled", "wide", "spread_ready", "line_ready", "written", "read") as (block, s):
            @block.sync
            def _(sp):
                sp.dma_start(tab[0:32, :], d["rel_bias"][:, group * H:(group + 1) * H]).then_inc(s["loaded"], 16)
                sp.dma_start(hot[:, :], d["cst_buckets"][:, group * L_TAB:(group + 1) * L_TAB]).then_inc(s["loaded"], 16)
                sp.wait_ge(s["line_ready"], H)
                sp.dma_start(scratch[:, :].rearrange("h (p c) -> p h c", p=P), line[:, :, :]).then_inc(s["written"], 16)
                sp.wait_ge(s["written"], 16)
                view = scratch[:, P - 1:P - 1 + P * (L_TAB - 1)].rearrange("h (p c) -> p h c", c=L_TAB - 1)
                sp.dma_start(tables[:, :, width - 256:width], view[:, :, 0:256]).then_inc(s["read"], 16)
                sp.wait_ge(s["read"], 16)

            @block.vector
            def _(dve):
                dve.memset(tab[32:33, :], MASKED).then_inc(s["filled"], 1)
                dve.wait_ge(s["filled"], 1)
                dve.wait_ge(s["loaded"], 32)
                for h in range(H):
                    last = dve.tensor_copy(tab_wide[:, h, :], tab[:, h:h + 1].to_broadcast([33, P]))
                last.then_inc(s["wide"], 1)

            @block.tensor
            def _(pe):
                pe.wait_ge(s["wide"], 1)
                for h in range(H):
                    if h >= 2:
                        pe.wait_ge(s["line_ready"], h - 1)
                    pe.matmul(spread[:, h % 2, 0:L_TAB], tab_wide[:, h, :], hot[:, :], start=True,
                              stop=True).then_inc(s["spread_ready"], 1)

            @block.scalar
            def _(act):
                for h in range(H):
                    act.wait_ge(s["spread_ready"], h + 1)
                    act.copy(line[:, h, :], spread[:, h % 2, 0:L_TAB]).then_inc(s["line_ready"], 1)
                if width > 256:
                    for h in range(H):
                        act.wait_ge(s["line_ready"], h + 1)
                        act.activation(tables[:, h, 0:width - 256], prog.zeros[:, 0:width - 256], ACT.Identity,
                                       bias=line[:, h, 0:1])


def feature_tiles(ring, chunk, stride, start, hT, dst):
    w = ring.slot(chunk, DK, stride)
    out = []
    for i in range(dst.shape[1]):
        out.append((chunk, lambda k, i=i: w[:, k, start + i * P:start + (i + 1) * P], lambda k: hT[:, k, :], P, T,
                    [(slice(0, P), slice(0, T), dst[:, i, :])]))
    return out


def twin_tiles(ring, chunk, stride, start, hT, dst, shifted=False):
    w = ring.slot(chunk, DK, stride)
    out = []
    for g in range(2):
        for side in range(2):
            ps = slice(side * HD, side * HD + HD)
            if side and shifted:
                parts = [(slice(0, HD), slice(1, T), dst[ps, g, 0:T - 1])]
            else:
                parts = [(slice(0, HD), slice(0, T), dst[ps, g, :])]
            if side == 0:
                lhs = (lambda k, g=g: w[:, k, start + g * HD:start + (g + 1) * HD])
                out.append((chunk, lhs, lambda k: hT[:, k, :], HD, T, parts))
            else:
                out[-1][5].extend(parts)
    return out


def token_tiles(ring, chunk, stride, start, n, hT, dst, at=0):
    w = ring.slot(chunk, DK, stride, at)
    return [(chunk, lambda k, t=t: hT[:, k, t * P:(t + 1) * P], lambda k: w[:, k, start:start + n], P, n,
             [(slice(0, P), slice(0, n), dst[:, t, :])]) for t in range(TT)]


def mixer_a(prog, ring, at, hT, oT, gains):
    nc, d = prog.nc, prog.dram
    with ExitStack() as ctx:
        tables = prog.sb(ctx, "tables", [P, H, T])
        qT = prog.sb(ctx, "qT", [P, 4, T])
        cT = prog.sb(ctx, "cT", [P, 2, 2, T])
        kT = prog.sb(ctx, "kT", [P, 2, 2, T])
        v_tok = prog.sb(ctx, "v_tok", [P, TT, P])
        w_tok = prog.sb(ctx, "w_tok", [P, TT, P + 3 * H])
        kcT = prog.sb(ctx, "kcT", [P, 2, N_CMP])
        vc = prog.sb(ctx, "vc", [N_CMP, 2, HD])
        o_tok = prog.sb(ctx, "o_tok", [P, TT, 512])

        bias_tables(prog, tables, 0, T)
        q, kv, w = at["a_q"], at["a_kv"], at["a_w"]
        tiles = feature_tiles(ring, q, 512, 0, hT, qT)
        tiles += twin_tiles(ring, kv, 512, 0, hT, cT[:, 0, :, :], shifted=True)
        tiles += twin_tiles(ring, kv, 512, 128, hT, cT[:, 1, :, :], shifted=True)
        tiles += twin_tiles(ring, kv, 512, 256, hT, kT[:, 0, :, :])
        tiles += token_tiles(ring, kv, 512, 384, P, hT, v_tok)
        tiles += twin_tiles(ring, w, 280, 0, hT, kT[:, 1, :, :])
        tiles += token_tiles(ring, w, 280, 128, P + 3 * H, hT, w_tok)
        project(prog, ring, tiles, hT, q, w + 1)
        compress(prog, ring, at, cT, kcT, vc)
        norm_heads(prog, [(qT[:, i, :], gains[:, 0:1]) for i in range(4)]
                   + [(kT[:, i, g, :], gains[:, 1:2]) for i in range(2) for g in range(2)]
                   + [(kcT[:, g, :], gains[:, 1:2]) for g in range(2)])
        with prog.stage("gated") as (block, s):
            @block.scalar
            def _(act):
                act.activation(w_tok[:, :, P:P + 3 * H], w_tok[:, :, P:P + 3 * H], ACT.Sigmoid)

        factors = prog.sb(ctx, "factors", [P, H])
        with prog.stage("none") as (block, s):
            @block.vector
            def _(dve):
                for h in range(H):
                    g = w_tok[:, 0, P + 3 * h:P + 3 * h + 1]
                    dve.tensor_scalar(factors[:, h:h + 1], g, prog.seen, None, ALU.mult)
        units = []
        for h in range(H):
            g = h // 4
            for t in range(TT):
                query = qT[half(h), h // 2, t * P:(t + 1) * P]
                out = o_tok[:, t, h * HD:(h + 1) * HD]
                gate = [w_tok[:, t, P + 3 * h + i:P + 3 * h + i + 1] for i in range(3)]
                n = (t + 1) * P
                units.append(unit(query, kT[half(h), 0, g, 0:n], n,
                                  [(P, v_tok[:, j, g * HD:(g + 1) * HD]) for j in range(t + 1)], out,
                                  bias=tables[:, h, T - n:T], factor=gate[1]))
        for h in range(H):
            g = h // 4
            for t in range(TT):
                query = qT[half(h), h // 2, t * P:(t + 1) * P]
                out = o_tok[:, t, h * HD:(h + 1) * HD]
                gate = [w_tok[:, t, P + 3 * h + i:P + 3 * h + i + 1] for i in range(3)]
                j0 = max(0, t - 2)
                n = (t + 1 - j0) * P
                far = ((prog.ident[:, :], prog.window[:, :]), P) if t >= 2 else None
                units.append(unit(query, kT[half(h), 1, g, j0 * P:j0 * P + n], n,
                                  [(P, w_tok[:, j, g * HD:(g + 1) * HD]) for j in range(j0, t + 1)], out,
                                  bias=tables[:, h, T - n:T], extra=far, factor=gate[2], adds=True))
        for h in range(H):
            g = h // 4
            for t in range(TT):
                query = qT[half(h), h // 2, t * P:(t + 1) * P]
                out = o_tok[:, t, h * HD:(h + 1) * HD]
                n = 7 + 8 * t
                first = 415 - P * t
                factor = factors[:, h:h + 1] if t == 0 else w_tok[:, t, P + 3 * h:P + 3 * h + 1]
                units.append(unit(query, kcT[half(h), g, 0:n], n, [(n, vc[0:n, g, :])], out,
                                  bias=tables[:, h, first:first + 16 * (n - 1) + 1:16], factor=factor, adds=True))
        attention(prog, units)
        to_features(prog, o_tok, oT[:, 0, :, :])


def to_features(prog, o_tok, oT):
    transpose_tiles(prog, [([o_tok[:, t, m * P:(m + 1) * P] for t in range(TT)], oT[:, m, :]) for m in range(4)])


def compress(prog, ring, at, cT, kcT, vc):
    nc, d = prog.nc, prog.dram
    with ExitStack() as ctx:
        pos = prog.sb(ctx, "pos", [P, 2, 16])
        w2 = prog.sb(ctx, "w2", [P, 2, 2, HD])
        hid = prog.sb(ctx, "hid", [P, 2, 2, 2 * N_CMP])
        shift = prog.sb(ctx, "shift", [P, 4])
        banks = prog.ps(ctx, "hidden", [P, 4, T])
        banks2 = prog.ps(ctx, "compressed", [P, 3, T])
        with prog.stage("loaded", "hidden_ready", "shift_ready", "gelu_ready", "out_ready") as (block, s):
            @block.sync
            def _(sp):
                with nc.allow_non_contiguous_dma(reason="8 KB of positions"):
                    for which in range(2):
                        sp.dma_start(pos[:, which, :], d["cmp_pos"][0, which].rearrange(
                            "(l two) d -> (two d) l", two=2)).then_inc(s["loaded"], 16)
                        sp.dma_start(w2[:, which, :, :], rows(d["cmp_w2"][0, which], 2)).then_inc(s["loaded"], 16)
                ring.run_ahead(sp, at["cmp_w1"] + 2)

            @block.tensor
            def _(pe):
                pe.wait_ge(s["loaded"], 64)
                for which in range(2):
                    c = at["cmp_w1"] + which
                    ring.wait(pe, c)
                    w = ring.slot(c, 16, CMP_HID)
                    for m in range(2):
                        j = 2 * which + m
                        for l in range(16):
                            pe.matmul(banks[:, j, 0:2 * N_CMP], w[:, l, m * P:(m + 1) * P],
                                      cT[:, which, :, 2 * l:2 * l + 16 * (N_CMP - 1) + 1:16], start=(l == 0),
                                      stop=(l == 15))
                        for l in range(16):
                            last = pe.matmul(banks[:, j, 2 * N_CMP:2 * N_CMP + 1], w[:, l, m * P:(m + 1) * P],
                                             pos[:, which, l:l + 1], start=(l == 0), stop=(l == 15))
                        last.then_inc(s["hidden_ready"], 1)
                    pe.wait_ge(s["hidden_ready"], 2 * which + 2)
                    pe.sem_inc(ring.used, 1)
                pe.wait_ge(s["gelu_ready"], 2)
                for side in range(2):
                    for m in range(2):
                        last = pe.matmul(banks2[side * HD:(side + 1) * HD, side, 0:2 * N_CMP], w2[:, 0, m, :], hid[:, 0, m, :],
                                         start=(m == 0), stop=(m == 1))
                pe.wait_ge(s["gelu_ready"], 4)
                for g in range(2):
                    for m in range(2):
                        last = pe.matmul(banks2[0:N_CMP, 2, g * HD:(g + 1) * HD],
                                         hid[:, 1, m, g * N_CMP:(g + 1) * N_CMP], w2[:, 1, m, :],
                                         start=(m == 0), stop=(m == 1))
                last.then_inc(s["out_ready"], 1)

            @block.vector
            def _(dve):
                for j in range(4):
                    dve.wait_ge(s["hidden_ready"], j + 1)
                    dve.tensor_copy(shift[:, j:j + 1], banks[:, j, 2 * N_CMP:2 * N_CMP + 1]).then_inc(s["shift_ready"], 1)
                dve.wait_ge(s["out_ready"], 1)
                for side in range(2):
                    ps = slice(side * HD, side * HD + HD)
                    dve.tensor_copy(kcT[ps, :, :], banks2[ps, side, 0:2 * N_CMP].rearrange("p (g n) -> p g n", g=2))
                dve.tensor_copy(vc[:, :, :], banks2[0:N_CMP, 2, 0:2 * HD].rearrange("p (g n) -> p g n", g=2))

            @block.scalar
            def _(act):
                for j in range(4):
                    act.wait_ge(s["shift_ready"], j + 1)
                    act.activation(hid[:, j // 2, j % 2, :], banks[:, j, 0:2 * N_CMP], ACT.Gelu_apprx_tanh,
                                   bias=shift[:, j:j + 1]).then_inc(s["gelu_ready"], 1)


def mixer_b(prog, ring, at, hT, oT, gains):
    nc, d = prog.nc, prog.dram
    with ExitStack() as ctx:
        tables = prog.sb(ctx, "tables_b", [P, H, 256])
        qT = prog.sb(ctx, "qT_b", [P, 4, T])
        kT = prog.sb(ctx, "kT_b", [P, 2, T])
        v_tok = prog.sb(ctx, "v_tok_b", [P, TT, P])
        sinks = prog.sb(ctx, "sinks", [P, 2, H])
        o_tok = prog.sb(ctx, "o_tok_b", [P, TT, 512])
        bias_tables(prog, tables, 1, 128)
        with prog.stage("loaded") as (block, s):
            @block.sync
            def _(sp):
                sp.dma_start(sinks[:, 0, :], d["sinks"].to_broadcast([P, H])).then_inc(s["loaded"], 16)

            @block.vector
            def _(dve):
                dve.wait_ge(s["loaded"], 16)
                dve.tensor_scalar(sinks[:, 1, :], sinks[:, 0, :], -1.0, None, ALU.mult)
        q, kv = at["b_q"], at["b_kv"]
        tiles = feature_tiles(ring, q, 512, 0, hT, qT)
        tiles += twin_tiles(ring, kv, 256, 0, hT, kT)
        tiles += token_tiles(ring, kv, 256, 128, P, hT, v_tok)
        project(prog, ring, tiles, hT, q, kv + 1)
        norm_heads(prog, [(qT[:, i, :], gains[:, 2:3]) for i in range(4)]
                   + [(kT[:, g, :], gains[:, 3:4]) for g in range(2)])
        units = []
        for h in range(H):
            g = h // 4
            for t in range(TT):
                j0 = max(0, t - 1)
                n = (t + 1 - j0) * P
                units.append(unit(qT[half(h), h // 2, t * P:(t + 1) * P], kT[half(h), g, j0 * P:j0 * P + n], n,
                                  [(P, v_tok[:, j, g * HD:(g + 1) * HD]) for j in range(j0, t + 1)],
                                  o_tok[:, t, h * HD:(h + 1) * HD], bias=tables[:, h, 256 - n:256],
                                  sink=sinks[:, 0, h:h + 1], minus_sink=sinks[:, 1, h:h + 1]))
        attention(prog, units)
        to_features(prog, o_tok, oT[:, 1, :, :])


def mixer_c(prog, ring, at, hT, oT, gains):
    nc, d = prog.nc, prog.dram
    with ExitStack() as ctx:
        qT = prog.sb(ctx, "qT_c", [P, 4, T])
        kT = prog.sb(ctx, "kT_c", [P, 4, T])
        v_tok = prog.sb(ctx, "v_tok_c", [P, TT, 512])
        f = prog.sb(ctx, "f", [H, T])
        o_tok = prog.sb(ctx, "o_tok_c", [P, TT, 512])
        left = prog.sb(ctx, "left", [P, T])
        right = prog.sb(ctx, "right", [P, H, T])
        c = at["c_v"]
        tiles = feature_tiles(ring, at["c_q"], 512, 0, hT, qT)
        tiles += feature_tiles(ring, at["c_k"], 512, 0, hT, kT)
        tiles += token_tiles(ring, c, 512, 0, 512, hT, v_tok)
        wf = ring.slot(c, DK, H, DK * 512)
        tiles.append((c, lambda k: wf[:, k, :], lambda k: hT[:, k, :], H, T, [(slice(0, H), slice(0, T), f[:, :])]))
        project(prog, ring, tiles, hT, at["c_q"], c + 1)
        norm_heads(prog, [(qT[:, i, :], gains[:, 4:5]) for i in range(4)]
                   + [(kT[:, i, :], gains[:, 5:6]) for i in range(4)])
        with ExitStack() as inner:
            fb = prog.sb(inner, "fb", [H, 1])
            work = prog.sb(inner, "work", [H, 3, T])
            minus = prog.sb(inner, "minus", [P, T])
            with prog.stage("loaded", "step", "logs_ready", "minus_ready", "ones_ready") as (block, s):
                @block.sync
                def _(sp):
                    sp.dma_start(fb[:, :], d["forget_bias"].rearrange("a h -> h a")).then_inc(s["loaded"], 16)

                @block.scalar
                def _(act):
                    link = Chain(s["step"], act)
                    act.wait_ge(s["loaded"], 16)
                    link(act.activation(work[:, 0, :], f[:, :], ACT.Identity, bias=fb[:, 0:1]))
                    link(act.activation(work[:, 1, :], work[:, 0, :], ACT.Abs))
                    link(act.activation(work[:, 1, :], work[:, 1, :], ACT.Exp, scale=-1.0))
                    act.activation(work[:, 1, :], work[:, 1, :], ACT.Ln, bias=1.0).then_inc(s["logs_ready"], 1)

                @block.gpsimd
                def _(pool):
                    pool.memset(right[:, :, :], 0.0).then_inc(s["ones_ready"], 1)
                    pool.memset(left[:, :], 0.0).then_inc(s["ones_ready"], 1)

                @block.vector
                def _(dve):
                    dve.wait_ge(s["logs_ready"], 1)
                    dve.wait_ge(s["ones_ready"], 2)

                    def link(ins, n):
                        ins.then_inc(s["minus_ready"], 1)
                        dve.wait_ge(s["minus_ready"], n)

                    link(dve.scalar_tensor_tensor(out=work[:, 2, :], in0=work[:, 0, :], scalar=0.0,
                                                  in1=work[:, 1, :], op0=ALU.min, op1=ALU.subtract), 1)
                    link(dve.tensor_tensor_scan(left[0:H, :], prog.ones[0:H, 0:1].to_broadcast([H, T]),
                                                work[:, 2, :], 0.0, ALU.mult, ALU.add), 2)
                    link(dve.tensor_copy(left[HD:HD + H, :], left[0:H, :]), 3)
                    for base in (0, HD):
                        lo, hi = slice(base, base + H), slice(base + 32, base + 32 + H)
                        link(dve.tensor_scalar(minus[hi, :], left[lo, :], -1.0, None, ALU.mult), 4 + base // HD)
                        dve.memset(left[hi, :], 1.0)
                        for h in range(base // HD, H, 2):
                            dve.tensor_scalar(right[lo, h, :], prog.zeros[lo, :], prog.fox[lo, h:h + 1], None, ALU.add)
                            dve.tensor_scalar(right[hi, h, :], minus[hi, :], prog.fox[hi, h:h + 1], None, ALU.mult)
        units = []
        for h in range(H):
            for t in range(TT):
                n = (t + 1) * P
                units.append(unit(qT[half(h), h // 2, t * P:(t + 1) * P], kT[half(h), h // 2, 0:n], n,
                                  [(P, v_tok[:, j, h * HD:(h + 1) * HD]) for j in range(t + 1)],
                                  o_tok[:, t, h * HD:(h + 1) * HD], bias=prog.causal[:, T - n:T],
                                  extra=((left[rows_of(h), t * P:(t + 1) * P], right[rows_of(h), h, 0:n]), n)))
        attention(prog, units)
        to_features(prog, o_tok, oT[:, 2, :, :])


def merge_branches(prog, ring, c0, hT, oT, yT, n_branch):
    nc = prog.nc
    with ExitStack() as ctx:
        gate = prog.sb(ctx, "gate", [P, 2, T])
        part = prog.sb(ctx, "part", [P, 2, T])
        gate_ps = prog.ps(ctx, "gate_ps", [P, 2, T])
        branch_ps = prog.ps(ctx, "branch_ps", [P, 2, T])
        with prog.stage("gate_made", "branch_made", "gate_ready", "part_ready", "added") as (block, s):
            @block.sync
            def _(sp):
                ring.run_ahead(sp, c0 + DK)

            @block.tensor
            def _(pe):
                for m in range(DK):
                    ring.wait(pe, c0 + m)
                    for b in range(n_branch):
                        i = n_branch * m + b
                        wm = ring.slot(c0 + m, DK, P, b * DK * P)
                        wb = ring.slot(c0 + m, 4, P, n_branch * DK * P + b * 4 * P)
                        if i >= 2:
                            pe.wait_ge(s["gate_ready"], i - 1)
                        for k in range(DK):
                            last = pe.matmul(gate_ps[:, i % 2, :], wm[:, k, :], hT[:, k, :], start=(k == 0),
                                             stop=(k == DK - 1))
                        last.then_inc(s["gate_made"], 1)
                        if i >= 2:
                            pe.wait_ge(s["part_ready"], i - 1)
                        for k in range(4):
                            last = pe.matmul(branch_ps[:, i % 2, :], wb[:, k, :], oT[:, b, k, :], start=(k == 0),
                                             stop=(k == 3))
                        last.then_inc(s["branch_made"], 1)
                    pe.wait_ge(s["branch_made"], n_branch * (m + 1))
                    pe.sem_inc(ring.used, 1)

            @block.scalar
            def _(act):
                for i in range(n_branch * DK):
                    act.wait_ge(s["gate_made"], i + 1)
                    if i >= 2:
                        act.wait_ge(s["part_ready"], i - 1)
                    act.activation(gate[:, i % 2, :], gate_ps[:, i % 2, :], ACT.Sigmoid).then_inc(s["gate_ready"], 1)

            @block.vector
            def _(dve):
                added = 0
                for i in range(n_branch * DK):
                    m, b = i // n_branch, i % n_branch
                    dst = yT[:, m, :] if b == 0 else part[:, b - 1, :]
                    dve.wait_ge(s["gate_ready"], i + 1)
                    dve.wait_ge(s["branch_made"], i + 1)
                    dve.tensor_tensor(dst, branch_ps[:, i % 2, :], gate[:, i % 2, :], ALU.mult).then_inc(s["part_ready"], 1)
                    dve.wait_ge(s["part_ready"], i + 1)
                    if b:
                        dve.tensor_tensor(yT[:, m, :], yT[:, m, :], dst, ALU.add).then_inc(s["added"], 1)
                        added += 1
                        dve.wait_ge(s["added"], added)


def residual_product(prog, ring, c0, yT, xT, factor=None):
    nc = prog.nc
    with ExitStack() as ctx:
        banks = prog.ps(ctx, "banks", [P, 4, T])
        with prog.stage("made", "added") as (block, s):
            @block.sync
            def _(sp):
                ring.run_ahead(sp, c0 + 2)

            @block.tensor
            def _(pe):
                for m in range(DK):
                    c = c0 + m // 4
                    if m % 4 == 0:
                        ring.wait(pe, c)
                    w = ring.slot(c, DK, 512)
                    if m >= 4:
                        pe.wait_ge(s["added"], m - 3)
                    for k in range(DK):
                        last = pe.matmul(banks[:, m % 4, :], w[:, k, (m % 4) * P:(m % 4 + 1) * P], yT[:, k, :],
                                         start=(k == 0), stop=(k == DK - 1))
                    last.then_inc(s["made"], 1)
                    if m % 4 == 3:
                        pe.wait_ge(s["made"], m + 1)
                        pe.sem_inc(ring.used, 1)

            @block.vector
            def _(dve):
                for m in range(DK):
                    dve.wait_ge(s["made"], m + 1)
                    scale = 1.0 if factor is None else factor[:, m:m + 1]
                    dve.scalar_tensor_tensor(out=xT[:, m, :], in0=banks[:, m % 4, :], scalar=scale, in1=xT[:, m, :],
                                             op0=ALU.mult, op1=ALU.add).then_inc(s["added"], 1)


def conv_ffn(prog, ring, at, hT, xT, conv_w, conv_b):
    nc = prog.nc
    with ExitStack() as ctx:
        hid = prog.sb(ctx, "hid_ffn", [P, FT, T])
        taps = prog.sb(ctx, "taps", [P, 2, T])
        gate_ps = prog.ps(ctx, "gate_ps", [P, 2, T])
        up_ps = prog.ps(ctx, "up_ps", [P, 2, T])
        c0 = at["ffn"]
        with prog.stage("gate_made", "up_made", "tap_ready", "conv_ready", "gelu_ready", "hid_ready", "step") as (block, s):
            @block.sync
            def _(sp):
                ring.run_ahead(sp, c0 + FT // 2)

            @block.tensor
            def _(pe):
                for m in range(FT):
                    c = c0 + m // 2
                    if m % 2 == 0:
                        ring.wait(pe, c)
                    for j, (bank, ready) in enumerate(((gate_ps, s["gate_made"]), (up_ps, s["up_made"]))):
                        w = ring.slot(c, DK, 256, j * DK * 256)
                        if m >= 2:
                            pe.wait_ge(s["conv_ready"] if j == 0 else s["hid_ready"], m - 1)
                        for k in range(DK):
                            last = pe.matmul(bank[:, m % 2, :], w[:, k, (m % 2) * P:(m % 2 + 1) * P], hT[:, k, :],
                                             start=(k == 0), stop=(k == DK - 1))
                        last.then_inc(ready, 1)
                    if m % 2 == 1:
                        pe.wait_ge(s["up_made"], m + 1)
                        pe.sem_inc(ring.used, 1)

            @block.scalar
            def _(act):
                def tap(m):
                    act.wait_ge(s["gate_made"], m + 1)
                    if m >= 2:
                        act.wait_ge(s["hid_ready"], m - 1)
                    act.activation(taps[:, m % 2, :], gate_ps[:, m % 2, :], ACT.Copy,
                                   scale=conv_w[:, 2, m:m + 1]).then_inc(s["tap_ready"], 1)

                def gelu(m):
                    act.wait_ge(s["conv_ready"], m + 1)
                    act.activation(taps[:, m % 2, :], taps[:, m % 2, :], ACT.Gelu_apprx_tanh,
                                   bias=conv_b[:, m:m + 1]).then_inc(s["gelu_ready"], 1)

                for m in range(FT):
                    tap(m)
                    if m >= 1:
                        gelu(m - 1)
                gelu(FT - 1)

            @block.vector
            def _(dve):
                def conv(m):
                    dve.wait_ge(s["tap_ready"], m + 1)
                    for i in (1, 2):
                        dve.scalar_tensor_tensor(out=taps[:, m % 2, i:T], in0=gate_ps[:, m % 2, 0:T - i],
                                                 scalar=conv_w[:, 2 - i, m:m + 1], in1=taps[:, m % 2, i:T],
                                                 op0=ALU.mult, op1=ALU.add).then_inc(s["conv_ready"] if i == 2 else s["step"], 1)
                        if i == 1:
                            dve.wait_ge(s["step"], m + 1)

                def product(m):
                    dve.wait_ge(s["gelu_ready"], m + 1)
                    dve.wait_ge(s["up_made"], m + 1)
                    dve.tensor_tensor(hid[:, m, :], up_ps[:, m % 2, :], taps[:, m % 2, :], ALU.mult).then_inc(s["hid_ready"], 1)

                for m in range(FT):
                    conv(m)
                    if m >= 1:
                        product(m - 1)
                product(FT - 1)
        banks = prog.ps(ctx, "down", [P, 4, T])
        c1 = at["w_down"]
        with prog.stage("made", "added") as (block, s):
            @block.sync
            def _(sp):
                ring.run_ahead(sp, c1 + DK)

            @block.tensor
            def _(pe):
                for m in range(DK):
                    ring.wait(pe, c1 + m)
                    w = ring.slot(c1 + m, FT, P)
                    if m >= 4:
                        pe.wait_ge(s["added"], m - 3)
                    for k in range(FT):
                        last = pe.matmul(banks[:, m % 4, :], w[:, k, :], hid[:, k, :], start=(k == 0),
                                         stop=(k == FT - 1))
                    last.then_inc(s["made"], 1)
                    pe.wait_ge(s["made"], m + 1)
                    pe.sem_inc(ring.used, 1)

            @block.vector
            def _(dve):
                for m in range(DK):
                    dve.wait_ge(s["made"], m + 1)
                    dve.tensor_tensor(xT[:, m, :], banks[:, m % 4, :], xT[:, m, :], ALU.add).then_inc(s["added"], 1)



LAYERS = 2
ALPHA = (2 * LAYERS) ** 0.25
LN_EPS = 1e-5
SGU = 512
SGU_GROUPS = 8
EXPERTS, TOP, GROUPS, TOP_GROUPS = 64, 8, 8, 4
FF = 256
ROUTED_SCALE = 2.5
EXPERT = 3 * DK * FF
BUFFERS = SLOTS * SLOT // EXPERT
SHIFT1, SCALE1, GATE1, SHIFT2, SCALE2, GATE2 = [i * DK for i in range(6)]
C2_Q, C2_K, C2_V, C2_U, C2_Z, C2_GA, C2_GB = 0, 512, 640, 768, 1280, 1792, 2816


def second_chunks(d, l):
    w, ada = rows(d["w_in_2"][l]), rows(d["w_ada_2"][l])
    wba, wbb, wo = rows(d["w_branch_a_2"][l], 4), rows(d["w_branch_b_2"][l], 4), rows(d["w_out_2"][l])
    out, chunks = {}, []

    def add(name, *parts):
        out.setdefault(name, len(chunks))
        at, listed = 0, []
        for view in parts:
            k, n = view.shape[1], view.shape[2]
            listed.append((at, k, n, view))
            at += k * n
        chunks.append(listed)

    for m in range(12):
        add("ada", ada[:, :, m * 512:(m + 1) * 512])
    add("q", w[:, :, C2_Q:C2_Q + 512])
    add("kv", w[:, :, C2_K:C2_K + 256])
    add("u", w[:, :, C2_U:C2_U + 512])
    add("z", w[:, :, C2_Z:C2_Z + 512])
    for m in range(DK):
        add("merge", w[:, :, C2_GA + m * P:C2_GA + (m + 1) * P], w[:, :, C2_GB + m * P:C2_GB + (m + 1) * P],
            wba[:, :, m * P:(m + 1) * P], wbb[:, :, m * P:(m + 1) * P])
    for m in range(2):
        add("w_out", wo[:, :, m * 512:(m + 1) * 512])
    add("shared", rows(d["ws_gate_2"][l]), rows(d["ws_up_2"][l]))
    add("shared_down", rows(d["ws_down_2"][l], 2))
    return chunks, out


def modulation(prog, ring, c0, l, cond, mod):
    nc, d = prog.nc, prog.dram
    n = 6 * DK
    with ExitStack() as ctx:
        bias = prog.sb(ctx, "b_ada", [P, n])
        bank = prog.ps(ctx, "mod_ps", [P, n])
        with prog.stage("loaded", "made", "step") as (block, s):
            @block.sync
            def _(sp):
                with nc.allow_non_contiguous_dma(reason="24 KB"):
                    sp.dma_start(bias[:, :], column(d["b_ada_2"][l])).then_inc(s["loaded"], 16)
                ring.run_ahead(sp, c0 + 12)

            @block.tensor
            def _(pe):
                for j in range(n):
                    c = c0 + j // 4
                    if j % 4 == 0:
                        ring.wait(pe, c)
                    w = ring.slot(c, DK, 512)
                    for k in range(DK):
                        last = pe.matmul(bank[:, j:j + 1], w[:, k, (j % 4) * P:(j % 4 + 1) * P], cond[:, k:k + 1],
                                         start=(k == 0), stop=(k == DK - 1))
                    if j % 4 == 3:
                        last.then_inc(s["made"], 1)
                        pe.wait_ge(s["made"], j // 4 + 1)
                        pe.sem_inc(ring.used, 1)

            @block.vector
            def _(dve):
                link = Chain(s["step"], dve)
                dve.wait_ge(s["loaded"], 16)
                dve.wait_ge(s["made"], n // 4)
                link(dve.tensor_tensor(mod[:, :], bank[:, :], bias[:, :], ALU.add))
                for at in (SCALE1, SCALE2):
                    link(dve.tensor_scalar(mod[:, at:at + DK], mod[:, at:at + DK], 1.0, None, ALU.add))


def modulate(prog, xT, hT, mod, scale, shift):
    with prog.stage("read") as (block, s):
        @block.vector
        def _(dve):
            for k in range(DK):
                dve.tensor_scalar(hT[:, k, :], xT[:, k, :], mod[:, scale + k:scale + k + 1],
                                  mod[:, shift + k:shift + k + 1], ALU.mult, ALU.add).then_inc(s["read"], 1)

        @block.scalar
        def _(act):
            for k in range(DK):
                act.wait_ge(s["read"], k + 1)
                act.mul(xT[:, k, :], xT[:, k, :], ALPHA)


def layer_norm(prog, xT, gain, shift):
    nc = prog.nc
    with ExitStack() as ctx:
        sq = prog.sb(ctx, "squares", [P, 2, T])
        mean = prog.sb(ctx, "mean", [P, T])
        root = prog.sb(ctx, "root", [P, T])
        rstd = prog.sb(ctx, "rstd", [P, T])
        total = prog.ps(ctx, "total", [P, 2, T])
        with prog.stage("total_ready", "mean_ready", "centred", "squared", "summed", "root_ready",
                        "rstd_ready", "scaled") as (block, s):
            @block.tensor
            def _(pe):
                for k in range(DK):
                    last = pe.matmul(total[:, 0, :], prog.ones[:, :], xT[:, k, :], start=(k == 0), stop=(k == DK - 1))
                last.then_inc(s["total_ready"], 1)
                for k in range(DK):
                    pe.wait_ge(s["squared"], k + 1)
                    pe.matmul(total[:, 1, :], prog.ones[:, :], sq[:, k % 2, :], start=(k == 0),
                              stop=(k == DK - 1)).then_inc(s["summed"], 1)

            @block.scalar
            def _(act):
                for k in range(DK):
                    act.wait_ge(s["centred"], k + 1)
                    if k >= 2:
                        act.wait_ge(s["summed"], k - 1)
                    act.activation(sq[:, k % 2, :], xT[:, k, :], ACT.Square).then_inc(s["squared"], 1)
                act.wait_ge(s["summed"], DK)
                act.activation(root[:, :], total[:, 1, :], ACT.Sqrt, bias=prog.ln_eps[:, 0:1],
                               scale=1.0 / D).then_inc(s["root_ready"], 1)
                for k in range(DK):
                    act.wait_ge(s["scaled"], k + 1)
                    act.activation(xT[:, k, :], xT[:, k, :], ACT.Identity, bias=shift[:, k:k + 1])

            @block.vector
            def _(dve):
                dve.wait_ge(s["total_ready"], 1)
                dve.tensor_scalar(mean[:, :], total[:, 0, :], 1.0 / D, None, ALU.mult).then_inc(s["mean_ready"], 1)
                dve.wait_ge(s["mean_ready"], 1)
                for k in range(DK):
                    dve.tensor_tensor(xT[:, k, :], xT[:, k, :], mean[:, :], ALU.subtract).then_inc(s["centred"], 1)
                dve.wait_ge(s["root_ready"], 1)
                dve.reciprocal(rstd[:, :], root[:, :]).then_inc(s["rstd_ready"], 1)
                dve.wait_ge(s["rstd_ready"], 1)
                for k in range(DK):
                    dve.scalar_tensor_tensor(out=xT[:, k, :], in0=xT[:, k, :], scalar=gain[:, k:k + 1],
                                             in1=rstd[:, :], op0=ALU.mult, op1=ALU.mult).then_inc(s["scaled"], 1)


def rotate(prog, tiles):
    nc, d = prog.nc, prog.dram
    with ExitStack() as ctx:
        rope = prog.sb(ctx, "rope", [P, 2 * T + P])
        turned = prog.sb(ctx, "rotated", [P, 2, T])
        banks = prog.ps(ctx, "swapped", [P, 2, T])
        cos, sin, swap = rope[:, 0:T], rope[:, T:2 * T], rope[:, 2 * T:2 * T + P]
        with prog.stage("loaded", "swapped", "sin_ready", "cos_ready", "done") as (block, s):
            @block.sync
            def _(sp):
                sp.dma_start(rope[:, :], d["cst_rope"]).then_inc(s["loaded"], 16)

            @block.tensor
            def _(pe):
                pe.wait_ge(s["loaded"], 16)
                for i, x in enumerate(tiles):
                    if i >= 2:
                        pe.wait_ge(s["sin_ready"], i - 1)
                    pe.matmul(banks[:, i % 2, :], swap, x, start=True, stop=True).then_inc(s["swapped"], 1)

            @block.vector
            def _(dve):
                for i, x in enumerate(tiles):
                    dve.wait_ge(s["swapped"], i + 1)
                    dve.tensor_tensor(turned[:, i % 2, :], banks[:, i % 2, :], sin, ALU.mult).then_inc(s["sin_ready"], 1)
                    dve.tensor_tensor(x, x, cos, ALU.mult).then_inc(s["cos_ready"], 1)
                    dve.wait_ge(s["sin_ready"], i + 1)
                    dve.wait_ge(s["cos_ready"], i + 1)
                    dve.tensor_tensor(x, x, turned[:, i % 2, :], ALU.add).then_inc(s["done"], 1)
                    dve.wait_ge(s["done"], i + 1)


def self_attention(prog, ring, at, hT, oT, qk):
    with ExitStack() as ctx:
        qT = prog.sb(ctx, "qT_s", [P, 4, T])
        kT = prog.sb(ctx, "kT_s", [P, 2, T])
        v_tok = prog.sb(ctx, "v_tok_s", [P, TT, P])
        o_tok = prog.sb(ctx, "o_tok_s", [P, TT, 512])
        q, kv = at["q"], at["kv"]
        tiles = feature_tiles(ring, q, 512, 0, hT, qT)
        tiles += twin_tiles(ring, kv, 256, 0, hT, kT)
        tiles += token_tiles(ring, kv, 256, 128, P, hT, v_tok)
        project(prog, ring, tiles, hT, q, kv + 1)
        norm_heads(prog, [(qT[:, i, :], qk[:, 0:1]) for i in range(4)] + [(kT[:, g, :], qk[:, 1:2]) for g in range(2)])
        rotate(prog, [qT[:, i, :] for i in range(4)] + [kT[:, g, :] for g in range(2)])
        units = []
        for h in range(H):
            g = h // 4
            for t in range(TT):
                units.append(unit(qT[half(h), h // 2, t * P:(t + 1) * P], kT[half(h), g, :], T,
                                  [(P, v_tok[:, j, g * HD:(g + 1) * HD]) for j in range(TT)],
                                  o_tok[:, t, h * HD:(h + 1) * HD]))
        attention(prog, units)
        to_features(prog, o_tok, oT)


def spatial_gating(prog, ring, at, l, hT, oT):
    nc, d = prog.nc, prog.dram
    with ExitStack() as ctx:
        v = prog.sb(ctx, "v_sgu", [P, TT, SGU])
        affine = prog.sb(ctx, "affine", [P, 2, SGU])
        w_s = prog.sb(ctx, "w_s", [P, SGU_GROUPS, P])
        w_sT = prog.sb(ctx, "w_sT", [P, SGU_GROUPS, P])
        b_s = prog.sb(ctx, "b_s", [SGU_GROUPS, P])
        pairs = prog.sb(ctx, "pairs", [SGU_GROUPS, SGU])
        b_wide = prog.sb(ctx, "b_wide", [P, 4, P])
        stats = prog.sb(ctx, "stats", [P, TT, 6])
        moments = prog.sb(ctx, "moments", [P, TT, 4])
        work = prog.sb(ctx, "work", [P, 2, T])
        u, z = at["u"], at["z"]
        tiles = feature_tiles(ring, u, 512, 0, hT, oT)
        tiles += token_tiles(ring, z, 512, 0, 512, hT, v)
        project(prog, ring, tiles, hT, u, z + 1)
        wide = prog.ps(ctx, "wide", [P, 4, P])
        banks = prog.ps(ctx, "mixed", [P, 2, T])
        with prog.stage("loaded", "gelu_u", "gelu_v", "step", "moments_ready", "root_ready") as (block, s):
            @block.sync
            def _(sp):
                sp.dma_start(w_s[:, :, :], d["w_spatial_2"][l].rearrange("g i j -> i g j")).then_inc(s["loaded"], 16)
                sp.dma_start(b_s[:, :], d["b_spatial_2"][l]).then_inc(s["loaded"], 16)
                sp.dma_start(pairs[:, :], d["cst_pairs"]).then_inc(s["loaded"], 16)
                sp.dma_start(affine[:, 0, :], d["sgu_ln_g_2"][bass.ds(l, 1), :].to_broadcast([P, SGU])).then_inc(s["loaded"], 16)
                sp.dma_start(affine[:, 1, :], d["sgu_ln_b_2"][bass.ds(l, 1), :].to_broadcast([P, SGU])).then_inc(s["loaded"], 16)
                sp.wait_ge(s["loaded"], 80)

            @block.scalar
            def _(act):
                for t in range(TT):
                    act.activation(v[:, t, :], v[:, t, :], ACT.Gelu).then_inc(s["gelu_v"], 1)
                for m in range(4):
                    act.activation(oT[:, m, :], oT[:, m, :], ACT.Gelu)
                act.wait_ge(s["moments_ready"], TT)
                act.activation(moments[:, :, 2], moments[:, :, 1], ACT.Sqrt,
                               bias=prog.ln_eps[:, 0:1]).then_inc(s["root_ready"], 1)

            @block.vector
            def _(dve):
                link = Chain(s["step"], dve)
                for t in range(TT):
                    dve.wait_ge(s["gelu_v"], t + 1)
                    link(dve.bn_stats(stats[:, t, :], v[:, t, :]))
                    dve.bn_aggr(moments[:, t, 0:2], stats[:, t, :]).then_inc(s["moments_ready"], 1)
                dve.wait_ge(s["root_ready"], 1)
                dve.wait_ge(s["loaded"], 80)
                link(dve.reciprocal(moments[:, :, 3], moments[:, :, 2]))
                for t in range(TT):
                    link(dve.tensor_scalar(v[:, t, :], v[:, t, :], moments[:, t, 0:1], moments[:, t, 3:4],
                                           ALU.subtract, ALU.mult))
                    link(dve.tensor_tensor(v[:, t, :], v[:, t, :], affine[:, 0, :], ALU.mult))
                    link(dve.tensor_tensor(v[:, t, :], v[:, t, :], affine[:, 1, :], ALU.add))
        transpose_tiles(prog, [([w_s[:, g, :] for g in range(4 * j, 4 * j + 4)],
                                w_sT[:, 4 * j:4 * j + 4, :].rearrange("p g i -> p (g i)")) for j in range(2)])
        with prog.stage("wide_ready", "b_ready", "mixed_ready", "step") as (block, s):
            @block.tensor
            def _(pe):
                for m in range(4):
                    last = pe.matmul(wide[:, m, :], pairs[:, m * P:(m + 1) * P], b_s[:, :], start=True, stop=True)
                last.then_inc(s["wide_ready"], 1)
                for m in range(4):
                    if m >= 2:
                        pe.wait_ge(s["step"], 2 * (m - 1))
                    for g in (2 * m, 2 * m + 1):
                        ps = half(g)
                        for t in range(TT):
                            last = pe.matmul(banks[ps, m % 2, t * P:(t + 1) * P], v[:, t, g * HD:(g + 1) * HD],
                                             w_sT[:, g, :], start=True, stop=True)
                    last.then_inc(s["mixed_ready"], 1)

            @block.vector
            def _(dve):
                link = Chain(s["step"], dve)
                dve.wait_ge(s["wide_ready"], 1)
                dve.tensor_copy(b_wide[:, :, :], wide[:, :, :]).then_inc(s["b_ready"], 1)
                dve.wait_ge(s["b_ready"], 1)
                for m in range(4):
                    dve.wait_ge(s["mixed_ready"], m + 1)
                    for_each = b_wide[:, m:m + 1, :].to_broadcast([P, TT, P])
                    link(dve.tensor_tensor(work[:, m % 2, :].rearrange("p (t i) -> p t i", t=TT),
                                           banks[:, m % 2, :].rearrange("p (t i) -> p t i", t=TT), for_each, ALU.add))
                    link(dve.tensor_tensor(oT[:, m, :], oT[:, m, :], work[:, m % 2, :], ALU.mult))


def route(prog, l, hT, weight):
    nc, d = prog.nc, prog.dram
    with ExitStack() as ctx:
        rw = prog.sb(ctx, "router", [P, DK, EXPERTS])
        rb = prog.sb(ctx, "router_bias", [P, EXPERTS])
        score = prog.sb(ctx, "score", [P, TT, EXPERTS])
        sel = prog.sb(ctx, "sel", [P, TT, EXPERTS])
        left = prog.sb(ctx, "left_over", [P, TT, EXPERTS])
        best = prog.sb(ctx, "best", [P, TT, GROUPS, 8])
        groups = prog.sb(ctx, "group_scores", [P, TT, 2 * GROUPS])
        rank = prog.sb(ctx, "rank", [P, TT, 2 * GROUPS])
        mass = prog.sb(ctx, "mass", [P, TT, 2])
        bank = prog.ps(ctx, "router_ps", [P, TT, EXPERTS])
        NONE = -3e38
        with prog.stage("loaded", "made", "scored", "step") as (block, s):
            @block.sync
            def _(sp):
                sp.dma_start(rw[:, :, :], rows(d["router_w_2"][l])).then_inc(s["loaded"], 16)
                sp.dma_start(rb[:, :], d["router_bias_2"][bass.ds(l, 1), :].to_broadcast([P, EXPERTS])).then_inc(s["loaded"], 16)

            @block.tensor
            def _(pe):
                pe.wait_ge(s["loaded"], 32)
                for t in range(TT):
                    for k in range(DK):
                        last = pe.matmul(bank[:, t, :], hT[:, k, t * P:(t + 1) * P], rw[:, k, :], start=(k == 0),
                                         stop=(k == DK - 1))
                last.then_inc(s["made"], 1)

            @block.scalar
            def _(act):
                act.wait_ge(s["made"], 1)
                act.activation(score[:, :, :], bank[:, :, :], ACT.Sigmoid).then_inc(s["scored"], 1)

            @block.vector
            def _(dve):
                link = Chain(s["step"], dve)
                dve.wait_ge(s["scored"], 1)
                dve.wait_ge(s["loaded"], 32)
                link(dve.memset(groups[:, :, :], NONE))
                link(dve.tensor_tensor(sel[:, :, :], score[:, :, :],
                                       rb[:, :].unsqueeze(1).to_broadcast([P, TT, EXPERTS]), ALU.add))
                for t in range(TT):
                    for g in range(GROUPS):
                        last = dve.max(best[:, t, g, :], sel[:, t, g * 8:(g + 1) * 8])
                link(last)
                link(dve.tensor_tensor(groups[:, :, 0:GROUPS], best[:, :, :, 0], best[:, :, :, 1], ALU.add))
                for t in range(TT):
                    last = dve.max(rank[:, t, 0:8], groups[:, t, 0:GROUPS])
                link(last)
                link(dve.memset(rank[:, :, TOP_GROUPS:8], NONE))
                for t in range(TT):
                    last = dve.match_replace(left[:, t, 0:2 * GROUPS], rank[:, t, 0:8], groups[:, t, :], -2e38)
                link(last)
                link(dve.tensor_tensor(groups[:, :, 0:GROUPS], left[:, :, 0:GROUPS], groups[:, :, 0:GROUPS],
                                       ALU.not_equal))
                spread = groups[:, :, 0:GROUPS].unsqueeze(3).to_broadcast([P, TT, GROUPS, 8])
                by_group = (lambda x: x[:, :, :].rearrange("p t (g e) -> p t g e", g=GROUPS))
                link(dve.tensor_tensor(by_group(sel), by_group(sel), spread, ALU.mult))
                link(dve.tensor_scalar(groups[:, :, 0:GROUPS], groups[:, :, 0:GROUPS], 1.0, 1e30, ALU.subtract,
                                       ALU.mult))
                link(dve.tensor_tensor(by_group(sel), by_group(sel), spread, ALU.add))
                for t in range(TT):
                    last = dve.max(rank[:, t, 0:8], sel[:, t, :])
                link(last)
                for t in range(TT):
                    last = dve.match_replace(left[:, t, :], rank[:, t, 0:8], sel[:, t, :], NONE)
                link(last)
                link(dve.tensor_tensor(sel[:, :, :], left[:, :, :], sel[:, :, :], ALU.not_equal))
                link(dve.tensor_tensor(weight[:, :, :], score[:, :, :], sel[:, :, :], ALU.mult))
                link(dve.tensor_reduce(mass[:, :, 0], weight[:, :, :], AX.X, ALU.add))
                link(dve.reciprocal(mass[:, :, 1], mass[:, :, 0]))
                for t in range(TT):
                    link(dve.tensor_scalar(weight[:, t, :], weight[:, t, :], mass[:, t, 1:2], ROUTED_SCALE, ALU.mult,
                                           ALU.mult))


def experts(prog, ring, at, l, hT, weight, acc):
    nc, d = prog.nc, prog.dram
    mem = ring.mem[:, :, :].rearrange("p s n -> p (s n)")
    with ExitStack() as ctx:
        act_sb = prog.sb(ctx, "gated", [P, 2, T])
        hid = prog.sb(ctx, "hid_moe", [P, BUFFERS, 2, T])
        gate_ps = prog.ps(ctx, "gate_ps", [P, 2, T])
        up_ps = prog.ps(ctx, "up_ps", [P, 2, T])
        down_ps = prog.ps(ctx, "down_ps", [P, 4, T])
        c0 = at["shared"]
        with prog.stage("loaded", "gate_made", "up_made", "silu_ready", "hid_ready", "down_made", "added") as (block, s):
            @block.sync
            def _(sp):
                ring.run_ahead(sp, c0 + 2)

            @block.tensor
            def _(pe):
                ring.wait(pe, c0)
                for m in range(2):
                    for j, (bank, ready) in enumerate(((gate_ps, s["gate_made"]), (up_ps, s["up_made"]))):
                        w = ring.slot(c0, DK, FF, j * DK * FF)
                        for k in range(DK):
                            last = pe.matmul(bank[:, m, :], w[:, k, m * P:(m + 1) * P], hT[:, k, :], start=(k == 0),
                                             stop=(k == DK - 1))
                        last.then_inc(ready, 1)
                ring.wait(pe, c0 + 1)
                pe.wait_ge(s["hid_ready"], 2)
                w = ring.slot(c0 + 1, 2, D)
                for j in range(2 * TT):
                    t, side = j // 2, j % 2
                    if j >= 4:
                        pe.wait_ge(s["added"], j - 3)
                    for k in range(2):
                        last = pe.matmul(down_ps[:, j % 4, :], hid[:, 0, k, t * P:(t + 1) * P],
                                         w[:, k, side * 512:(side + 1) * 512], start=(k == 0), stop=(k == 1))
                    last.then_inc(s["down_made"], 1)

            @block.scalar
            def _(act):
                for m in range(2):
                    act.wait_ge(s["gate_made"], m + 1)
                    act.activation(act_sb[:, m, :], gate_ps[:, m, :], ACT.Silu).then_inc(s["silu_ready"], 1)

            @block.vector
            def _(dve):
                for m in range(2):
                    dve.wait_ge(s["silu_ready"], m + 1)
                    dve.wait_ge(s["up_made"], m + 1)
                    dve.tensor_tensor(hid[:, 0, m, :], up_ps[:, m, :], act_sb[:, m, :], ALU.mult).then_inc(s["hid_ready"], 1)
                for j in range(2 * TT):
                    t, side = j // 2, j % 2
                    dve.wait_ge(s["down_made"], j + 1)
                    dve.tensor_copy(acc[:, t, side * 512:(side + 1) * 512], down_ps[:, j % 4, :]).then_inc(s["added"], 1)

        wg, wu, wd = d["w_gate_2"], d["w_up_2"], d["w_down_2"]
        with prog.stage("loaded_0", "loaded_1", "loaded_2", "gate_made", "up_made", "silu_ready", "hid_ready",
                        "down_made", "added") as (block, s):
            loaded = (s["loaded_0"], s["loaded_1"], s["loaded_2"])

            def part(b, at, k, n):
                return mem[:, b * EXPERT + at:b * EXPERT + at + k * n].rearrange("p (k n) -> p k n", k=k)

            turns = EXPERTS // BUFFERS

            @block.sync
            def _(sp):
                def load(e, b):
                    sp.dma_start(part(b, 0, DK, FF), rows(wg[l, e])).then_inc(loaded[b], 16)
                    sp.dma_start(part(b, DK * FF, DK, FF), rows(wu[l, e])).then_inc(loaded[b], 16)
                    sp.dma_start(part(b, 2 * DK * FF, 2, D), rows(wd[l, e], 2)).then_inc(loaded[b], 16)

                for b in range(BUFFERS):
                    load(b, b)
                with sp.Fori(1, turns) as r:
                    for b in range(BUFFERS):
                        sp.wait_ge(s["down_made"], 2 * TT * (BUFFERS * r + b - BUFFERS + 1))
                        load(BUFFERS * r + b, b)
                sp.wait_ge(s["down_made"], 2 * TT * (EXPERTS - BUFFERS))
                load(EXPERTS - 1, 0)

            @block.tensor
            def _(pe):
                def up(r, b, first):
                    e = BUFFERS * r + b
                    pe.wait_ge(loaded[b], 48 * (r + 1))
                    for m in range(2):
                        for j, (bank, ready) in enumerate(((gate_ps, s["gate_made"]), (up_ps, s["up_made"]))):
                            if not first:
                                pe.wait_ge(s["silu_ready"] if j == 0 else s["hid_ready"], 2 * e - 1 + m)
                            w = part(b, j * DK * FF, DK, FF)
                            for k in range(DK):
                                last = pe.matmul(bank[:, m, :], w[:, k, m * P:(m + 1) * P], hT[:, k, :],
                                                 start=(k == 0), stop=(k == DK - 1))
                            last.then_inc(ready, 1)

                def down(r, b, first):
                    e = BUFFERS * r + b
                    pe.wait_ge(s["hid_ready"], 2 * e + 2)
                    w = part(b, 2 * DK * FF, 2, D)
                    for j in range(2 * TT):
                        t, side = j // 2, j % 2
                        if not (first and j < 4):
                            pe.wait_ge(s["added"], 2 * TT * e + j - 3)
                        for k in range(2):
                            last = pe.matmul(down_ps[:, j % 4, :], hid[:, b, k, t * P:(t + 1) * P],
                                             w[:, k, side * 512:(side + 1) * 512], start=(k == 0), stop=(k == 1))
                        last.then_inc(s["down_made"], 1)

                up(0, 0, True)
                for b in range(1, BUFFERS):
                    up(0, b, False)
                    down(0, b - 1, b == 1)
                with pe.Fori(1, turns) as r:
                    up(r, 0, False)
                    down(r - 1, BUFFERS - 1, False)
                    for b in range(1, BUFFERS):
                        up(r, b, False)
                        down(r, b - 1, False)
                up(turns, 0, False)
                down(turns - 1, BUFFERS - 1, False)
                down(turns, 0, False)

            @block.scalar
            def _(act):
                def silu(e, first):
                    for m in range(2):
                        act.wait_ge(s["gate_made"], 2 * e + m + 1)
                        if not first:
                            act.wait_ge(s["hid_ready"], 2 * e + m - 1)
                        act.activation(act_sb[:, m, :], gate_ps[:, m, :], ACT.Silu).then_inc(s["silu_ready"], 1)

                silu(0, True)
                with act.Fori(1, EXPERTS) as e:
                    silu(e, False)

            @block.vector
            def _(dve):
                def product(r, b, first):
                    e = BUFFERS * r + b
                    for m in range(2):
                        dve.wait_ge(s["silu_ready"], 2 * e + m + 1)
                        dve.wait_ge(s["up_made"], 2 * e + m + 1)
                        if not first:
                            dve.wait_ge(s["down_made"], 2 * TT * (e - BUFFERS + 1))
                        dve.tensor_tensor(hid[:, b, m, :], up_ps[:, m, :], act_sb[:, m, :],
                                          ALU.mult).then_inc(s["hid_ready"], 1)

                def add(r, b, first):
                    e = BUFFERS * r + b
                    for j in range(2 * TT):
                        t, side = j // 2, j % 2
                        dve.wait_ge(s["down_made"], 2 * TT * e + j + 1)
                        if not first:
                            dve.wait_ge(s["added"], 2 * TT * (e - 1) + j + 1)
                        to = acc[:, t, side * 512:(side + 1) * 512]
                        dve.scalar_tensor_tensor(out=to, in0=down_ps[:, j % 4, :], scalar=weight[:, t, bass.ds(e, 1)],
                                                 in1=to, op0=ALU.mult, op1=ALU.add).then_inc(s["added"], 1)

                product(0, 0, True)
                for b in range(1, BUFFERS):
                    product(0, b, True)
                    add(0, b - 1, b == 1)
                with dve.Fori(1, turns) as r:
                    product(r, 0, False)
                    add(r - 1, BUFFERS - 1, False)
                    for b in range(1, BUFFERS):
                        product(r, b, False)
                        add(r, b - 1, False)
                product(turns, 0, False)
                add(turns - 1, BUFFERS - 1, False)
                add(turns, 0, False)


def add_tokens(prog, acc, xT, factor):
    nc = prog.nc
    with ExitStack() as ctx:
        banks = prog.ps(ctx, "turned_acc", [P, 4, T])
        with prog.stage("turned", "added") as (block, s):
            @block.tensor
            def _(pe):
                for m in range(DK):
                    if m >= 4:
                        pe.wait_ge(s["added"], m - 3)
                    for t in range(TT):
                        last = pe.transpose(banks[:, m % 4, t * P:(t + 1) * P], acc[:, t, m * P:(m + 1) * P],
                                            prog.ident[:, :])
                    last.then_inc(s["turned"], 1)

            @block.vector
            def _(dve):
                for m in range(DK):
                    dve.wait_ge(s["turned"], m + 1)
                    dve.scalar_tensor_tensor(out=xT[:, m, :], in0=banks[:, m % 4, :], scalar=factor[:, m:m + 1],
                                             in1=xT[:, m, :], op0=ALU.mult, op1=ALU.add).then_inc(s["added"], 1)


def second_block(prog, xT):
    nc, d = prog.nc, prog.dram
    with ExitStack() as ctx:
        cond = prog.sb(ctx, "cond", [P, DK])
        mod = prog.sb(ctx, "mod", [P, 6 * DK])
        norms = prog.sb(ctx, "norms", [P, 4, DK])
        qk = prog.sb(ctx, "qk", [P, 2])
        ring = Ring(prog, ctx, [])
        with prog.stage("loaded") as (block, s):
            @block.sync
            def _(sp):
                with nc.allow_non_contiguous_dma(reason="4 KB, once"):
                    sp.dma_start(cond[:, :], column(d["c_2"][0])).then_inc(s["loaded"], 16)

            @block.scalar
            def _(act):
                act.wait_ge(s["loaded"], 16)
                act.activation(cond[:, :], cond[:, :], ACT.Silu)
        prog.finish()
        with nc.Fori(0, LAYERS) as l:
            ring.chunks, at = second_chunks(d, l)
            ring.plan()
            with prog.stage("loaded") as (block, s):
                @block.sync
                def _(sp):
                    with nc.allow_non_contiguous_dma(reason="small vectors"):
                        for i, name in enumerate(("ln1_g_2", "ln1_b_2", "ln2_g_2", "ln2_b_2")):
                            sp.dma_start(norms[:, i, :], column(d[name][l])).then_inc(s["loaded"], 16)
                        for i, name in enumerate(("q_scale_2", "k_scale_2")):
                            view = d[name][l].rearrange("(d a) -> d a", a=1)
                            for side in range(2):
                                sp.dma_start(qk[side * HD:(side + 1) * HD, i:i + 1], view).then_inc(s["loaded"], 16)
                    ring.run_ahead(sp, 0)
                    sp.wait_ge(s["loaded"], 128)

                @block.vector
                def _(dve):
                    dve.wait_ge(s["loaded"], 128)
                    dve.tensor_scalar(qk[:, 0:1], qk[:, 0:1], HD ** -0.5, None, ALU.mult)
            modulation(prog, ring, at["ada"], l, cond, mod)
            with ExitStack() as mixer:
                hT = prog.sb(mixer, "hT_m", [P, DK, T])
                oT = prog.sb(mixer, "oT_m", [P, 2, 4, T])
                modulate(prog, xT, hT, mod, SCALE1, SHIFT1)
                self_attention(prog, ring, at, hT, oT[:, 0, :, :], qk)
                spatial_gating(prog, ring, at, l, hT, oT[:, 1, :, :])
                yT = prog.sb(mixer, "yT_m", [P, DK, T])
                merge_branches(prog, ring, at["merge"], hT, oT, yT, 2)
                residual_product(prog, ring, at["w_out"], yT, xT, mod[:, GATE1:GATE1 + DK])
            layer_norm(prog, xT, norms[:, 0, :], norms[:, 1, :])
            with ExitStack() as moe:
                hT = prog.sb(moe, "hT_e", [P, DK, T])
                weight = prog.sb(moe, "weight", [P, TT, EXPERTS])
                acc = prog.sb(moe, "acc", [P, TT, D])
                modulate(prog, xT, hT, mod, SCALE2, SHIFT2)
                route(prog, l, hT, weight)
                experts(prog, ring, at, l, hT, weight, acc)
                add_tokens(prog, acc, xT, mod[:, GATE2:GATE2 + DK])
            layer_norm(prog, xT, norms[:, 2, :], norms[:, 3, :])
            with prog.stage("none") as (block, s):
                @block.sync
                def _(sp):
                    ring.clear(sp)
            prog.finish()


def store(prog, xT, out):
    nc = prog.nc
    with ExitStack() as ctx:
        x_tok = prog.sb(ctx, "x_tok", [P, TT, D])
        transpose_tiles(prog, [([xT[:, m, t * P:(t + 1) * P] for m in range(4 * j, 4 * j + 4)],
                                x_tok[:, t, j * 512:(j + 1) * 512]) for t in range(TT) for j in range(2)])
        with prog.stage("stored") as (block, s):
            @block.sync
            def _(sp):
                for t in range(TT):
                    sp.dma_start(out[0, t * P:(t + 1) * P, :], x_tok[:, t, :]).then_inc(s["stored"], 16)
                sp.wait_ge(s["stored"], 16 * TT)


def build(nc, dram, out):
    prog = Program(nc, dram)
    dram["scratch"] = nc.dram_tensor("scratch", [H, P * L_TAB], F32, kind="Internal").ap()
    with ExitStack() as ctx:
        square = prog.sb(ctx, "square", [P, CST_W])
        prog.ones = prog.sb(ctx, "ones", [P, P])
        prog.zeros = prog.sb(ctx, "zeros", [P, T])
        prog.eps = prog.sb(ctx, "eps", [P, 1])
        prog.ln_eps = prog.sb(ctx, "ln_eps", [P, 1])
        prog.ident = square[:, IDENT:IDENT + P]
        prog.block_ones = square[:, BLOCK:BLOCK + P]
        prog.window = square[:, WIN:WIN + P]
        prog.causal = square[:, CAUSAL:CAUSAL + T]
        prog.seen = square[:, SEEN:SEEN + 1]
        prog.fox = square[:, FOXSEL:FOXSEL + H]
        xT = prog.sb(ctx, "xT", [P, DK, T])
        with prog.stage("loaded") as (block, s):
            @block.sync
            def _(sp):
                sp.dma_start(square[:, :], dram["cst_square"]).then_inc(s["loaded"], 16)
                sp.wait_ge(s["loaded"], 16)

            @block.gpsimd
            def _(pool):
                pool.memset(prog.ones[:, :], 1.0)
                pool.memset(prog.zeros[:, :], 0.0)
                pool.memset(prog.eps[:, :], RMS_EPS)
                pool.memset(prog.ln_eps[:, :], LN_EPS)
        first_block(prog, xT)
        second_block(prog, xT)
        store(prog, xT, out)
        prog.finish()


INPUTS = ["x", "rel_bias", "norm_mix", "norm_ffn", "w_in", "forget_bias", "qk_gain", "cmp_pos", "cmp_w1", "cmp_w2",
          "sinks", "w_branch", "w_out", "w_gate", "w_up", "conv_w", "conv_b", "w_down", "c_2", "w_ada_2", "b_ada_2",
          "w_in_2", "q_scale_2", "k_scale_2", "sgu_ln_g_2", "sgu_ln_b_2", "w_spatial_2", "b_spatial_2",
          "w_branch_a_2", "w_branch_b_2", "w_out_2", "ln1_g_2", "ln1_b_2", "router_w_2", "router_bias_2", "w_gate_2",
          "w_up_2", "w_down_2", "ws_gate_2", "ws_up_2", "ws_down_2", "ln2_g_2", "ln2_b_2"]


def kernel(**inputs):
    import concourse.bacc as bacc
    from concourse.bass_utils import run_bass_kernel_spmd

    nc = bacc.Bacc("TRN2", target_bir_lowering=False, num_devices=1)
    arrays, dram = {}, {}
    given = {name: np.ascontiguousarray(inputs[name]) for name in INPUTS}
    given.update(shape_constants())
    for name, a in given.items():
        arrays[f"in_{name}_dram"] = a
        dram[name] = nc.dram_tensor(f"in_{name}_dram", a.shape, mybir.dt.from_np(a.dtype), kind="ExternalInput").ap()
    out = nc.dram_tensor("out_0_dram", (1, T, D), F32, kind="ExternalOutput").ap()
    build(nc, dram, out)
    return run_bass_kernel_spmd(nc, [arrays], core_ids=[0]).results[0]["out_0_dram"]
```

```python
from contextlib import ExitStack

import numpy as np

import concourse.bass as bass
from concourse import mybir

F32 = mybir.dt.float32
R32 = mybir.dt.float32r
ACT = mybir.ActivationFunctionType
ALU = mybir.AluOpType
AX = mybir.AxisListType

P = 128
T = 512
TT = T // P
D = 1024
DK = D // P
HD = 64
H = 8
MASKED = -1e30
RMS_EPS = 1e-6
F_HID = 2816
FT = F_HID // P
N_CMP = 31
CMP_HID = 256
L_TAB = 384

C_AQ, C_KC, C_KS, C_VS, C_KW, C_VW, C_GATE = 0, 512, 768, 896, 1024, 1152, 1280
C_BQ, C_BK, C_BV = 1304, 1816, 1944
C_CQ, C_CK, C_CV, C_CF, C_MERGE = 2072, 2584, 3096, 3608, 3616


def shape_constants():
    p = np.arange(P)[:, None]
    c = np.arange(P)[None, :]
    ident = np.eye(P, dtype=np.float32)
    block = ((p // HD) == (c // HD)).astype(np.float32)
    win = np.where(p >= c, np.float32(MASKED), np.float32(0)).astype(np.float32)
    causal = np.zeros((P, T), np.float32)
    causal[:, T - P:] = np.where(c > p, MASKED, 0)
    seen = (p >= 31).astype(np.float32)
    foxsel = np.zeros((P, H), np.float32)
    for quarter in range(4):
        foxsel[32 * quarter + np.arange(H), np.arange(H)] = 1
    square = np.concatenate([ident, block, win, causal, seen, foxsel], axis=1).astype(np.float32)

    y = np.arange(L_TAB)
    dist = 255 - y
    d = np.maximum(dist, 1)
    large = np.minimum(16 + (np.log(d / 16.0) / np.log(8.0) * 16 + 1e-9).astype(np.int64), 31)
    bucket = np.where(dist < 16, np.maximum(dist, 0), large)
    rows = []
    for reach in (512, 128):
        hot = np.zeros((33, L_TAB), np.float32)
        hot[np.where((dist >= 0) & (dist < reach), bucket, 32), y] = 1
        rows.append(hot)

    t = np.arange(T)
    freq = (np.float32(10000.0) ** (-np.arange(HD // 4, dtype=np.float32) / np.float32(HD // 4))).astype(np.float32)
    at_row = (t // 64 - (T // 64) // 2).astype(np.float32)
    at_col = (t % 64 - 32).astype(np.float32)
    angle = np.concatenate([at_row[:, None] * freq, at_col[:, None] * freq], axis=1).astype(np.float32)
    angle = np.repeat(angle, 2, axis=1).T
    angle = np.concatenate([angle, angle], axis=0)
    swap = np.zeros((P, P), np.float32)
    even = np.arange(0, P, 2)
    swap[even + 1, even] = -1
    swap[even, even + 1] = 1
    rope = np.concatenate([np.cos(angle), np.sin(angle), swap], axis=1).astype(np.float32)
    pairs = (np.arange(8)[:, None] == (np.arange(512) // HD)[None, :]).astype(np.float32)
    index = np.arange(P, dtype=np.float32)[:, None]
    before = (np.arange(P)[:, None] < np.arange(P)[None, :]).astype(np.float32)
    count = np.broadcast_to(np.arange((T // P + 1) * P, dtype=np.float32), (P, (T // P + 1) * P))
    token = index + P * np.arange(T // P, dtype=np.float32)[None, :]
    lists = np.concatenate([before, count, index, token], axis=1).astype(np.float32)
    return {"cst_lists": lists, "cst_square": square, "cst_buckets": np.concatenate(rows, axis=1), "cst_rope": rope, "cst_pairs": pairs}


IDENT, BLOCK, WIN, CAUSAL, SEEN, FOXSEL = 0, 128, 256, 384, 896, 897
CST_W = 897 + H


class Chain:

    def __init__(self, sem, eng):
        self.sem, self.n, self.eng = sem, 0, eng

    def __call__(self, ins):
        ins.then_inc(self.sem, 1)
        self.n += 1
        self.eng.wait_ge(self.sem, self.n)


class Program:

    def __init__(self, nc, dram):
        self.nc, self.dram, self.previous, self.stages = nc, dram, None, 0

    def sb(self, ctx, name, shape, dtype=F32):
        return ctx.enter_context(self.nc.sbuf_tensor(f"{name}_{self.stages}", shape, dtype))

    def ps(self, ctx, name, shape):
        return ctx.enter_context(self.nc.psum_tensor(f"{name}_{self.stages}", shape, F32))

    def stage(self, *names, pool_dma=()):
        return Stage(self, names, pool_dma)

    def finish(self):
        with Stage(self, (), ()):
            pass
        self.previous = None


class Stage:

    def __init__(self, prog, names, pool_dma):
        self.prog, self.names, self.pool_dma = prog, names + pool_dma, pool_dma

    def __enter__(self):
        nc = self.prog.nc
        self.holder = ExitStack()
        self.prog.stages += 1
        self.sems = [self.holder.enter_context(nc.semaphore(f"{n}_{self.prog.stages}")) for n in self.names]
        self.block = nc.Block()
        block = self.block.__enter__()
        before = self.prog.previous
        if before is not None and before.sems:
            @block.sync
            def _(sp):
                for name, sem in zip(before.names, before.sems):
                    if name not in before.pool_dma:
                        sp.sem_clear(sem)
        if before is not None and before.pool_dma:
            @block.gpsimd
            def _(pool):
                for name, sem in zip(before.names, before.sems):
                    if name in before.pool_dma:
                        pool.dma_reset(range(sem.num, sem.num + 1))
                        pool.sem_clear(sem)
        return block, dict(zip(self.names, self.sems))

    def __exit__(self, *exc):
        self.block.__exit__(*exc)
        if exc[0] is None:
            if self.prog.previous is not None:
                self.prog.previous.holder.close()
            self.prog.previous = self


class Ring:

    def __init__(self, prog, ctx, chunks, slots, size):
        self.nc, self.chunks, self.slots = prog.nc, chunks, slots
        self.mem = prog.sb(ctx, "weights", [P, slots, size])
        self.loaded = [ctx.enter_context(prog.nc.semaphore(f"weights_loaded_{i}")) for i in range(slots)]
        self.used = ctx.enter_context(prog.nc.semaphore("weights_used"))
        self.plan()

    def plan(self):
        chunks = self.chunks
        self.issued = 0
        total = [0] * self.slots
        self.need = []
        for c, parts in enumerate(chunks):
            total[c % self.slots] += 16 * len(parts)
            self.need.append(total[c % self.slots])

    def slot(self, c, k, n, at=0):
        return self.mem[:, c % self.slots, at:at + k * n].rearrange("p (k n) -> p k n", k=k)

    def run_ahead(self, sp, end):
        for c in range(self.issued, min(end + self.slots, len(self.chunks))):
            if c >= self.slots:
                sp.wait_ge(self.used, c - self.slots + 1)
            for at, k, n, src in self.chunks[c]:
                sp.dma_start(self.slot(c, k, n, at), src).then_inc(self.loaded[c % self.slots], 16)
        self.issued = max(self.issued, min(end + self.slots, len(self.chunks)))

    def wait(self, eng, c):
        eng.wait_ge(self.loaded[c % self.slots], self.need[c])

    def clear(self, sp):
        for sem in self.loaded + [self.used]:
            sp.sem_clear(sem)


class Split:
    SEMS = ("hi_ready", "lo_ready", "piece_used")
    BUFFERS = 3

    def __init__(self, prog, ctx, ring, pieces):
        self.ring, self.pieces = ring, pieces
        self.hi = prog.sb(ctx, "pieces_hi", [P, self.BUFFERS, 4, P], R32)
        self.lo = prog.sb(ctx, "pieces_lo", [P, self.BUFFERS, 4, P], R32)

    def round(self, act, s, i):
        chunk, view, leaves = self.pieces[i]
        self.ring.wait(act, chunk)
        if i >= self.BUFFERS:
            act.wait_ge(s["piece_used"], i - self.BUFFERS + 1)
        act.copy(self.hi[:, i % self.BUFFERS, 0:view.shape[1], 0:view.shape[2]], view).then_inc(s["hi_ready"], 1)

    def rest(self, dve, s, i):
        chunk, view, leaves = self.pieces[i]
        dve.wait_ge(s["hi_ready"], i + 1)
        b, k, n = i % self.BUFFERS, view.shape[1], view.shape[2]
        dve.tensor_tensor(self.lo[:, b, 0:k, 0:n], view, self.hi[:, b, 0:k, 0:n].bitcast(F32),
                          ALU.subtract).then_inc(s["lo_ready"], 1)
        if leaves:
            dve.wait_ge(s["lo_ready"], i + 1)
            dve.sem_inc(self.ring.used, 1)

    def product(self, pe, s, i, bank, x_hi, x_lo, k0, start, stop):
        pe.wait_ge(s["lo_ready"], i + 1)
        n, b = self.pieces[i][1].shape[1], i % self.BUFFERS
        for k in range(n):
            pe.matmul(bank, self.hi[:, b, k, :], x_hi[:, k0 + k, :], start=(start and k == 0), stop=False)
            pe.matmul(bank, self.hi[:, b, k, :], x_lo[:, k0 + k, :], start=False, stop=False)
            last = pe.matmul(bank, self.lo[:, b, k, :], x_hi[:, k0 + k, :], start=False, stop=(stop and k == n - 1))
        last.then_inc(s["piece_used"], 1)


def split_pair(prog, ctx):
    return [prog.sb(ctx, name, [P, DK, T], R32) for name in ("h_hi", "h_lo")]


def split_tiles(prog, src, hi, lo):
    with prog.stage("hi_ready") as (block, s):
        @block.scalar
        def _(act):
            for k in range(src.shape[1]):
                act.copy(hi[:, k, :], src[:, k, :]).then_inc(s["hi_ready"], 1)

        @block.vector
        def _(dve):
            for k in range(src.shape[1]):
                dve.wait_ge(s["hi_ready"], k + 1)
                dve.tensor_tensor(lo[:, k, :], src[:, k, :], hi[:, k, :].bitcast(F32), ALU.subtract)


def rows(w, k=DK):
    return w.rearrange("(k p) n -> p k n", p=P)


def vectors(prog, ring, dst, views):
    nc = prog.nc
    n = dst.shape[-1]
    with ExitStack() as ctx:
        lines = prog.sb(ctx, "lines", [n, P])
        bank = prog.ps(ctx, "lines_turned", [P, P])
        with prog.stage("loaded", "turned") as (block, s):
            @block.sync
            def _(sp):
                for at, count, cols, view in views:
                    sp.dma_start(lines[at:at + count, cols], view).then_inc(s["loaded"], 16)
                if ring:
                    ring.run_ahead(sp, 0)

            @block.tensor
            def _(pe):
                pe.wait_ge(s["loaded"], 16 * len(views))
                pe.transpose(bank[:, 0:n], lines[:, :], prog.ident[0:n, 0:n]).then_inc(s["turned"], 1)

            @block.vector
            def _(dve):
                dve.wait_ge(s["turned"], 1)
                dve.tensor_copy(dst, bank[:, 0:n])


def as_rows(view):
    return view.rearrange("(k p) -> k p", p=P)


ALL, LEFT, RIGHT = slice(0, P), slice(0, HD), slice(HD, P)


def norm_model(prog, src, gain, dst):
    nc = prog.nc
    with ExitStack() as ctx:
        sq = prog.sb(ctx, "squares", [P, 2, T])
        root = prog.sb(ctx, "root", [P, T])
        rstd = prog.sb(ctx, "rstd", [P, T])
        total = prog.ps(ctx, "total", [P, T])
        with prog.stage("squared", "summed", "total_ready", "root_ready", "rstd_ready") as (block, s):
            @block.scalar
            def _(act):
                for k in range(DK):
                    if k >= 2:
                        act.wait_ge(s["summed"], k - 1)
                    act.activation(sq[:, k % 2, :], src[:, k, :], ACT.Square).then_inc(s["squared"], 1)
                act.wait_ge(s["summed"], DK)
                act.activation(root[:, :], total[:, :], ACT.Sqrt, bias=prog.eps[:, 0:1],
                               scale=1.0 / D).then_inc(s["root_ready"], 1)

            @block.tensor
            def _(pe):
                for k in range(DK):
                    pe.wait_ge(s["squared"], k + 1)
                    pe.matmul(total[:, :], prog.ones[:, :], sq[:, k % 2, :], start=(k == 0),
                              stop=(k == DK - 1)).then_inc(s["summed"], 1)

            @block.vector
            def _(dve):
                dve.wait_ge(s["root_ready"], 1)
                dve.reciprocal(rstd[:, :], root[:, :]).then_inc(s["rstd_ready"], 1)
                dve.wait_ge(s["rstd_ready"], 1)
                for k in range(DK):
                    dve.scalar_tensor_tensor(out=dst[:, k, :], in0=src[:, k, :], scalar=gain[:, k:k + 1],
                                             in1=rstd[:, :], op0=ALU.mult, op1=ALU.mult)


def norm_heads(prog, tiles):
    nc = prog.nc
    with ExitStack() as ctx:
        sq = prog.sb(ctx, "squares", [P, 2, T])
        root = prog.sb(ctx, "root", [P, 2, T])
        rstd = prog.sb(ctx, "rstd", [P, 2, T])
        total = prog.ps(ctx, "total", [P, 2, T])
        with prog.stage("squared", "summed", "root_ready", "rstd_ready", "normed") as (block, s):
            @block.scalar
            def _(act):
                def roots(i):
                    n = tiles[i][0].shape[-1]
                    act.wait_ge(s["summed"], i + 1)
                    if i >= 2:
                        act.wait_ge(s["rstd_ready"], i - 1)
                    act.activation(root[:, i % 2, 0:n], total[:, i % 2, 0:n], ACT.Sqrt,
                                   bias=prog.eps[:, 0:1], scale=1.0 / HD).then_inc(s["root_ready"], 1)

                for i, (x, g) in enumerate(tiles):
                    if i >= 2:
                        act.wait_ge(s["summed"], i - 1)
                    act.activation(sq[:, i % 2, 0:x.shape[-1]], x, ACT.Square).then_inc(s["squared"], 1)
                    if i >= 1:
                        roots(i - 1)
                roots(len(tiles) - 1)

            @block.tensor
            def _(pe):
                for i, (x, g) in enumerate(tiles):
                    n = x.shape[-1]
                    pe.wait_ge(s["squared"], i + 1)
                    if i >= 2:
                        pe.wait_ge(s["root_ready"], i - 1)
                    pe.matmul(total[:, i % 2, 0:n], prog.block_ones[:, :], sq[:, i % 2, 0:n], start=True,
                              stop=True).then_inc(s["summed"], 1)

            @block.vector
            def _(dve):
                for i, (x, g) in enumerate(tiles):
                    n = x.shape[-1]
                    dve.wait_ge(s["root_ready"], i + 1)
                    if i >= 2:
                        dve.wait_ge(s["normed"], i - 1)
                    dve.reciprocal(rstd[:, i % 2, 0:n], root[:, i % 2, 0:n]).then_inc(s["rstd_ready"], 1)
                    dve.wait_ge(s["rstd_ready"], i + 1)
                    dve.scalar_tensor_tensor(out=x, in0=x, scalar=g, in1=rstd[:, i % 2, 0:n],
                                             op0=ALU.mult, op1=ALU.mult).then_inc(s["normed"], 1)


def transpose_tiles(prog, jobs, pieces=1):
    nc = prog.nc
    with ExitStack() as ctx:
        banks = prog.ps(ctx, "turned", [P, 4, T])
        with prog.stage("turned", "emptied_dve", "emptied_act") as (block, s):
            @block.tensor
            def _(pe):
                for j, (sources, dst) in enumerate(jobs):
                    if j >= 4:
                        pe.wait_ge(s["emptied_dve"] if j % 2 == 0 else s["emptied_act"], (j - 4) // 2 + 1)
                    for i, src in enumerate(sources):
                        last = pe.transpose(banks[:, j % 4, i * P:(i + 1) * P], src, prog.ident[:, :])
                    last.then_inc(s["turned"], 1)

            @block.vector
            def _(dve):
                for j in range(0, len(jobs), 2):
                    dve.wait_ge(s["turned"], j + 1)
                    dst = jobs[j][1]
                    dve.tensor_copy(dst, banks[:, j % 4, 0:P * len(jobs[j][0])]).then_inc(s["emptied_dve"], 1)

            @block.scalar
            def _(act):
                for j in range(1, len(jobs), 2):
                    act.wait_ge(s["turned"], j + 1)
                    dst = jobs[j][1]
                    act.copy(dst, banks[:, j % 4, 0:P * len(jobs[j][0])]).then_inc(s["emptied_act"], 1)


def project(prog, ring, tiles, h, first, end):
    nc = prog.nc
    h_hi, h_lo = h
    with ExitStack() as ctx:
        banks = prog.ps(ctx, "products", [P, 4, T])
        pieces = []
        for j, (chunk, w, parts) in enumerate(tiles):
            leaves = j + 1 == len(tiles) or tiles[j + 1][0] != chunk
            pieces += [(chunk, w[:, 0:4, :], False), (chunk, w[:, 4:8, :], leaves)]
        split = Split(prog, ctx, ring, pieces)
        with prog.stage(*Split.SEMS, "emptied_dve", "emptied_act") as (block, s):
            @block.sync
            def _(sp):
                ring.run_ahead(sp, end)

            @block.tensor
            def _(pe):
                for j in range(len(tiles)):
                    bank = banks[:, j % 4, :]
                    if j >= 4:
                        pe.wait_ge(s["emptied_dve"] if j % 2 == 0 else s["emptied_act"], (j - 4) // 2 + 1)
                    split.product(pe, s, 2 * j, bank, h_hi, h_lo, 0, True, False)
                    split.product(pe, s, 2 * j + 1, bank, h_hi, h_lo, 4, False, True)

            @block.vector
            def _(dve):
                def empty(j):
                    dve.wait_ge(s["piece_used"], 2 * j + 2)
                    for ps, cols, dst in tiles[j][2]:
                        last = dve.tensor_copy(dst, banks[ps, j % 4, cols])
                    last.then_inc(s["emptied_dve"], 1)

                for j in range(len(tiles)):
                    split.rest(dve, s, 2 * j)
                    if j % 2 == 1:
                        empty(j - 1)
                    split.rest(dve, s, 2 * j + 1)
                if len(tiles) % 2 == 1:
                    empty(len(tiles) - 1)

            @block.scalar
            def _(act):
                def empty(j):
                    act.wait_ge(s["piece_used"], 2 * j + 2)
                    for ps, cols, dst in tiles[j][2]:
                        last = act.copy(dst, banks[ps, j % 4, cols])
                    last.then_inc(s["emptied_act"], 1)

                for j in range(len(tiles)):
                    split.round(act, s, 2 * j)
                    if j >= 2 and j % 2 == 0:
                        empty(j - 1)
                    split.round(act, s, 2 * j + 1)
                if len(tiles) % 2 == 0:
                    empty(len(tiles) - 1)


def attention(prog, units, beside=None):
    nc = prog.nc
    with ExitStack() as ctx:
        scores = prog.ps(ctx, "scores", [P, 3, T])
        turned = prog.ps(ctx, "turned", [P, 2, T])
        summed = prog.ps(ctx, "summed", [P, 2, T])
        prob = prog.sb(ctx, "prob", [P, 4, T])
        probT = prog.sb(ctx, "probT", [P, 2, T])
        low = prog.sb(ctx, "low", [P, 8])
        mass = prog.sb(ctx, "mass", [P, 8])
        sinkm = prog.sb(ctx, "sinkm", [P, 8])
        inv = prog.sb(ctx, "inv", [P, 8, 2])
        with prog.stage("scores_ready", "logits_ready", "probs_ready", "turned_ready", "probsT_ready",
                        "summed_ready", "out_ready", "dve_step", "pool_step", "folded", "ada_step") as (block, s):
            last_unit = len(units) - 1

            if beside:
                ring, c0, cond, acc = beside

                @block.sync
                def _(sp):
                    ring.run_ahead(sp, c0 + ADA - ADA_FIRST)

                @block.gpsimd
                def _(pool):
                    step = Chain(s["pool_step"], pool)
                    for i in range(ADA - ADA_FIRST):
                        fold_rows(pool, ring, c0 + i, cond, acc[:, i, :], step).then_inc(s["folded"], 1)

            @block.tensor
            def _(pe):
                def make_scores(u):
                    x = units[u]
                    if u >= 3:
                        pe.wait_ge(s["logits_ready"], u - 2)
                    reach = x["extra"][1] if x["extra"] else 0
                    if reach:
                        pe.matmul(scores[:, u % 3, 0:reach], x["q"], x["k"][:, 0:reach], start=True, stop=False)
                        last = pe.matmul(scores[:, u % 3, 0:reach], *x["extra"][0], start=False, stop=True)
                    if reach < x["n"]:
                        last = pe.matmul(scores[:, u % 3, reach:x["n"]], x["q"], x["k"][:, reach:x["n"]], start=True,
                                         stop=True)
                    last.then_inc(s["scores_ready"], 1)

                def turn(u):
                    pe.wait_ge(s["probs_ready"], u + 1)
                    if u >= 2:
                        pe.wait_ge(s["probsT_ready"], u - 1)
                    c = 0
                    for i, (r, v) in enumerate(units[u]["v"]):
                        last = pe.transpose(turned[0:r, u % 2, i * P:(i + 1) * P], prob[:, u % 4, c:c + r],
                                            prog.ident[:, :])
                        c += r
                    last.then_inc(s["turned_ready"], 1)

                def weigh(u):
                    pe.wait_ge(s["probsT_ready"], u + 1)
                    if u >= 2:
                        pe.wait_ge(s["out_ready"], u - 1)
                    vs = units[u]["v"]
                    for i, (r, v) in enumerate(vs):
                        last = pe.matmul(summed[:, u % 2, 0:HD], probT[0:r, u % 2, i * P:(i + 1) * P], v,
                                         start=(i == 0), stop=(i == len(vs) - 1))
                    last.then_inc(s["summed_ready"], 1)

                for i in range(len(units) + 3):
                    if i <= last_unit:
                        make_scores(i)
                    if 2 <= i <= last_unit + 2:
                        turn(i - 2)
                    if i >= 3:
                        weigh(i - 3)

            @block.scalar
            def _(act):
                def exponentials(u):
                    x = units[u]
                    act.wait_ge(s["logits_ready"], u + 1)
                    if u >= 8:
                        act.wait_ge(s["out_ready"], u - 7)
                    if x["sink"] is not None:
                        act.activation(sinkm[:, u % 8:u % 8 + 1], x["sink"], ACT.Exp, bias=low[:, u % 8:u % 8 + 1])
                    act.activation(prob[:, u % 4, 0:x["n"]], prob[:, u % 4, 0:x["n"]], ACT.Exp,
                                   bias=low[:, u % 8:u % 8 + 1], scale=-1.0,
                                   accum_out=mass[:, u % 8:u % 8 + 1]).then_inc(s["probs_ready"], 1)

                def copy_turned(u):
                    act.wait_ge(s["turned_ready"], u + 1)
                    if u >= 2:
                        act.wait_ge(s["summed_ready"], u - 1)
                    vs = units[u]["v"]
                    r = vs[0][0]
                    act.copy(probT[0:r, u % 2, 0:P * len(vs)],
                             turned[0:r, u % 2, 0:P * len(vs)]).then_inc(s["probsT_ready"], 1)

                for i in range(len(units) + 2):
                    if i >= 2:
                        copy_turned(i - 2)
                    if i <= last_unit:
                        exponentials(i)

            @block.vector
            def _(dve):
                link = Chain(s["dve_step"], dve)

                def logits(u):
                    x = units[u]
                    dve.wait_ge(s["scores_ready"], u + 1)
                    if u >= 4:
                        dve.wait_ge(s["turned_ready"], u - 3)
                    sc = scores[:, u % 3, 0:x["n"]]
                    bias = prog.zeros[:, 0:x["n"]] if x["bias"] is None else x["bias"]
                    start = 3e38 if x["sink"] is None else x["minus_sink"]
                    dve.tensor_tensor_reduce(prob[:, u % 4, 0:x["n"]], sc, bias, -1.0, start, ALU.add, ALU.min,
                                             low[:, u % 8:u % 8 + 1]).then_inc(s["logits_ready"], 1)

                def finish(u):
                    x = units[u]
                    a, b = inv[:, u % 8, 0:1], inv[:, u % 8, 1:2]
                    m = mass[:, u % 8:u % 8 + 1]
                    dve.wait_ge(s["summed_ready"], u + 1)
                    if x["sink"] is not None:
                        link(dve.tensor_tensor(b, m, sinkm[:, u % 8:u % 8 + 1], ALU.add))
                        m = b
                    link(dve.reciprocal(a, m))
                    if x["factor"] is not None:
                        link(dve.tensor_tensor(b, a, x["factor"], ALU.mult))
                        a = b
                    if x["adds"]:
                        dve.scalar_tensor_tensor(out=x["out"], in0=summed[:, u % 2, 0:HD], scalar=a, in1=x["out"],
                                                 op0=ALU.mult, op1=ALU.add).then_inc(s["out_ready"], 1)
                    else:
                        dve.tensor_scalar(x["out"], summed[:, u % 2, 0:HD], a, None,
                                          ALU.mult).then_inc(s["out_ready"], 1)

                def add_row(n):
                    i, k = n // 4, 4 + n % 4
                    if n >= 1:
                        dve.wait_ge(s["ada_step"], n)
                    if k == 4:
                        dve.wait_ge(s["folded"], i + 1)
                    dve.scalar_tensor_tensor(out=acc[:, i, :], in0=ring.slot(c0 + i, DK, 512)[:, k, :],
                                             scalar=cond[:, k:k + 1], in1=acc[:, i, :], op0=ALU.mult,
                                             op1=ALU.add).then_inc(s["ada_step"], 1)
                    if k == 7:
                        dve.wait_ge(s["ada_step"], n + 1)
                        dve.sem_inc(ring.used, 1)

                rows_left = 4 * (ADA - ADA_FIRST) if beside else 0
                for i in range(len(units) + 3):
                    if i <= last_unit:
                        logits(i)
                    if i >= 3:
                        finish(i - 3)
                    if 3 <= i < 3 + rows_left:
                        add_row(i - 3)


def unit(q, k, n, v, out, bias=None, extra=None, sink=None, minus_sink=None, factor=None, adds=False):
    return dict(q=q, k=k, n=n, v=v, out=out, bias=bias, extra=extra, sink=sink, minus_sink=minus_sink,
                factor=factor, adds=adds)


def half(h):
    return slice(HD * (h % 2), HD * (h % 2) + HD)


def pad_heads(prog, qT, padded, side_of):
    with prog.stage("none") as (block, s):
        @block.gpsimd
        def _(pool):
            for h in range(H):
                pool.memset(padded[half(1 - side_of(h)), h, :], 0.0)

        @block.vector
        def _(dve):
            for h in range(0, H, 2):
                dve.tensor_copy(padded[half(side_of(h)), h, :], qT[half(h), h // 2, :])

        @block.scalar
        def _(act):
            for h in range(1, H, 2):
                act.copy(padded[half(side_of(h)), h, :], qT[half(h), h // 2, :])


def first_chunks(d):
    w = rows(d["w_in"][0])
    w1 = d["cmp_w1"][0]
    wb, wg, wu, wd = d["w_branch"][0], rows(d["w_gate"][0]), rows(d["w_up"][0]), rows(d["w_down"][0], FT)
    wo = rows(d["w_out"][0])
    out = {}
    chunks = []

    def add(name, *parts):
        out.setdefault(name, len(chunks))
        at, listed = 0, []
        for view in parts:
            k, n = view.shape[1], view.shape[2]
            listed.append((at, k, n, view))
            at += k * n
        chunks.append(listed)

    add("a_q", w[:, :, C_AQ:C_AQ + 512])
    add("a_kv", w[:, :, C_KC:C_KC + 512])
    add("a_w", w[:, :, C_KW:C_KW + 3 * P])
    for which in range(2):
        add("cmp_w1", rows(w1[which], 16))
    add("b_q", w[:, :, C_BQ:C_BQ + 512])
    add("b_kv", w[:, :, C_BK:C_BK + 256])
    add("c_q", w[:, :, C_CQ:C_CQ + 512])
    add("c_k", w[:, :, C_CK:C_CK + 512])
    add("c_v", w[:, :, C_CV:C_CV + 512])
    add("c_f", w[:, :, C_CF:C_CF + P])
    for m in range(DK):
        add("merge", *[w[:, :, C_MERGE + b * D + m * P:C_MERGE + b * D + (m + 1) * P] for b in range(3)],
            *[rows(wb[b], 4)[:, :, m * P:(m + 1) * P] for b in range(3)])
    for m in range(2):
        add("w_out", wo[:, :, m * 512:(m + 1) * 512])
    for m in range(FT // 2):
        add("ffn", wg[:, :, m * 256:(m + 1) * 256], wu[:, :, m * 256:(m + 1) * 256])
    for m in range(DK):
        add("w_down", wd[:, :, m * P:(m + 1) * P])
    return chunks, out


def first_block(prog, xT):
    nc, d = prog.nc, prog.dram
    chunks, at = first_chunks(d)
    with ExitStack() as ctx:
        ring = Ring(prog, ctx, chunks, 3, 36 * P)
        small = prog.sb(ctx, "small", [P, 6 + 2 * DK + 4 * FT])
        at_norm, at_taps = 6, 6 + 2 * DK
        gains = small[:, 0:6]
        norm_mix, norm_ffn = small[:, at_norm:at_norm + DK], small[:, at_norm + DK:at_taps]
        conv_w = small[:, at_taps:at_taps + 3 * FT].rearrange("p (i f) -> p i f", i=3)
        conv_b = small[:, at_taps + 3 * FT:at_taps + 4 * FT]
        with ExitStack() as mixers:
            oT = prog.sb(mixers, "oT", [P, 3, 4, T])
            h = split_pair(prog, mixers)
            x_tok = oT[:, 0:2, :, :].rearrange("p a b n -> p (a b n)").rearrange("p (t n) -> p t n", t=TT)
            with prog.stage("loaded") as (block, s):
                @block.sync
                def _(sp):
                    for t in range(TT):
                        sp.dma_start(x_tok[:, t, :], d["x"][0, t * P:(t + 1) * P, :]).then_inc(s["loaded"], 16)
                    sp.wait_ge(s["loaded"], 16 * TT)

            vectors(prog, ring, small[:, 0:at_taps + 4 * FT],
                    [(0, 6, LEFT, d["qk_gain"][0]), (0, 6, RIGHT, d["qk_gain"][0]),
                     (at_norm, DK, ALL, as_rows(d["norm_mix"][0])), (at_norm + DK, DK, ALL, as_rows(d["norm_ffn"][0])),
                     (at_taps + 3 * FT, FT, ALL, as_rows(d["conv_b"][0]))]
                    + [(at_taps + i * FT, FT, ALL, as_rows(d["conv_w"][0, i])) for i in range(3)])
            with prog.stage("none") as (block, s):
                @block.vector
                def _(dve):
                    for g in (0, 2, 4):
                        dve.tensor_scalar(gains[:, g:g + 1], gains[:, g:g + 1], HD ** -0.5, None, ALU.mult)
            transpose_tiles(prog, [([x_tok[:, t, m * P:(m + 1) * P] for t in range(TT)], xT[:, m, :])
                                   for m in range(DK)])
            with ExitStack() as whole:
                hT = prog.sb(whole, "hT", [P, DK, T])
                norm_model(prog, xT, norm_mix, hT)
                split_tiles(prog, hT, *h)
            mixer_a(prog, ring, at, h, oT, gains)
            mixer_b(prog, ring, at, h, oT, gains)
            mixer_c(prog, ring, at, h, oT, gains)
            with ExitStack() as merged:
                y = [prog.sb(merged, name, [P, DK, T], R32) for name in ("y_hi", "y_lo")]
                merge_branches(prog, ring, at["merge"], h, oT, y, 3)
                residual_product(prog, ring, at["w_out"], y, xT)
        with ExitStack() as ffn:
            hT = prog.sb(ffn, "hT_ffn", [P, DK, T])
            norm_model(prog, xT, norm_ffn, hT)
            conv_ffn(prog, ring, at, hT, xT, conv_w, conv_b)
        with prog.stage("none") as (block, s):
            @block.sync
            def _(sp):
                ring.clear(sp)


def bias_tables(prog, tables, group, reach):
    nc, d = prog.nc, prog.dram
    with ExitStack() as ctx:
        tab = prog.sb(ctx, "tab", [33, H])
        tab_wide = prog.sb(ctx, "tab_wide", [33, H, P])
        hot = prog.sb(ctx, "hot", [33, L_TAB])
        line = prog.sb(ctx, "line", [P, H, L_TAB])
        spread = prog.ps(ctx, "spread", [P, 2, T])
        width = tables.shape[2]
        scratch = d["scratch"]
        with prog.stage("loaded", "filled", "wide", "spread_ready", "line_ready", "written", "read") as (block, s):
            @block.sync
            def _(sp):
                sp.dma_start(tab[0:32, :], d["rel_bias"][:, group * H:(group + 1) * H]).then_inc(s["loaded"], 16)
                sp.dma_start(hot[:, :], d["cst_buckets"][:, group * L_TAB:(group + 1) * L_TAB]).then_inc(s["loaded"], 16)
                sp.wait_ge(s["line_ready"], H)
                sp.dma_start(scratch[:, :].rearrange("h (p c) -> p h c", p=P), line[:, :, :]).then_inc(s["written"], 16)
                sp.wait_ge(s["written"], 16)
                view = scratch[:, P - 1:P - 1 + P * (L_TAB - 1)].rearrange("h (p c) -> p h c", c=L_TAB - 1)
                sp.dma_start(tables[:, :, width - 256:width], view[:, :, 0:256]).then_inc(s["read"], 16)
                sp.wait_ge(s["read"], 16)

            @block.vector
            def _(dve):
                dve.memset(tab[32:33, :], MASKED).then_inc(s["filled"], 1)
                dve.wait_ge(s["filled"], 1)
                dve.wait_ge(s["loaded"], 32)
                for h in range(H):
                    last = dve.tensor_copy(tab_wide[:, h, :], tab[:, h:h + 1].to_broadcast([33, P]))
                last.then_inc(s["wide"], 1)

            @block.tensor
            def _(pe):
                pe.wait_ge(s["wide"], 1)
                for h in range(H):
                    if h >= 2:
                        pe.wait_ge(s["line_ready"], h - 1)
                    pe.matmul(spread[:, h % 2, 0:L_TAB], tab_wide[:, h, :], hot[:, :], start=True,
                              stop=True).then_inc(s["spread_ready"], 1)

            @block.scalar
            def _(act):
                for h in range(H):
                    act.wait_ge(s["spread_ready"], h + 1)
                    act.copy(line[:, h, :], spread[:, h % 2, 0:L_TAB]).then_inc(s["line_ready"], 1)
                if width > 256:
                    for h in range(H):
                        act.wait_ge(s["line_ready"], h + 1)
                        act.activation(tables[:, h, 0:width - 256], prog.zeros[:, 0:width - 256], ACT.Identity,
                                       bias=line[:, h, 0:1])


WHOLE = slice(0, T)


def feature_tiles(ring, chunk, stride, start, dst):
    w = ring.slot(chunk, DK, stride)
    return [(chunk, w[:, :, start + i * P:start + (i + 1) * P], [(ALL, WHOLE, dst[:, i, :])])
            for i in range(dst.shape[1])]


def twin_tiles(ring, chunk, stride, start, dst, shifted=False):
    w = ring.slot(chunk, DK, stride)
    parts = []
    for g in range(2):
        parts.append((half(g), WHOLE, dst[LEFT, g, :]))
        if shifted:
            parts.append((half(g), slice(1, T), dst[RIGHT, g, 0:T - 1]))
        else:
            parts.append((half(g), WHOLE, dst[RIGHT, g, :]))
    return [(chunk, w[:, :, start:start + P], parts)]


def to_tokens(prog, srcT, dst):
    n = srcT.shape[1]
    transpose_tiles(prog, [([srcT[:, i, t * P:(t + 1) * P] for i in range(n)], dst[:, t, :]) for t in range(TT)])


def mixer_a(prog, ring, at, h, oT, gains):
    nc, d = prog.nc, prog.dram
    with ExitStack() as ctx:
        tables = oT[:, 1:3, :, :].rearrange("p a b n -> p (a b) n")
        qT = prog.sb(ctx, "qT", [P, 4, T])
        cT = prog.sb(ctx, "cT", [P, 2, 2, T])
        kT = prog.sb(ctx, "kT", [P, 2, 2, T])
        v_tok = prog.sb(ctx, "v_tok", [P, TT, P])
        w_tok = prog.sb(ctx, "w_tok", [P, TT, 2 * P])
        kcT = prog.sb(ctx, "kcT", [P, 2, N_CMP])
        vc = prog.sb(ctx, "vc", [N_CMP, 2, HD])
        o_tok = prog.sb(ctx, "o_tok", [P, TT, 512])

        bias_tables(prog, tables, 0, T)
        q, kv, w = at["a_q"], at["a_kv"], at["a_w"]
        tiles = feature_tiles(ring, q, 512, 0, qT)
        tiles += twin_tiles(ring, kv, 512, 0, cT[:, 0, :, :], shifted=True)
        tiles += twin_tiles(ring, kv, 512, 128, cT[:, 1, :, :], shifted=True)
        tiles += twin_tiles(ring, kv, 512, 256, kT[:, 0, :, :])
        tiles += feature_tiles(ring, kv, 512, 384, o_tok[:, 0:1, :])
        tiles += twin_tiles(ring, w, 3 * P, 0, kT[:, 1, :, :])
        tiles += feature_tiles(ring, w, 3 * P, 128, o_tok[:, 1:3, :])
        project(prog, ring, tiles, h, q, w + 1)
        to_tokens(prog, o_tok[:, 0:1, :], v_tok)
        to_tokens(prog, o_tok[:, 1:3, :], w_tok)
        compress(prog, ring, at, cT, kcT, vc)
        norm_heads(prog, [(qT[:, i, :], gains[:, 0:1]) for i in range(4)]
                   + [(kT[:, i, g, :], gains[:, 1:2]) for i in range(2) for g in range(2)]
                   + [(kcT[:, g, :], gains[:, 1:2]) for g in range(2)])
        with prog.stage("gated") as (block, s):
            @block.scalar
            def _(act):
                act.activation(w_tok[:, :, P:P + 3 * H], w_tok[:, :, P:P + 3 * H], ACT.Sigmoid)

        factors = prog.sb(ctx, "factors", [P, H])
        with prog.stage("none") as (block, s):
            @block.vector
            def _(dve):
                for h in range(H):
                    g = w_tok[:, 0, P + 3 * h:P + 3 * h + 1]
                    dve.tensor_scalar(factors[:, h:h + 1], g, prog.seen, None, ALU.mult)
        padded = prog.sb(ctx, "padded", [P, H, T])
        pad_heads(prog, qT, padded, lambda h: h % 2)
        units = []
        for h in range(H):
            g = h // 4
            for t in range(TT):
                query = padded[:, h, t * P:(t + 1) * P]
                out = o_tok[:, t, h * HD:(h + 1) * HD]
                gate = [w_tok[:, t, P + 3 * h + i:P + 3 * h + i + 1] for i in range(3)]
                n = (t + 1) * P
                units.append(unit(query, kT[:, 0, g, 0:n], n,
                                  [(P, v_tok[:, j, g * HD:(g + 1) * HD]) for j in range(t + 1)], out,
                                  bias=tables[:, h, T - n:T], factor=gate[1]))
        for h in range(H):
            g = h // 4
            for t in range(TT):
                query = padded[:, h, t * P:(t + 1) * P]
                out = o_tok[:, t, h * HD:(h + 1) * HD]
                gate = [w_tok[:, t, P + 3 * h + i:P + 3 * h + i + 1] for i in range(3)]
                j0 = max(0, t - 2)
                n = (t + 1 - j0) * P
                far = ((prog.ident[:, :], prog.window[:, :]), P) if t >= 2 else None
                units.append(unit(query, kT[:, 1, g, j0 * P:j0 * P + n], n,
                                  [(P, w_tok[:, j, g * HD:(g + 1) * HD]) for j in range(j0, t + 1)], out,
                                  bias=tables[:, h, T - n:T], extra=far, factor=gate[2], adds=True))
        for h in range(H):
            g = h // 4
            for t in range(TT):
                query = padded[:, h, t * P:(t + 1) * P]
                out = o_tok[:, t, h * HD:(h + 1) * HD]
                n = 7 + 8 * t
                first = 415 - P * t
                factor = factors[:, h:h + 1] if t == 0 else w_tok[:, t, P + 3 * h:P + 3 * h + 1]
                units.append(unit(query, kcT[:, g, 0:n], n, [(n, vc[0:n, g, :])], out,
                                  bias=tables[:, h, first:first + 16 * (n - 1) + 1:16], factor=factor, adds=True))
        attention(prog, units)
        to_features(prog, o_tok, oT[:, 0, :, :])


def to_features(prog, o_tok, oT):
    transpose_tiles(prog, [([o_tok[:, t, m * P:(m + 1) * P] for t in range(TT)], oT[:, m, :]) for m in range(4)])


def compress(prog, ring, at, cT, kcT, vc):
    nc, d = prog.nc, prog.dram
    with ExitStack() as ctx:
        pos = prog.sb(ctx, "pos", [P, 2, 16])
        w2 = prog.sb(ctx, "w2", [P, 2, 2, HD])
        window = prog.sb(ctx, "window", [P, 2, 16, 2 * N_CMP])
        hid = prog.sb(ctx, "hid", [P, 2, 2, 2 * N_CMP])
        banks = prog.ps(ctx, "hidden", [P, 4, T])
        banks2 = prog.ps(ctx, "compressed", [P, 3, T])
        vectors(prog, None, pos[:, :, :].rearrange("p w l -> p (w l)"),
                [(16 * which, 16, ALL, d["cmp_pos"][0, which].rearrange("(l two) d -> l (two d)", two=2))
                 for which in range(2)])
        with prog.stage("loaded", "window_ready", "hidden_ready", "gelu_ready", "out_ready") as (block, s):
            @block.sync
            def _(sp):
                for which in range(2):
                    sp.dma_start(w2[:, which, :, :], rows(d["cmp_w2"][0, which], 2)).then_inc(s["loaded"], 16)
                ring.run_ahead(sp, at["cmp_w1"] + 2)

            @block.tensor
            def _(pe):
                pe.wait_ge(s["loaded"], 32)
                for which in range(2):
                    c = at["cmp_w1"] + which
                    ring.wait(pe, c)
                    w = ring.slot(c, 16, CMP_HID)
                    for m in range(2):
                        j = 2 * which + m
                        for l in range(16):
                            if m == 0:
                                pe.wait_ge(s["window_ready"], 16 * which + l + 1)
                            last = pe.matmul(banks[:, j, 0:2 * N_CMP], w[:, l, m * P:(m + 1) * P],
                                             window[:, which, l, :], start=(l == 0), stop=(l == 15))
                        last.then_inc(s["hidden_ready"], 1)
                    pe.wait_ge(s["hidden_ready"], 2 * which + 2)
                    pe.sem_inc(ring.used, 1)
                pe.wait_ge(s["gelu_ready"], 2)
                for side in range(2):
                    for m in range(2):
                        last = pe.matmul(banks2[side * HD:(side + 1) * HD, side, 0:2 * N_CMP], w2[:, 0, m, :], hid[:, 0, m, :],
                                         start=(m == 0), stop=(m == 1))
                pe.wait_ge(s["gelu_ready"], 4)
                for g in range(2):
                    for m in range(2):
                        last = pe.matmul(banks2[0:N_CMP, 2, g * HD:(g + 1) * HD],
                                         hid[:, 1, m, g * N_CMP:(g + 1) * N_CMP], w2[:, 1, m, :],
                                         start=(m == 0), stop=(m == 1))
                last.then_inc(s["out_ready"], 1)

            @block.vector
            def _(dve):
                for which in range(2):
                    for l in range(16):
                        dve.tensor_scalar(window[:, which, l, :].rearrange("p (g n) -> p g n", g=2),
                                          cT[:, which, :, 2 * l:2 * l + 16 * (N_CMP - 1) + 1:16],
                                          pos[:, which, l:l + 1], None, ALU.add).then_inc(s["window_ready"], 1)
                dve.wait_ge(s["out_ready"], 1)
                for side in range(2):
                    ps = slice(side * HD, side * HD + HD)
                    dve.tensor_copy(kcT[ps, :, :], banks2[ps, side, 0:2 * N_CMP].rearrange("p (g n) -> p g n", g=2))
                dve.tensor_copy(vc[:, :, :], banks2[0:N_CMP, 2, 0:2 * HD].rearrange("p (g n) -> p g n", g=2))

            @block.scalar
            def _(act):
                for j in range(4):
                    act.wait_ge(s["hidden_ready"], j + 1)
                    act.activation(hid[:, j // 2, j % 2, :], banks[:, j, 0:2 * N_CMP],
                                   ACT.Gelu_apprx_tanh).then_inc(s["gelu_ready"], 1)


def mixer_b(prog, ring, at, h, oT, gains):
    nc, d = prog.nc, prog.dram
    with ExitStack() as ctx:
        tables = prog.sb(ctx, "tables_b", [P, H, 256])
        qT = prog.sb(ctx, "qT_b", [P, 4, T])
        kT = prog.sb(ctx, "kT_b", [P, 2, T])
        v_tok = prog.sb(ctx, "v_tok_b", [P, TT, P])
        sinks = prog.sb(ctx, "sinks", [P, 2, H])
        o_tok = prog.sb(ctx, "o_tok_b", [P, TT, 512])
        bias_tables(prog, tables, 1, 128)
        with prog.stage("loaded") as (block, s):
            @block.sync
            def _(sp):
                sp.dma_start(sinks[:, 0, :], d["sinks"].to_broadcast([P, H])).then_inc(s["loaded"], 16)

            @block.vector
            def _(dve):
                dve.wait_ge(s["loaded"], 16)
                dve.tensor_scalar(sinks[:, 1, :], sinks[:, 0, :], -1.0, None, ALU.mult)
        q, kv = at["b_q"], at["b_kv"]
        tiles = feature_tiles(ring, q, 512, 0, qT)
        tiles += twin_tiles(ring, kv, 256, 0, kT)
        tiles += feature_tiles(ring, kv, 256, 128, o_tok[:, 0:1, :])
        project(prog, ring, tiles, h, q, kv + 1)
        to_tokens(prog, o_tok[:, 0:1, :], v_tok)
        norm_heads(prog, [(qT[:, i, :], gains[:, 2:3]) for i in range(4)]
                   + [(kT[:, g, :], gains[:, 3:4]) for g in range(2)])
        padded = prog.sb(ctx, "padded", [P, H, T])
        pad_heads(prog, qT, padded, lambda h: h % 2)
        units = []
        for h in range(H):
            g = h // 4
            for t in range(TT):
                j0 = max(0, t - 1)
                n = (t + 1 - j0) * P
                units.append(unit(padded[:, h, t * P:(t + 1) * P], kT[:, g, j0 * P:j0 * P + n], n,
                                  [(P, v_tok[:, j, g * HD:(g + 1) * HD]) for j in range(j0, t + 1)],
                                  o_tok[:, t, h * HD:(h + 1) * HD], bias=tables[:, h, 256 - n:256],
                                  sink=sinks[:, 0, h:h + 1], minus_sink=sinks[:, 1, h:h + 1]))
        attention(prog, units)
        to_features(prog, o_tok, oT[:, 1, :, :])


def mixer_c(prog, ring, at, h, oT, gains):
    nc, d = prog.nc, prog.dram
    with ExitStack() as ctx:
        qT = oT[:, 2, :, :]
        kT = prog.sb(ctx, "kT_c", [P, 4, T])
        v_tok = prog.sb(ctx, "v_tok_c", [P, TT, 512])
        f = prog.sb(ctx, "f", [H, T])
        o_tok = prog.sb(ctx, "o_tok_c", [P, TT, 512])
        left = prog.sb(ctx, "left", [P, T])
        right = prog.sb(ctx, "right", [P, H, T])
        c = at["c_v"]
        tiles = feature_tiles(ring, at["c_q"], 512, 0, qT)
        tiles += feature_tiles(ring, at["c_k"], 512, 0, kT)
        tiles += feature_tiles(ring, c, 512, 0, o_tok)
        tiles.append((at["c_f"], ring.slot(at["c_f"], DK, P), [(slice(0, H), WHOLE, f[:, :])]))
        project(prog, ring, tiles, h, at["c_q"], at["c_f"] + 1)
        to_tokens(prog, o_tok, v_tok)
        norm_heads(prog, [(qT[:, i, :], gains[:, 4:5]) for i in range(4)]
                   + [(kT[:, i, :], gains[:, 5:6]) for i in range(4)])
        with ExitStack() as inner:
            fb = prog.sb(inner, "fb", [H, 1])
            work = prog.sb(inner, "work", [H, 3, T])
            minus = prog.sb(inner, "minus", [P, T])
            with prog.stage("loaded", "step", "logs_ready", "minus_ready", "ones_ready") as (block, s):
                @block.sync
                def _(sp):
                    sp.dma_start(fb[:, :], d["forget_bias"].rearrange("a h -> h a")).then_inc(s["loaded"], 16)

                @block.scalar
                def _(act):
                    link = Chain(s["step"], act)
                    act.wait_ge(s["loaded"], 16)
                    link(act.activation(work[:, 0, :], f[:, :], ACT.Identity, bias=fb[:, 0:1]))
                    link(act.activation(work[:, 1, :], work[:, 0, :], ACT.Abs))
                    link(act.activation(work[:, 1, :], work[:, 1, :], ACT.Exp, scale=-1.0))
                    act.activation(work[:, 1, :], work[:, 1, :], ACT.Ln, bias=1.0).then_inc(s["logs_ready"], 1)

                @block.gpsimd
                def _(pool):
                    pool.memset(right[:, :, :], 0.0).then_inc(s["ones_ready"], 1)
                    pool.memset(left[:, :], 0.0).then_inc(s["ones_ready"], 1)

                @block.vector
                def _(dve):
                    dve.wait_ge(s["logs_ready"], 1)
                    dve.wait_ge(s["ones_ready"], 2)

                    def link(ins, n):
                        ins.then_inc(s["minus_ready"], 1)
                        dve.wait_ge(s["minus_ready"], n)

                    link(dve.scalar_tensor_tensor(out=work[:, 2, :], in0=work[:, 0, :], scalar=0.0,
                                                  in1=work[:, 1, :], op0=ALU.min, op1=ALU.subtract), 1)
                    link(dve.tensor_tensor_scan(left[0:H, :], prog.ones[0:H, 0:1].to_broadcast([H, T]),
                                                work[:, 2, :], 0.0, ALU.mult, ALU.add), 2)
                    link(dve.tensor_copy(left[HD:HD + H, :], left[0:H, :]), 3)
                    for base in (0, HD):
                        lo, hi = slice(base, base + H), slice(base + 32, base + 32 + H)
                        link(dve.tensor_scalar(minus[hi, :], left[lo, :], -1.0, None, ALU.mult), 4 + base // HD)
                        dve.memset(left[hi, :], 1.0)
                        for h in range(base // HD, H, 2):
                            dve.tensor_scalar(right[lo, h, :], prog.zeros[lo, :], prog.fox[lo, h:h + 1], None, ALU.add)
                            dve.tensor_scalar(right[hi, h, :], minus[hi, :], prog.fox[hi, h:h + 1], None, ALU.mult)
        padded = prog.sb(ctx, "padded", [P, H, T])
        pad_heads(prog, qT, padded, lambda h: h % 2)
        units = []
        for h in range(H):
            for t in range(TT):
                n = (t + 1) * P
                units.append(unit(padded[:, h, t * P:(t + 1) * P], kT[:, h // 2, 0:n], n,
                                  [(P, v_tok[:, j, h * HD:(h + 1) * HD]) for j in range(t + 1)],
                                  o_tok[:, t, h * HD:(h + 1) * HD], bias=prog.causal[:, T - n:T],
                                  extra=((left[:, t * P:(t + 1) * P], right[:, h, 0:n]), n)))
        attention(prog, units)
        to_features(prog, o_tok, oT[:, 2, :, :])


def merge_branches(prog, ring, c0, h, oT, y, n_branch):
    nc = prog.nc
    n = n_branch * DK
    h_hi, h_lo = h
    y_hi, y_lo = y
    with ExitStack() as ctx:
        whole = prog.sb(ctx, "y_whole", [P, 2, T])
        gate = prog.sb(ctx, "gate", [P, 2, T])
        gate_ps = prog.ps(ctx, "gate_ps", [P, 2, T])
        branch_ps = prog.ps(ctx, "branch_ps", [P, 2, T])
        pieces = []
        for i in range(n):
            c = c0 + i // n_branch
            wm = ring.slot(c, DK, P, i % n_branch * DK * P)
            pieces += [(c, wm[:, 0:4, :], False), (c, wm[:, 4:8, :], False)]
        split = Split(prog, ctx, ring, pieces)
        with prog.stage(*Split.SEMS, "branch_made", "gate_ready", "part_ready", "added", "y_rounded") as (block, s):
            @block.sync
            def _(sp):
                ring.run_ahead(sp, c0 + DK)

            @block.tensor
            def _(pe):
                for i in range(n):
                    m, b = i // n_branch, i % n_branch
                    wb = ring.slot(c0 + m, 4, P, n_branch * DK * P + b * 4 * P)
                    if i >= 2:
                        pe.wait_ge(s["gate_ready"], i - 1)
                    split.product(pe, s, 2 * i, gate_ps[:, i % 2, :], h_hi, h_lo, 0, True, False)
                    split.product(pe, s, 2 * i + 1, gate_ps[:, i % 2, :], h_hi, h_lo, 4, False, True)
                    if b == 0:
                        ring.wait(pe, c0 + m)
                    if i >= 2:
                        pe.wait_ge(s["part_ready"], i - 1)
                    for k in range(4):
                        last = pe.matmul(branch_ps[:, i % 2, :], wb[:, k, :], oT[:, b, k, :], start=(k == 0),
                                         stop=(k == 3))
                    last.then_inc(s["branch_made"], 1)
                    if b == n_branch - 1:
                        pe.wait_ge(s["branch_made"], i + 1)
                        pe.sem_inc(ring.used, 1)

            @block.scalar
            def _(act):
                def sigmoid(i):
                    act.wait_ge(s["piece_used"], 2 * i + 2)
                    if i >= 2:
                        act.wait_ge(s["part_ready"], i - 1)
                    act.activation(gate[:, i % 2, :], gate_ps[:, i % 2, :], ACT.Sigmoid).then_inc(s["gate_ready"], 1)

                def round_y(m):
                    act.wait_ge(s["part_ready"], n_branch * (m + 1))
                    act.copy(y_hi[:, m, :], whole[:, m % 2, :]).then_inc(s["y_rounded"], 1)

                for i in range(n):
                    split.round(act, s, 2 * i)
                    if i >= 1:
                        sigmoid(i - 1)
                    split.round(act, s, 2 * i + 1)
                    if i >= 2 and (i - 1) % n_branch == 0:
                        round_y((i - 1) // n_branch - 1)
                sigmoid(n - 1)
                round_y(DK - 1)

            @block.vector
            def _(dve):
                def weigh(i):
                    m, b = i // n_branch, i % n_branch
                    total = whole[:, m % 2, :]
                    dst = gate[:, i % 2, :] if b else total
                    dve.wait_ge(s["gate_ready"], i + 1)
                    dve.wait_ge(s["branch_made"], i + 1)
                    if b == 0:
                        dve.tensor_tensor(dst, branch_ps[:, i % 2, :], gate[:, i % 2, :], ALU.mult).then_inc(s["part_ready"], 1)
                        return
                    dve.tensor_tensor(dst, branch_ps[:, i % 2, :], gate[:, i % 2, :], ALU.mult).then_inc(s["added"], 1)
                    dve.wait_ge(s["added"], i - m)
                    if b >= 1:
                        dve.wait_ge(s["part_ready"], i)
                    dve.tensor_tensor(total, total, dst, ALU.add).then_inc(s["part_ready"], 1)

                def rest_of_y(m):
                    dve.wait_ge(s["y_rounded"], m + 1)
                    dve.tensor_tensor(y_lo[:, m, :], whole[:, m % 2, :], y_hi[:, m, :].bitcast(F32), ALU.subtract)

                for i in range(n):
                    split.rest(dve, s, 2 * i)
                    if i >= 1:
                        weigh(i - 1)
                    split.rest(dve, s, 2 * i + 1)
                    if i >= 2 and (i - 1) % n_branch == 0:
                        rest_of_y((i - 1) // n_branch - 1)
                weigh(n - 1)
                rest_of_y(DK - 1)


def residual_product(prog, ring, c0, y, xT, factor=None):
    nc = prog.nc
    with ExitStack() as ctx:
        banks = prog.ps(ctx, "banks", [P, 4, T])
        pieces = []
        for m in range(DK):
            w = ring.slot(c0 + m // 4, DK, 512)[:, :, (m % 4) * P:(m % 4 + 1) * P]
            pieces += [(c0 + m // 4, w[:, 0:4, :], False), (c0 + m // 4, w[:, 4:8, :], m % 4 == 3)]
        split = Split(prog, ctx, ring, pieces)
        with prog.stage(*Split.SEMS, "added") as (block, s):
            @block.sync
            def _(sp):
                ring.run_ahead(sp, c0 + 2)

            @block.tensor
            def _(pe):
                for m in range(DK):
                    if m >= 4:
                        pe.wait_ge(s["added"], m - 3)
                    for half in range(2):
                        split.product(pe, s, 2 * m + half, banks[:, m % 4, :], *y, 4 * half, half == 0, half == 1)

            @block.scalar
            def _(act):
                for i in range(2 * DK):
                    split.round(act, s, i)

            @block.vector
            def _(dve):
                def add(m):
                    dve.wait_ge(s["piece_used"], 2 * m + 2)
                    scale = 1.0 if factor is None else factor[:, m:m + 1]
                    dve.scalar_tensor_tensor(out=xT[:, m, :], in0=banks[:, m % 4, :], scalar=scale, in1=xT[:, m, :],
                                             op0=ALU.mult, op1=ALU.add).then_inc(s["added"], 1)

                for m in range(DK):
                    split.rest(dve, s, 2 * m)
                    split.rest(dve, s, 2 * m + 1)
                    if m >= 1:
                        add(m - 1)
                add(DK - 1)


def conv_ffn(prog, ring, at, hT, xT, conv_w, conv_b):
    nc = prog.nc
    with ExitStack() as ctx:
        hid = prog.sb(ctx, "hid_ffn", [P, FT, T])
        taps = prog.sb(ctx, "taps", [P, 2, T])
        h_hi, h_lo = split_pair(prog, ctx)
        gate_ps = prog.ps(ctx, "gate_ps", [P, 2, T])
        up_ps = prog.ps(ctx, "up_ps", [P, 2, T])
        c0 = at["ffn"]
        pieces = []
        for m in range(FT):
            for j in range(2):
                w = ring.slot(c0 + m // 2, DK, 256, j * DK * 256)[:, :, (m % 2) * P:(m % 2 + 1) * P]
                pieces += [(c0 + m // 2, w[:, 0:4, :], False), (c0 + m // 2, w[:, 4:8, :], m % 2 == 1 and j == 1)]
        split = Split(prog, ctx, ring, pieces)
        split_tiles(prog, hT, h_hi, h_lo)
        with prog.stage(*Split.SEMS, "tap_ready", "conv_ready", "gelu_ready", "hid_ready", "step") as (block, s):
            @block.sync
            def _(sp):
                ring.run_ahead(sp, c0 + FT // 2)

            @block.tensor
            def _(pe):
                for m in range(FT):
                    for j, bank in enumerate((gate_ps, up_ps)):
                        if m >= 2:
                            pe.wait_ge(s["conv_ready"] if j == 0 else s["hid_ready"], m - 1)
                        for half in range(2):
                            split.product(pe, s, 4 * m + 2 * j + half, bank[:, m % 2, :], h_hi, h_lo, 4 * half,
                                          half == 0, half == 1)

            @block.scalar
            def _(act):
                def tap(m):
                    act.wait_ge(s["piece_used"], 4 * m + 2)
                    if m >= 2:
                        act.wait_ge(s["hid_ready"], m - 1)
                    act.activation(taps[:, m % 2, :], gate_ps[:, m % 2, :], ACT.Copy,
                                   scale=conv_w[:, 2, m:m + 1]).then_inc(s["tap_ready"], 1)

                def gelu(m):
                    act.wait_ge(s["conv_ready"], m + 1)
                    act.activation(taps[:, m % 2, :], taps[:, m % 2, :], ACT.Gelu_apprx_tanh,
                                   bias=conv_b[:, m:m + 1]).then_inc(s["gelu_ready"], 1)

                split.round(act, s, 0)
                for m in range(FT):
                    split.round(act, s, 4 * m + 1)
                    if m >= 1:
                        gelu(m - 1)
                    split.round(act, s, 4 * m + 2)
                    split.round(act, s, 4 * m + 3)
                    tap(m)
                    if m + 1 < FT:
                        split.round(act, s, 4 * m + 4)
                gelu(FT - 1)

            @block.vector
            def _(dve):
                def conv(m):
                    dve.wait_ge(s["tap_ready"], m + 1)
                    for i in (1, 2):
                        dve.scalar_tensor_tensor(out=taps[:, m % 2, i:T], in0=gate_ps[:, m % 2, 0:T - i],
                                                 scalar=conv_w[:, 2 - i, m:m + 1], in1=taps[:, m % 2, i:T],
                                                 op0=ALU.mult, op1=ALU.add).then_inc(s["conv_ready"] if i == 2 else s["step"], 1)
                        if i == 1:
                            dve.wait_ge(s["step"], m + 1)

                def product(m):
                    dve.wait_ge(s["gelu_ready"], m + 1)
                    dve.wait_ge(s["piece_used"], 4 * m + 4)
                    dve.tensor_tensor(hid[:, m, :], up_ps[:, m % 2, :], taps[:, m % 2, :], ALU.mult).then_inc(s["hid_ready"], 1)

                split.rest(dve, s, 0)
                for m in range(FT):
                    split.rest(dve, s, 4 * m + 1)
                    if m >= 1:
                        product(m - 1)
                    split.rest(dve, s, 4 * m + 2)
                    split.rest(dve, s, 4 * m + 3)
                    conv(m)
                    if m + 1 < FT:
                        split.rest(dve, s, 4 * m + 4)
                product(FT - 1)
        banks = prog.ps(ctx, "down", [P, 4, T])
        c1 = at["w_down"]
        with prog.stage("made", "added") as (block, s):
            @block.sync
            def _(sp):
                ring.run_ahead(sp, c1 + DK)

            @block.tensor
            def _(pe):
                for m in range(DK):
                    ring.wait(pe, c1 + m)
                    w = ring.slot(c1 + m, FT, P)
                    if m >= 4:
                        pe.wait_ge(s["added"], m - 3)
                    for k in range(FT):
                        last = pe.matmul(banks[:, m % 4, :], w[:, k, :], hid[:, k, :], start=(k == 0),
                                         stop=(k == FT - 1))
                    last.then_inc(s["made"], 1)
                    pe.wait_ge(s["made"], m + 1)
                    pe.sem_inc(ring.used, 1)

            @block.vector
            def _(dve):
                for m in range(DK):
                    dve.wait_ge(s["made"], m + 1)
                    dve.tensor_tensor(xT[:, m, :], banks[:, m % 4, :], xT[:, m, :], ALU.add).then_inc(s["added"], 1)



LAYERS = 2
ALPHA = (2 * LAYERS) ** 0.25
LN_EPS = 1e-5
SGU = 512
SGU_GROUPS = 8
EXPERTS, TOP, GROUPS, TOP_GROUPS = 64, 8, 8, 4
FF = 256
ROUTED_SCALE = 2.5
EXPERT = 3 * DK * FF
ABSENT = 1 << 16
ADA, ADA_FIRST = 12, 4
SHIFT1, SCALE1, GATE1, SHIFT2, SCALE2, GATE2 = [i * DK for i in range(6)]
C2_Q, C2_K, C2_V, C2_U, C2_Z, C2_GA, C2_GB = 0, 512, 640, 768, 1280, 1792, 2816


def second_chunks(d, l):
    w, ada = rows(d["w_in_2"][l]), rows(d["w_ada_2"][l])
    wba, wbb, wo = rows(d["w_branch_a_2"][l], 4), rows(d["w_branch_b_2"][l], 4), rows(d["w_out_2"][l])
    out, chunks = {}, []

    def add(name, *parts):
        out.setdefault(name, len(chunks))
        at, listed = 0, []
        for view in parts:
            k, n = view.shape[1], view.shape[2]
            listed.append((at, k, n, view))
            at += k * n
        chunks.append(listed)

    for m in range(ADA_FIRST):
        add("ada", ada[:, :, m * 512:(m + 1) * 512])
    add("q", w[:, :, C2_Q:C2_Q + 512])
    add("kv", w[:, :, C2_K:C2_K + 256])
    for m in range(ADA_FIRST, ADA):
        add("ada_rest", ada[:, :, m * 512:(m + 1) * 512])
    add("u", w[:, :, C2_U:C2_U + 512])
    add("z", w[:, :, C2_Z:C2_Z + 512])
    for m in range(DK):
        add("merge", w[:, :, C2_GA + m * P:C2_GA + (m + 1) * P], w[:, :, C2_GB + m * P:C2_GB + (m + 1) * P],
            wba[:, :, m * P:(m + 1) * P], wbb[:, :, m * P:(m + 1) * P])
    for m in range(2):
        add("w_out", wo[:, :, m * 512:(m + 1) * 512])
    add("shared", rows(d["ws_gate_2"][l]), rows(d["ws_up_2"][l]))
    add("shared_down", rows(d["ws_down_2"][l], 2))
    return chunks, out


def scale_rows(eng, ring, c, cond, acc, step):
    w = ring.slot(c, DK, 512)
    ring.wait(eng, c)
    step(eng.tensor_scalar(acc, w[:, 0, :], cond[:, 0:1], None, ALU.mult))
    for k in range(1, DK):
        step(eng.scalar_tensor_tensor(out=acc, in0=w[:, k, :], scalar=cond[:, k:k + 1], in1=acc, op0=ALU.mult,
                                      op1=ALU.add))
    eng.sem_inc(ring.used, 1)


def fold_rows(pool, ring, c, cond, acc, step):
    w = ring.slot(c, DK, 512)[:, 0:4, :]
    ring.wait(pool, c)
    step(pool.tensor_tensor(w, w, cond[:, 0:4, None].to_broadcast([P, 4, 512]), ALU.mult))
    step(pool.tensor_tensor(w[:, 0:2, :], w[:, 0:2, :], w[:, 2:4, :], ALU.add))
    return pool.tensor_tensor(acc, w[:, 0, :], w[:, 1, :], ALU.add)


def sum_columns(prog, pe, acc, bank):
    for j in range(acc.shape[-1] // P):
        last = pe.matmul(bank[:, j:j + 1], acc[:, j * P:(j + 1) * P], prog.ones[:, 0:1], start=True, stop=True)
    return last


def modulation(prog, ring, c0, bias, cond, mod):
    n = ADA_FIRST * 4
    with ExitStack() as ctx:
        acc = prog.sb(ctx, "ada_acc", [P, ADA_FIRST, 512])
        bank = prog.ps(ctx, "mod_ps", [P, n])
        with prog.stage("ada_ready", "made", "step") as (block, s):
            @block.sync
            def _(sp):
                ring.run_ahead(sp, c0 + ADA_FIRST)

            @block.tensor
            def _(pe):
                for i in range(ADA_FIRST):
                    pe.wait_ge(s["ada_ready"], i + 1)
                    sum_columns(prog, pe, acc[:, i, :], bank[:, 4 * i:4 * i + 4]).then_inc(s["made"], 1)

            @block.vector
            def _(dve):
                step = Chain(s["step"], dve)
                for i in range(ADA_FIRST):
                    scale_rows(dve, ring, c0 + i, cond, acc[:, i, :], step)
                    dve.sem_inc(s["ada_ready"], 1)
                dve.wait_ge(s["made"], ADA_FIRST)
                step(dve.tensor_tensor(mod[:, 0:n], bank[:, :], bias[:, 0:n], ALU.add))
                dve.tensor_scalar(mod[:, SCALE1:SCALE1 + DK], mod[:, SCALE1:SCALE1 + DK], 1.0, None, ALU.add)


def modulate(prog, xT, hT, mod, scale, shift):
    with prog.stage("read") as (block, s):
        @block.vector
        def _(dve):
            for k in range(DK):
                dve.tensor_scalar(hT[:, k, :], xT[:, k, :], mod[:, scale + k:scale + k + 1],
                                  mod[:, shift + k:shift + k + 1], ALU.mult, ALU.add).then_inc(s["read"], 1)

        @block.scalar
        def _(act):
            for k in range(DK):
                act.wait_ge(s["read"], k + 1)
                act.mul(xT[:, k, :], xT[:, k, :], ALPHA)


def layer_norm(prog, xT, gain, shift):
    nc = prog.nc
    with ExitStack() as ctx:
        sq = prog.sb(ctx, "squares", [P, 2, T])
        mean = prog.sb(ctx, "mean", [P, T])
        root = prog.sb(ctx, "root", [P, T])
        rstd = prog.sb(ctx, "rstd", [P, T])
        total = prog.ps(ctx, "total", [P, 2, T])
        with prog.stage("total_ready", "mean_ready", "centred", "squared", "summed", "root_ready",
                        "rstd_ready", "scaled") as (block, s):
            @block.tensor
            def _(pe):
                for k in range(DK):
                    last = pe.matmul(total[:, 0, :], prog.ones[:, :], xT[:, k, :], start=(k == 0), stop=(k == DK - 1))
                last.then_inc(s["total_ready"], 1)
                for k in range(DK):
                    pe.wait_ge(s["squared"], k + 1)
                    pe.matmul(total[:, 1, :], prog.ones[:, :], sq[:, k % 2, :], start=(k == 0),
                              stop=(k == DK - 1)).then_inc(s["summed"], 1)

            @block.scalar
            def _(act):
                for k in range(DK):
                    act.wait_ge(s["centred"], k + 1)
                    if k >= 2:
                        act.wait_ge(s["summed"], k - 1)
                    act.activation(sq[:, k % 2, :], xT[:, k, :], ACT.Square).then_inc(s["squared"], 1)
                act.wait_ge(s["summed"], DK)
                act.activation(root[:, :], total[:, 1, :], ACT.Sqrt, bias=prog.ln_eps[:, 0:1],
                               scale=1.0 / D).then_inc(s["root_ready"], 1)
                for k in range(DK):
                    act.wait_ge(s["scaled"], k + 1)
                    act.activation(xT[:, k, :], xT[:, k, :], ACT.Identity, bias=shift[:, k:k + 1])

            @block.vector
            def _(dve):
                dve.wait_ge(s["total_ready"], 1)
                dve.tensor_scalar(mean[:, :], total[:, 0, :], 1.0 / D, None, ALU.mult).then_inc(s["mean_ready"], 1)
                dve.wait_ge(s["mean_ready"], 1)
                for k in range(DK):
                    dve.tensor_tensor(xT[:, k, :], xT[:, k, :], mean[:, :], ALU.subtract).then_inc(s["centred"], 1)
                dve.wait_ge(s["root_ready"], 1)
                dve.reciprocal(rstd[:, :], root[:, :]).then_inc(s["rstd_ready"], 1)
                dve.wait_ge(s["rstd_ready"], 1)
                for k in range(DK):
                    dve.scalar_tensor_tensor(out=xT[:, k, :], in0=xT[:, k, :], scalar=gain[:, k:k + 1],
                                             in1=rstd[:, :], op0=ALU.mult, op1=ALU.mult).then_inc(s["scaled"], 1)


def rotate(prog, tiles):
    nc, d = prog.nc, prog.dram
    with ExitStack() as ctx:
        turned = prog.sb(ctx, "rotated", [P, 2, T])
        banks = prog.ps(ctx, "swapped", [P, 2, T])
        cos, sin, swap = prog.cos, prog.sin, prog.swap
        with prog.stage("swapped", "sin_ready", "cos_ready", "done") as (block, s):
            @block.tensor
            def _(pe):
                for i, x in enumerate(tiles):
                    if i >= 2:
                        pe.wait_ge(s["sin_ready"], i - 1)
                    pe.matmul(banks[:, i % 2, :], swap, x, start=True, stop=True).then_inc(s["swapped"], 1)

            @block.vector
            def _(dve):
                for i, x in enumerate(tiles):
                    dve.wait_ge(s["swapped"], i + 1)
                    dve.tensor_tensor(turned[:, i % 2, :], banks[:, i % 2, :], sin, ALU.mult).then_inc(s["sin_ready"], 1)
                    dve.tensor_tensor(x, x, cos, ALU.mult).then_inc(s["cos_ready"], 1)
                    dve.wait_ge(s["sin_ready"], i + 1)
                    dve.wait_ge(s["cos_ready"], i + 1)
                    dve.tensor_tensor(x, x, turned[:, i % 2, :], ALU.add).then_inc(s["done"], 1)
                    dve.wait_ge(s["done"], i + 1)


def self_attention(prog, ring, at, h, oT, qk, cond, acc):
    with ExitStack() as ctx:
        qT = oT
        kT = prog.sb(ctx, "kT_s", [P, 1, T])
        v_tok = prog.sb(ctx, "v_tok_s", [P, TT, P])
        o_tok = prog.sb(ctx, "o_tok_s", [P, TT, 512])
        q, kv = at["q"], at["kv"]
        tiles = feature_tiles(ring, q, 512, 0, qT)
        tiles += feature_tiles(ring, kv, 256, 0, kT)
        tiles += feature_tiles(ring, kv, 256, 128, o_tok[:, 0:1, :])
        project(prog, ring, tiles, h, q, kv + 1)
        to_tokens(prog, o_tok[:, 0:1, :], v_tok)
        norm_heads(prog, [(qT[:, i, :], qk[:, 0:1]) for i in range(4)] + [(kT[:, 0, :], qk[:, 1:2])])
        rotate(prog, [qT[:, i, :] for i in range(4)] + [kT[:, 0, :]])
        padded = prog.sb(ctx, "padded", [P, H, T])
        pad_heads(prog, qT, padded, lambda h: h // 4)
        units = []
        for h in range(H):
            g = h // 4
            for t in range(TT):
                units.append(unit(padded[:, h, t * P:(t + 1) * P], kT[:, 0, :], T,
                                  [(P, v_tok[:, j, g * HD:(g + 1) * HD]) for j in range(TT)],
                                  o_tok[:, t, h * HD:(h + 1) * HD]))
        attention(prog, units, (ring, at["ada_rest"], cond, acc))
        to_features(prog, o_tok, oT)


def spatial_gating(prog, ring, at, l, h, oT, acc, bias, mod):
    nc, d = prog.nc, prog.dram
    with ExitStack() as ctx:
        v = prog.sb(ctx, "v_sgu", [P, TT, SGU])
        u, z = at["u"], at["z"]
        tiles = feature_tiles(ring, u, 512, 0, oT)
        zT = prog.sb(ctx, "zT", [P, 4, T])
        tiles += feature_tiles(ring, z, 512, 0, zT)
        project(prog, ring, tiles, h, u, z + 1)
        to_tokens(prog, zT, v)
        affine = prog.sb(ctx, "affine", [P, 2, SGU])
        w_s = prog.sb(ctx, "w_s", [P, SGU_GROUPS, P])
        w_sT = prog.sb(ctx, "w_sT", [P, SGU_GROUPS, P])
        b_s = prog.sb(ctx, "b_s", [SGU_GROUPS, P])
        pairs = prog.sb(ctx, "pairs", [SGU_GROUPS, SGU])
        b_wide = prog.sb(ctx, "b_wide", [P, 4, P])
        stats = prog.sb(ctx, "stats", [P, TT, 6])
        moments = prog.sb(ctx, "moments", [P, TT, 4])
        work = prog.sb(ctx, "work", [P, 2, T])
        rest = ADA_FIRST * 4
        mod_ps = prog.ps(ctx, "mod_ps", [P, 6 * DK - rest])
        wide = prog.ps(ctx, "wide", [P, 4, P])
        banks = prog.ps(ctx, "mixed", [P, 2, T])
        with prog.stage("loaded", "mod_made", "gelu_v", "step", "moments_ready", "root_ready") as (block, s):
            @block.tensor
            def _(pe):
                sum_columns(prog, pe, acc[:, :, :].rearrange("p i n -> p (i n)"), mod_ps).then_inc(s["mod_made"], 1)

            @block.sync
            def _(sp):
                sp.dma_start(w_s[:, :, :], d["w_spatial_2"][l].rearrange("g i j -> i g j")).then_inc(s["loaded"], 16)
                sp.dma_start(b_s[:, :], d["b_spatial_2"][l]).then_inc(s["loaded"], 16)
                sp.dma_start(pairs[:, :], d["cst_pairs"]).then_inc(s["loaded"], 16)
                sp.dma_start(affine[:, 0, :], d["sgu_ln_g_2"][bass.ds(l, 1), :].to_broadcast([P, SGU])).then_inc(s["loaded"], 16)
                sp.dma_start(affine[:, 1, :], d["sgu_ln_b_2"][bass.ds(l, 1), :].to_broadcast([P, SGU])).then_inc(s["loaded"], 16)
                sp.wait_ge(s["loaded"], 80)

            @block.scalar
            def _(act):
                for t in range(TT):
                    act.activation(v[:, t, :], v[:, t, :], ACT.Gelu).then_inc(s["gelu_v"], 1)
                for m in range(4):
                    act.activation(oT[:, m, :], oT[:, m, :], ACT.Gelu)
                act.wait_ge(s["moments_ready"], TT)
                act.activation(moments[:, :, 2], moments[:, :, 1], ACT.Sqrt,
                               bias=prog.ln_eps[:, 0:1]).then_inc(s["root_ready"], 1)

            @block.vector
            def _(dve):
                link = Chain(s["step"], dve)
                for t in range(TT):
                    dve.wait_ge(s["gelu_v"], t + 1)
                    link(dve.bn_stats(stats[:, t, :], v[:, t, :]))
                    dve.bn_aggr(moments[:, t, 0:2], stats[:, t, :]).then_inc(s["moments_ready"], 1)
                dve.wait_ge(s["root_ready"], 1)
                dve.wait_ge(s["loaded"], 80)
                link(dve.reciprocal(moments[:, :, 3], moments[:, :, 2]))
                for t in range(TT):
                    link(dve.tensor_scalar(v[:, t, :], v[:, t, :], moments[:, t, 0:1], moments[:, t, 3:4],
                                           ALU.subtract, ALU.mult))
                    link(dve.tensor_tensor(v[:, t, :], v[:, t, :], affine[:, 0, :], ALU.mult))
                    link(dve.tensor_tensor(v[:, t, :], v[:, t, :], affine[:, 1, :], ALU.add))
                dve.wait_ge(s["mod_made"], 1)
                link(dve.tensor_tensor(mod[:, rest:6 * DK], mod_ps[:, :], bias[:, rest:6 * DK], ALU.add))
                dve.tensor_scalar(mod[:, SCALE2:SCALE2 + DK], mod[:, SCALE2:SCALE2 + DK], 1.0, None, ALU.add)
        transpose_tiles(prog, [([w_s[:, g, :] for g in range(4 * j, 4 * j + 4)],
                                w_sT[:, 4 * j:4 * j + 4, :].rearrange("p g i -> p (g i)")) for j in range(2)])
        with prog.stage("wide_ready", "b_ready", "mixed_ready", "step") as (block, s):
            @block.tensor
            def _(pe):
                for m in range(4):
                    last = pe.matmul(wide[:, m, :], pairs[:, m * P:(m + 1) * P], b_s[:, :], start=True, stop=True)
                last.then_inc(s["wide_ready"], 1)
                for m in range(4):
                    if m >= 2:
                        pe.wait_ge(s["step"], 2 * (m - 1))
                    for g in (2 * m, 2 * m + 1):
                        ps = half(g)
                        for t in range(TT):
                            last = pe.matmul(banks[ps, m % 2, t * P:(t + 1) * P], v[:, t, g * HD:(g + 1) * HD],
                                             w_sT[:, g, :], start=True, stop=True)
                    last.then_inc(s["mixed_ready"], 1)

            @block.vector
            def _(dve):
                link = Chain(s["step"], dve)
                dve.wait_ge(s["wide_ready"], 1)
                dve.tensor_copy(b_wide[:, :, :], wide[:, :, :]).then_inc(s["b_ready"], 1)
                dve.wait_ge(s["b_ready"], 1)
                for m in range(4):
                    dve.wait_ge(s["mixed_ready"], m + 1)
                    for_each = b_wide[:, m:m + 1, :].to_broadcast([P, TT, P])
                    link(dve.tensor_tensor(work[:, m % 2, :].rearrange("p (t i) -> p t i", t=TT),
                                           banks[:, m % 2, :].rearrange("p (t i) -> p t i", t=TT), for_each, ALU.add))
                    link(dve.tensor_tensor(oT[:, m, :], oT[:, m, :], work[:, m % 2, :], ALU.mult))


def route(prog, ring, at, rw, rb, hT, h_tok, weight, sel, hid):
    nc, d = prog.nc, prog.dram
    with ExitStack() as ctx:
        score = prog.sb(ctx, "score", [P, TT, EXPERTS])
        left = prog.sb(ctx, "left_over", [P, TT, EXPERTS])
        best = prog.sb(ctx, "best", [P, TT, GROUPS, 8])
        groups = prog.sb(ctx, "group_scores", [P, TT, 2 * GROUPS])
        rank = prog.sb(ctx, "rank", [P, TT, 2 * GROUPS])
        mass = prog.sb(ctx, "mass", [P, TT, 2])
        bank = prog.ps(ctx, "router_ps", [P, TT, EXPERTS])
        NONE = -3e38
        silu = prog.sb(ctx, "silu", [P, 2, T])
        gate_ps = prog.ps(ctx, "gate_ps", [P, 2, T])
        up_ps = prog.ps(ctx, "up_ps", [P, 2, T])
        c0 = at["shared"]
        with prog.stage("made", "scored", "step", "gate_made", "up_made", "silu_ready", "stored") as (block, s):
            @block.sync
            def _(sp):
                ring.run_ahead(sp, c0 + 2)
                sp.dma_start(d["tokens"].rearrange("(t p) n -> p t n", p=P), h_tok[:, :, :]).then_inc(s["stored"], 16)
                sp.wait_ge(s["stored"], 16)

            @block.tensor
            def _(pe):
                for t in range(TT):
                    for k in range(DK):
                        last = pe.matmul(bank[:, t, :], hT[:, k, t * P:(t + 1) * P], rw[:, k, :], start=(k == 0),
                                         stop=(k == DK - 1))
                last.then_inc(s["made"], 1)
                ring.wait(pe, c0)
                for m in range(2):
                    for j, (shared_ps, ready) in enumerate(((gate_ps, s["gate_made"]), (up_ps, s["up_made"]))):
                        w = ring.slot(c0, DK, FF, j * DK * FF)
                        for k in range(DK):
                            last = pe.matmul(shared_ps[:, m, :], w[:, k, m * P:(m + 1) * P], hT[:, k, :],
                                             start=(k == 0), stop=(k == DK - 1))
                        last.then_inc(ready, 1)

            @block.scalar
            def _(act):
                act.wait_ge(s["made"], 1)
                act.activation(score[:, :, :], bank[:, :, :], ACT.Sigmoid).then_inc(s["scored"], 1)
                for m in range(2):
                    act.wait_ge(s["gate_made"], m + 1)
                    act.activation(silu[:, m, :], gate_ps[:, m, :], ACT.Silu).then_inc(s["silu_ready"], 1)

            @block.vector
            def _(dve):
                link = Chain(s["step"], dve)
                dve.wait_ge(s["scored"], 1)
                link(dve.memset(groups[:, :, :], NONE))
                link(dve.tensor_tensor(sel[:, :, :], score[:, :, :],
                                       rb[:, :].unsqueeze(1).to_broadcast([P, TT, EXPERTS]), ALU.add))
                for t in range(TT):
                    for g in range(GROUPS):
                        last = dve.max(best[:, t, g, :], sel[:, t, g * 8:(g + 1) * 8])
                link(last)
                link(dve.tensor_tensor(groups[:, :, 0:GROUPS], best[:, :, :, 0], best[:, :, :, 1], ALU.add))
                for t in range(TT):
                    last = dve.max(rank[:, t, 0:8], groups[:, t, 0:GROUPS])
                link(last)
                link(dve.memset(rank[:, :, TOP_GROUPS:8], NONE))
                for t in range(TT):
                    last = dve.match_replace(left[:, t, 0:2 * GROUPS], rank[:, t, 0:8], groups[:, t, :], -2e38)
                link(last)
                link(dve.tensor_tensor(groups[:, :, 0:GROUPS], left[:, :, 0:GROUPS], groups[:, :, 0:GROUPS],
                                       ALU.not_equal))
                spread = groups[:, :, 0:GROUPS].unsqueeze(3).to_broadcast([P, TT, GROUPS, 8])
                by_group = (lambda x: x[:, :, :].rearrange("p t (g e) -> p t g e", g=GROUPS))
                link(dve.tensor_tensor(by_group(sel), by_group(sel), spread, ALU.mult))
                link(dve.tensor_scalar(groups[:, :, 0:GROUPS], groups[:, :, 0:GROUPS], 1.0, 1e30, ALU.subtract,
                                       ALU.mult))
                link(dve.tensor_tensor(by_group(sel), by_group(sel), spread, ALU.add))
                for t in range(TT):
                    last = dve.max(rank[:, t, 0:8], sel[:, t, :])
                link(last)
                for t in range(TT):
                    last = dve.match_replace(left[:, t, :], rank[:, t, 0:8], sel[:, t, :], NONE)
                link(last)
                link(dve.tensor_tensor(sel[:, :, :], left[:, :, :], sel[:, :, :], ALU.not_equal))
                link(dve.tensor_tensor(weight[:, :, :], score[:, :, :], sel[:, :, :], ALU.mult))
                link(dve.tensor_reduce(mass[:, :, 0], weight[:, :, :], AX.X, ALU.add))
                link(dve.reciprocal(mass[:, :, 1], mass[:, :, 0]))
                for t in range(TT):
                    link(dve.tensor_scalar(weight[:, t, :], weight[:, t, :], mass[:, t, 1:2], ROUTED_SCALE, ALU.mult,
                                           ALU.mult))
                for m in range(2):
                    dve.wait_ge(s["silu_ready"], m + 1)
                    dve.wait_ge(s["up_made"], m + 1)
                    dve.tensor_tensor(hid[:, m, :], up_ps[:, m, :], silu[:, m, :], ALU.mult)


def make_lists(prog, ring, at, hid, acc, weight, sel, seat, info, plan):
    nc, d = prog.nc, prog.dram
    with ExitStack() as ctx:
        before, index, token = prog.before, prog.index, prog.token
        count = prog.sb(ctx, "count", [P, EXPERTS])
        blocks = prog.sb(ctx, "blocks", [P, EXPERTS])
        more = prog.sb(ctx, "more", [P, EXPERTS])
        upto = prog.sb(ctx, "upto", [P, EXPERTS])
        begun = prog.sb(ctx, "begun", [P, EXPERTS])
        turn = prog.sb(ctx, "turn", [P, TT, EXPERTS])
        col = prog.sb(ctx, "col", [P, 4])
        pairs = prog.sb(ctx, "pair_count", [1, EXPERTS + 1])
        place_ps = prog.ps(ctx, "place_ps", [P, TT, EXPERTS])
        count_ps = prog.ps(ctx, "count_ps", [P, EXPERTS])
        plan_ps = prog.ps(ctx, "plan_ps", [1, 2 * P])
        down_ps = prog.ps(ctx, "down_ps", [P, 4, T])
        with prog.stage("counted", "cols_ready", "turned", "step", "down_made", "copied") as (block, s):
            @block.tensor
            def _(pe):
                for t in range(TT):
                    for j in range(t + 1):
                        pe.matmul(place_ps[:, t, :], before if j == t else prog.ones[:, :], sel[:, j, :],
                                  start=(j == 0), stop=(j == t))
                for t in range(TT):
                    last = pe.matmul(count_ps[:, :], prog.ones[:, :], sel[:, t, :], start=(t == 0), stop=(t == TT - 1))
                last.then_inc(s["counted"], 1)
                c = at["shared_down"]
                ring.wait(pe, c)
                w = ring.slot(c, 2, D)
                for j in range(2 * TT):
                    t, side = j // 2, j % 2
                    if j >= 4:
                        pe.wait_ge(s["copied"], j - 3)
                    for k in range(2):
                        last = pe.matmul(down_ps[:, j % 4, :], hid[:, k, t * P:(t + 1) * P],
                                         w[:, k, side * 512:(side + 1) * 512], start=(k == 0), stop=(k == 1))
                    last.then_inc(s["down_made"], 1)
                pe.wait_ge(s["cols_ready"], 1)
                for i in range(2):
                    last = pe.matmul(plan_ps[:, i * P:(i + 1) * P], col[:, i:i + 1], prog.ident[:, :], start=True,
                                     stop=True)
                last.then_inc(s["turned"], 1)

            @block.scalar
            def _(act):
                for j in range(2 * TT):
                    t, side = j // 2, j % 2
                    act.wait_ge(s["down_made"], j + 1)
                    act.copy(acc[:, t, side * 512:(side + 1) * 512], down_ps[:, j % 4, :]).then_inc(s["copied"], 1)

            @block.vector
            def _(dve):
                link = Chain(s["step"], dve)
                dve.wait_ge(s["counted"], 1)
                link(dve.tensor_copy(count[:, :], count_ps[:, :]))
                link(dve.tensor_scalar(blocks[:, :], count[:, :], 0.0, None, ALU.is_gt))
                for m in range(1, TT):
                    link(dve.tensor_scalar(more[:, :], count[:, :], float(P * m), None, ALU.is_gt))
                    link(dve.tensor_tensor(blocks[:, :], blocks[:, :], more[:, :], ALU.add))
                one = prog.ones[:, 0:EXPERTS]
                link(dve.tensor_tensor_scan(upto[:, :], one, blocks[:, :], 0.0, ALU.mult, ALU.add))
                link(dve.tensor_tensor(begun[:, :], upto[:, :], blocks[:, :], ALU.subtract))
                link(dve.tensor_scalar(more[:, :], begun[:, :], index, None, ALU.is_le))
                link(dve.tensor_reduce(col[:, 2:3], more[:, :], AX.X, ALU.add))
                link(dve.tensor_scalar(col[:, 0:1], col[:, 2:3], -1.0, None, ALU.add))
                link(dve.tensor_tensor(more[:, :], more[:, :], begun[:, :], ALU.mult))
                link(dve.tensor_reduce(col[:, 2:3], more[:, :], AX.X, ALU.max))
                link(dve.tensor_tensor(col[:, 3:4], index, col[:, 2:3], ALU.subtract))
                dve.tensor_scalar(col[:, 1:2], col[:, 3:4], float(TT), None, ALU.min).then_inc(s["cols_ready"], 1)
                link(dve.tensor_scalar(pairs[:, 0:EXPERTS], prog.count[0:1, 0:2 * EXPERTS:2],
                                       upto[0:1, EXPERTS - 1:EXPERTS], None, ALU.is_lt))
                link(dve.tensor_reduce(pairs[:, EXPERTS:EXPERTS + 1], pairs[:, 0:EXPERTS], AX.X, ALU.add))
                link(dve.tensor_scalar(plan[:, 2 * P:2 * P + 1], pairs[:, EXPERTS:EXPERTS + 1], -1.0, None, ALU.add))
                dve.wait_ge(s["turned"], 1)
                link(dve.tensor_copy(plan[:, 0:2 * P], plan_ps[:, :]))
                link(dve.scalar_tensor_tensor(out=seat[:, :, :], in0=place_ps[:, :, :], scalar=1.0, in1=sel[:, :, :],
                                              op0=ALU.add, op1=ALU.mult))
                link(dve.tensor_scalar(seat[:, :, :], seat[:, :, :], -1.0, None, ALU.add))
                for t in range(TT):
                    link(dve.tensor_tensor_scan(turn[:, t, :], one, sel[:, t, :], 0.0, ALU.mult, ALU.add))
                    link(dve.tensor_tensor(turn[:, t, :], turn[:, t, :], sel[:, t, :], ALU.subtract))
                    link(dve.tensor_scalar(col[:, 2:3], token[:, t:t + 1], float(TOP), -float(ABSENT), ALU.mult, ALU.add))
                    link(dve.tensor_scalar(info[:, t, :, 1], turn[:, t, :], col[:, 2:3], None, ALU.add))
                    link(dve.tensor_scalar(col[:, 2:3], token[:, t:t + 1], -float(ABSENT), None, ALU.add))
                    link(dve.tensor_scalar(info[:, t, :, 0], prog.zeros[:, 0:EXPERTS], col[:, 2:3], None, ALU.add))
                    link(dve.tensor_copy(info[:, t, :, 2], weight[:, t, :]))


def routed_experts(prog, ring, l, seat, info, plan):
    nc, d = prog.nc, prog.dram
    mem = ring.mem[:, :, :].rearrange("p s n -> p (s n)")
    gu = [mem[:, b * EXPERT:b * EXPERT + 2 * DK * FF].rearrange("p (k n) -> p k n", k=DK) for b in range(2)]
    dn = [mem[:, b * EXPERT + 2 * DK * FF:(b + 1) * EXPERT].rearrange("p (k n) -> p k n", k=2) for b in range(2)]
    wg, wu, wd = d["w_gate_2"], d["w_up_2"], d["w_down_2"]
    with ExitStack() as ctx:
        seats = prog.sb(ctx, "seats", [P, 2, TT, P])
        note = prog.sb(ctx, "note", [P, P, 3])
        read_at = ctx.enter_context(nc.sbuf_tensor(f"read_at_{prog.stages}", [P, 2], mybir.dt.uint32))
        write_at = ctx.enter_context(nc.sbuf_tensor(f"write_at_{prog.stages}", [P, 2], mybir.dt.uint32))
        x = prog.sb(ctx, "x_seats", [P, 2, D])
        xT = prog.sb(ctx, "x_turned", [P, 2, DK, P])
        gated = prog.sb(ctx, "gated", [P, 2, FF])
        hid = prog.sb(ctx, "hid_seats", [P, 2, FF])
        hidT = prog.sb(ctx, "hid_turned", [P, 2, FF])
        y = prog.sb(ctx, "y_seats", [P, 2, D])
        find_ps = prog.ps(ctx, "find_ps", [P, T])
        turn_ps = prog.ps(ctx, "turn_ps", [P, 2, T])
        up_ps = prog.ps(ctx, "up_ps", [P, 2, T])
        hid_ps = prog.ps(ctx, "hid_ps", [P, T])
        y_ps = prog.ps(ctx, "y_ps", [P, 2, T])
        with prog.stage("gu_loaded_0", "gu_loaded_1", "dn_loaded_0", "dn_loaded_1", "matched", "found", "noted",
                        "read_noted", "turned", "copied_dve", "copied_act", "up_made", "silu_ready",
                        "hid_ready", "hid_turned", "hid_copied", "down_made", "write_noted", "y_dve", "y_act",
                        "cleared", "go", pool_dma=("gathered_0", "gathered_1", "scattered_0", "scattered_1")) as (block, s):
            gathered, scattered = (s["gathered_0"], s["gathered_1"]), (s["scattered_0"], s["scattered_1"])
            gu_loaded, dn_loaded = (s["gu_loaded_0"], s["gu_loaded_1"]), (s["dn_loaded_0"], s["dn_loaded_1"])

            def end_of(eng):
                return eng.value_load(plan[0:1, 2 * P:2 * P + 1], min_val=15, max_val=47)

            def past(j, n):
                return not isinstance(j, int) or j >= n

            def expert_of(eng, j):
                return eng.value_load(plan[0:1, bass.ds(j, 1)], min_val=0, max_val=EXPERTS - 1)

            @block.sync
            def _(sp):
                def load(r, b):
                    j = 2 * r + b
                    e = expert_of(sp, j)
                    if past(j, 2):
                        sp.wait_ge(s["up_made"], j - 1)
                    sp.dma_start(gu[b][:, :, 0:FF], rows(wg[l, e])).then_inc(gu_loaded[b], 16)
                    sp.dma_start(gu[b][:, :, FF:2 * FF], rows(wu[l, e])).then_inc(gu_loaded[b], 16)
                    if past(j, 2):
                        sp.wait_ge(s["down_made"], 2 * (j - 1))
                    sp.dma_start(dn[b], rows(wd[l, e], 2)).then_inc(dn_loaded[b], 16)

                for b in range(2):
                    load(0, b)
                with sp.Fori(1, end_of(sp) + 1) as r:
                    for b in range(2):
                        load(r, b)

            @block.gpsimd
            def _(pool):
                def gather(r, b):
                    j = 2 * r + b
                    pool.wait_ge(s["cleared"], 1)
                    pool.wait_ge(s["read_noted"], j + 1)
                    if past(j, 2):
                        pool.wait_ge(s["turned"], j - 1)
                    pool.sem_inc(s["go"], 1)
                    pool.indirect_dma_start(x[:, b, :], None, d["tokens"],
                                            bass.IndirectOffsetOnAxis(ap=read_at[:, b:b + 1], axis=0),
                                            bounds_check=last_token, oob_is_err=False).then_inc(gathered[b], 16)

                def scatter(r, b):
                    j = 2 * r + b
                    pool.wait_ge(s["cleared"], 1)
                    pool.wait_ge(s["write_noted"], j + 1)
                    pool.wait_ge(s["y_dve"], j + 1)
                    pool.wait_ge(s["y_act"], j + 1)
                    pool.wait_ge(s["cleared"], 1)
                    pool.sem_inc(s["go"], 1)
                    pool.indirect_dma_start(d["results"],
                                            bass.IndirectOffsetOnAxis(ap=write_at[:, b:b + 1], axis=0), y[:, b, :],
                                            None, bounds_check=last_row, oob_is_err=False).then_inc(scattered[b], 16)

                pool.memset(x[:, :, :], 0.0).then_inc(s["cleared"], 1)
                end = end_of(pool)
                last_token, last_row = pool.to_reg(T - 1), pool.to_reg(TOP * T - 1)
                gather(0, 0)
                gather(0, 1)
                gather(1, 0)
                gather(1, 1)
                scatter(0, 0)
                def both(r):
                    gather(r + 1, 0)
                    scatter(r - 1, 1)
                    gather(r + 1, 1)
                    scatter(r, 0)

                both(1)
                with pool.Fori(2, end + 1) as r:
                    both(r)
                scatter(end, 1)
                for b in range(2):
                    pool.wait_ge(scattered[b], 16 * end + 16)
                    pool.wait_ge(gathered[b], 16 * end + 32)

            @block.tensor
            def _(pe):
                def find(r, b):
                    j = 2 * r + b
                    e = expert_of(pe, j)
                    pe.wait_ge(s["matched"], j + 1)
                    if past(j, 1):
                        pe.wait_ge(s["noted"], j)
                    for t in range(TT):
                        last = pe.matmul(find_ps[:, 0:3], seats[:, b, t, :], info[:, t, bass.ds(e, 1), :],
                                         start=(t == 0), stop=(t == TT - 1))
                    last.then_inc(s["found"], 1)

                def turn(r, b):
                    j = 2 * r + b
                    pe.wait_ge(gathered[b], 16 * (r + 1))
                    if past(j, 1):
                        pe.wait_ge(s["copied_dve"], j)
                        pe.wait_ge(s["copied_act"], j)
                    for k in range(DK):
                        last = pe.transpose(turn_ps[:, k // 4, (k % 4) * P:(k % 4 + 1) * P], x[:, b, k * P:(k + 1) * P],
                                            prog.ident[:, :])
                    last.then_inc(s["turned"], 1)

                def up(r, b):
                    j = 2 * r + b
                    pe.wait_ge(gu_loaded[b], 32 * (r + 1))
                    pe.wait_ge(s["copied_dve"], j + 1)
                    pe.wait_ge(s["copied_act"], j + 1)
                    if past(j, 2):
                        pe.wait_ge(s["hid_ready"], j - 1)
                    for k in range(DK):
                        last = pe.matmul(up_ps[:, b, :], xT[:, b, k, :], gu[b][:, k, :], start=(k == 0),
                                         stop=(k == DK - 1))
                    last.then_inc(s["up_made"], 1)

                def turn_hidden(r, b):
                    j = 2 * r + b
                    pe.wait_ge(s["hid_ready"], j + 1)
                    if past(j, 1):
                        pe.wait_ge(s["hid_copied"], j)
                    for k in range(2):
                        last = pe.transpose(hid_ps[:, k * P:(k + 1) * P], hid[:, b, k * P:(k + 1) * P], prog.ident[:, :])
                    last.then_inc(s["hid_turned"], 1)

                def down(r, b):
                    j = 2 * r + b
                    pe.wait_ge(dn_loaded[b], 16 * (r + 1))
                    pe.wait_ge(s["hid_copied"], j + 1)
                    for side in range(2):
                        if past(j, 1):
                            pe.wait_ge(s["y_dve"] if side == 0 else s["y_act"], j)
                        for k in range(2):
                            last = pe.matmul(y_ps[:, side, :], hidT[:, b, k * P:(k + 1) * P],
                                             dn[b][:, k, side * 512:(side + 1) * 512], start=(k == 0), stop=(k == 1))
                        last.then_inc(s["down_made"], 1)

                end = end_of(pe)
                find(0, 0)
                find(0, 1)
                turn(0, 0)
                find(1, 0)
                up(0, 0)
                turn(0, 1)
                turn_hidden(0, 0)
                find(1, 1)
                up(0, 1)
                down(0, 0)
                turn(1, 0)
                turn_hidden(0, 1)
                def both(r):
                    find(r + 1, 0)
                    up(r, 0)
                    down(r - 1, 1)
                    turn(r, 1)
                    turn_hidden(r, 0)
                    find(r + 1, 1)
                    up(r, 1)
                    down(r, 0)
                    turn(r + 1, 0)
                    turn_hidden(r, 1)

                both(1)
                with pe.Fori(2, end + 1) as r:
                    both(r)
                down(end, 1)

            @block.scalar
            def _(act):
                def copy(r, b):
                    j = 2 * r + b
                    act.wait_ge(s["turned"], j + 1)
                    if past(j, 2):
                        act.wait_ge(s["up_made"], j - 1)
                    act.copy(xT[:, b, 4:8, :].rearrange("p k n -> p (k n)"), turn_ps[:, 1, :]).then_inc(s["copied_act"], 1)

                def silu(r, b):
                    j = 2 * r + b
                    act.wait_ge(s["up_made"], j + 1)
                    if past(j, 2):
                        act.wait_ge(s["hid_ready"], j - 1)
                    act.activation(gated[:, b, :], up_ps[:, b, 0:FF], ACT.Silu).then_inc(s["silu_ready"], 1)

                def copy_hidden(r, b):
                    j = 2 * r + b
                    act.wait_ge(s["hid_turned"], j + 1)
                    if past(j, 2):
                        act.wait_ge(s["down_made"], 2 * (j - 1))
                    act.copy(hidT[:, b, :], hid_ps[:, 0:FF]).then_inc(s["hid_copied"], 1)

                def weigh(r, b):
                    j = 2 * r + b
                    act.wait_ge(s["down_made"], 2 * (j + 1))
                    act.wait_ge(s["noted"], j + 1)
                    if past(j, 2):
                        act.wait_ge(scattered[b], 16 * r)
                    act.activation(y[:, b, 512:1024], y_ps[:, 1, :], ACT.Copy,
                                   scale=note[:, bass.ds(j, 1), 2]).then_inc(s["y_act"], 1)

                end = end_of(act)
                copy(0, 0)
                silu(0, 0)
                copy(0, 1)
                copy_hidden(0, 0)
                silu(0, 1)
                weigh(0, 0)
                copy(1, 0)
                copy_hidden(0, 1)
                def both(r):
                    silu(r, 0)
                    weigh(r - 1, 1)
                    copy(r, 1)
                    copy_hidden(r, 0)
                    silu(r, 1)
                    weigh(r, 0)
                    copy(r + 1, 0)
                    copy_hidden(r, 1)

                both(1)
                with act.Fori(2, end + 1) as r:
                    both(r)
                weigh(end, 1)

            @block.vector
            def _(dve):
                def match(r, b):
                    j = 2 * r + b
                    e = expert_of(dve, j)
                    k = dve.value_load(plan[0:1, bass.ds(j + P, 1)], min_val=0, max_val=TT)
                    if past(j, 2):
                        dve.wait_ge(s["found"], j - 1)
                    for t in range(TT):
                        last = dve.tensor_scalar(seats[:, b, t, :], prog.count[:, bass.ds(k * P, P)],
                                                 seat[:, t, bass.ds(e, 1)], None, ALU.is_equal)
                    last.then_inc(s["matched"], 1)

                def keep(r, b):
                    j = 2 * r + b
                    dve.wait_ge(s["found"], j + 1)
                    if past(j, 2):
                        dve.wait_ge(gathered[b], 16 * r)
                    dve.tensor_scalar(read_at[:, b:b + 1], find_ps[:, 0:1], float(ABSENT), None,
                                      ALU.add).then_inc(s["read_noted"], 1)
                    dve.tensor_copy(note[:, bass.ds(j, 1), :].rearrange("p a n -> p (a n)"),
                                    find_ps[:, 0:3]).then_inc(s["noted"], 1)

                def copy(r, b):
                    j = 2 * r + b
                    dve.wait_ge(s["turned"], j + 1)
                    if past(j, 2):
                        dve.wait_ge(s["up_made"], j - 1)
                    dve.tensor_copy(xT[:, b, 0:4, :].rearrange("p k n -> p (k n)"),
                                    turn_ps[:, 0, :]).then_inc(s["copied_dve"], 1)

                def product(r, b):
                    j = 2 * r + b
                    dve.wait_ge(s["silu_ready"], j + 1)
                    if past(j, 2):
                        dve.wait_ge(s["hid_turned"], j - 1)
                    dve.tensor_tensor(hid[:, b, :], up_ps[:, b, FF:2 * FF], gated[:, b, :],
                                      ALU.mult).then_inc(s["hid_ready"], 1)

                def weigh(r, b):
                    j = 2 * r + b
                    dve.wait_ge(s["noted"], j + 1)
                    if past(j, 2):
                        dve.wait_ge(scattered[b], 16 * r)
                    dve.tensor_scalar(write_at[:, b:b + 1], note[:, bass.ds(j, 1), 1], float(ABSENT), None,
                                      ALU.add).then_inc(s["write_noted"], 1)
                    dve.wait_ge(s["down_made"], 2 * j + 1)
                    dve.tensor_scalar(y[:, b, 0:512], y_ps[:, 0, :], note[:, bass.ds(j, 1), 2], None,
                                      ALU.mult).then_inc(s["y_dve"], 1)

                end = end_of(dve)
                match(0, 0)
                match(0, 1)
                keep(0, 0)
                match(1, 0)
                keep(0, 1)
                copy(0, 0)
                match(1, 1)
                keep(1, 0)
                product(0, 0)
                copy(0, 1)
                match(2, 0)
                keep(1, 1)
                product(0, 1)
                weigh(0, 0)
                copy(1, 0)
                match(2, 1)
                def both(r):
                    keep(r + 1, 0)
                    product(r, 0)
                    weigh(r - 1, 1)
                    copy(r, 1)
                    match(r + 2, 0)
                    keep(r + 1, 1)
                    product(r, 1)
                    weigh(r, 0)
                    copy(r + 1, 0)
                    match(r + 2, 1)

                both(1)
                with dve.Fori(2, end + 1) as r:
                    both(r)
                weigh(end, 1)


def combine(prog, acc):
    nc, d = prog.nc, prog.dram
    results = d["results"].rearrange("(t p r) n -> t p r n", p=P, r=TOP)
    with ExitStack() as ctx:
        rows_sb = prog.sb(ctx, "rows_sb", [P, 2, TOP, 512])
        total = prog.sb(ctx, "total", [P, 2, 512])
        with prog.stage("loaded_0", "loaded_1", "summed", "added") as (block, s):
            loaded = (s["loaded_0"], s["loaded_1"])

            @block.sync
            def _(sp):
                for j in range(2 * TT):
                    t, side = j // 2, j % 2
                    if j >= 2:
                        sp.wait_ge(s["summed"], j - 1)
                    sp.dma_start(rows_sb[:, j % 2, :, :],
                                 results[t, :, :, side * 512:(side + 1) * 512]).then_inc(loaded[j % 2], 16)

            @block.vector
            def _(dve):
                for j in range(2 * TT):
                    t, side = j // 2, j % 2
                    dve.wait_ge(loaded[j % 2], 16 * (j // 2 + 1))
                    dve.tensor_reduce(total[:, j % 2, :], rows_sb[:, j % 2, :, :].rearrange("p r n -> p n r"), AX.X,
                                      ALU.add).then_inc(s["summed"], 1)
                    dve.wait_ge(s["summed"], j + 1)
                    to = acc[:, t, side * 512:(side + 1) * 512]
                    dve.tensor_tensor(to, to, total[:, j % 2, :], ALU.add)


def add_tokens(prog, acc, xT, factor):
    nc = prog.nc
    with ExitStack() as ctx:
        banks = prog.ps(ctx, "turned_acc", [P, 4, T])
        with prog.stage("turned", "added") as (block, s):
            @block.tensor
            def _(pe):
                for m in range(DK):
                    if m >= 4:
                        pe.wait_ge(s["added"], m - 3)
                    for t in range(TT):
                        last = pe.transpose(banks[:, m % 4, t * P:(t + 1) * P], acc[:, t, m * P:(m + 1) * P],
                                            prog.ident[:, :])
                    last.then_inc(s["turned"], 1)

            @block.vector
            def _(dve):
                for m in range(DK):
                    dve.wait_ge(s["turned"], m + 1)
                    dve.scalar_tensor_tensor(out=xT[:, m, :], in0=banks[:, m % 4, :], scalar=factor[:, m:m + 1],
                                             in1=xT[:, m, :], op0=ALU.mult, op1=ALU.add).then_inc(s["added"], 1)


def second_block(prog, xT):
    nc, d = prog.nc, prog.dram
    with ExitStack() as ctx:
        small = prog.sb(ctx, "small_2", [P, 11 * DK + 2])
        mod = prog.sb(ctx, "mod", [P, 6 * DK])
        b_ada, cond = small[:, 0:6 * DK], small[:, 6 * DK:7 * DK]
        norms = small[:, 7 * DK:11 * DK].rearrange("p (i k) -> p i k", i=4)
        qk = small[:, 11 * DK:11 * DK + 2]
        rope = prog.sb(ctx, "rope", [P, 2 * T + P])
        router = prog.sb(ctx, "router", [P, DK * EXPERTS])
        rb = prog.sb(ctx, "router_bias", [P, EXPERTS])
        prog.cos, prog.sin, prog.swap = rope[:, 0:T], rope[:, T:2 * T], rope[:, 2 * T:2 * T + P]
        rw = router[:, :].rearrange("p (k n) -> p k n", k=DK)
        ring = Ring(prog, ctx, [], 4, DK * 512)
        lists = prog.sb(ctx, "lists", [P, P + (TT + 1) * P + 1 + TT])
        prog.before = lists[:, 0:P]
        prog.count = lists[:, P:P + (TT + 1) * P]
        prog.index = lists[:, P + (TT + 1) * P:P + (TT + 1) * P + 1]
        prog.token = lists[:, P + (TT + 1) * P + 1:P + (TT + 1) * P + 1 + TT]
        with prog.stage("loaded") as (block, s):
            @block.sync
            def _(sp):
                sp.dma_start(lists[:, :], d["cst_lists"]).then_inc(s["loaded"], 16)
                sp.dma_start(rope[:, :], d["cst_rope"]).then_inc(s["loaded"], 16)
                sp.wait_ge(s["loaded"], 32)

        prog.finish()
        with nc.Fori(0, LAYERS) as l:
            ring.chunks, at = second_chunks(d, l)
            ring.plan()
            with prog.stage("loaded") as (block, s):
                @block.sync
                def _(sp):
                    sp.dma_start(rw, rows(d["router_w_2"][l])).then_inc(s["loaded"], 16)
                    sp.dma_start(rb[:, :], d["router_bias_2"][bass.ds(l, 1), :].to_broadcast([P, EXPERTS])).then_inc(s["loaded"], 16)
                    sp.wait_ge(s["loaded"], 32)
            vectors(prog, ring, small[:, :],
                    [(0, 6 * DK, ALL, as_rows(d["b_ada_2"][l])), (6 * DK, DK, ALL, as_rows(d["c_2"][0]))]
                    + [((7 + i) * DK, DK, ALL, as_rows(d[name][l])) for i, name in
                       enumerate(("ln1_g_2", "ln1_b_2", "ln2_g_2", "ln2_b_2"))]
                    + [(11 * DK + i, 1, cols, d[name][bass.ds(l, 1), :]) for i, name in enumerate(("q_scale_2", "k_scale_2"))
                       for cols in (LEFT, RIGHT)])
            with prog.stage("none") as (block, s):
                @block.vector
                def _(dve):
                    dve.tensor_scalar(qk[:, 0:1], qk[:, 0:1], HD ** -0.5, None, ALU.mult)

                @block.scalar
                def _(act):
                    act.activation(cond, cond, ACT.Silu)
            modulation(prog, ring, at["ada"], b_ada, cond, mod)
            with ExitStack() as mixer:
                h = split_pair(prog, mixer)
                oT = prog.sb(mixer, "oT_m", [P, 2, 4, T])
                with ExitStack() as whole:
                    hT = prog.sb(whole, "hT_m", [P, DK, T])
                    modulate(prog, xT, hT, mod, SCALE1, SHIFT1)
                    split_tiles(prog, hT, *h)
                with ExitStack() as rest:
                    acc = prog.sb(rest, "ada_rest", [P, ADA - ADA_FIRST, 512])
                    self_attention(prog, ring, at, h, oT[:, 0, :, :], qk, cond, acc)
                    spatial_gating(prog, ring, at, l, h, oT[:, 1, :, :], acc, b_ada, mod)
                y = [prog.sb(mixer, name, [P, DK, T], R32) for name in ("y_hi", "y_lo")]
                merge_branches(prog, ring, at["merge"], h, oT, y, 2)
                residual_product(prog, ring, at["w_out"], y, xT, mod[:, GATE1:GATE1 + DK])
            layer_norm(prog, xT, norms[:, 0, :], norms[:, 1, :])
            with ExitStack() as moe:
                hT = prog.sb(moe, "hT_e", [P, DK, T])
                weight = prog.sb(moe, "weight", [P, TT, EXPERTS])
                sel = prog.sb(moe, "chosen", [P, TT, EXPERTS])
                seat = prog.sb(moe, "seat", [P, TT, EXPERTS])
                info = prog.sb(moe, "info", [P, TT, EXPERTS, 3])
                plan = moe.enter_context(nc.sbuf_tensor("plan", [1, 2 * P + 1], mybir.dt.int32))
                acc = prog.sb(moe, "acc", [P, TT, D])
                modulate(prog, xT, hT, mod, SCALE2, SHIFT2)
                with ExitStack() as early:
                    h_tok = prog.sb(early, "h_tok", [P, TT, D])
                    hid = prog.sb(early, "hid_shared", [P, 2, T])
                    transpose_tiles(prog, [([hT[:, m, t * P:(t + 1) * P] for m in range(4 * j, 4 * j + 4)],
                                            h_tok[:, t, j * 512:(j + 1) * 512]) for t in range(TT) for j in range(2)])
                    route(prog, ring, at, rw, rb, hT, h_tok, weight, sel, hid)
                    make_lists(prog, ring, at, hid, acc, weight, sel, seat, info, plan)
                routed_experts(prog, ring, l, seat, info, plan)
                combine(prog, acc)
                add_tokens(prog, acc, xT, mod[:, GATE2:GATE2 + DK])
            layer_norm(prog, xT, norms[:, 2, :], norms[:, 3, :])
            with prog.stage("none") as (block, s):
                @block.sync
                def _(sp):
                    ring.clear(sp)
            prog.finish()


def store(prog, xT, out):
    nc = prog.nc
    with ExitStack() as ctx:
        x_tok = prog.sb(ctx, "x_tok", [P, TT, D])
        transpose_tiles(prog, [([xT[:, m, t * P:(t + 1) * P] for m in range(4 * j, 4 * j + 4)],
                                x_tok[:, t, j * 512:(j + 1) * 512]) for t in range(TT) for j in range(2)])
        with prog.stage("stored") as (block, s):
            @block.sync
            def _(sp):
                for t in range(TT):
                    sp.dma_start(out[0, t * P:(t + 1) * P, :], x_tok[:, t, :]).then_inc(s["stored"], 16)
                sp.wait_ge(s["stored"], 16 * TT)


def build(nc, dram, out):
    prog = Program(nc, dram)
    dram["scratch"] = nc.dram_tensor("scratch", [H, P * L_TAB], F32, kind="Internal").ap()
    dram["tokens"] = nc.dram_tensor("tokens", [T, D], F32, kind="Internal").ap()
    dram["results"] = nc.dram_tensor("results", [T * TOP, D], F32, kind="Internal").ap()
    with ExitStack() as ctx:
        square = prog.sb(ctx, "square", [P, CST_W])
        prog.ones = prog.sb(ctx, "ones", [P, P])
        prog.zeros = prog.sb(ctx, "zeros", [P, T])
        prog.eps = prog.sb(ctx, "eps", [P, 1])
        prog.ln_eps = prog.sb(ctx, "ln_eps", [P, 1])
        prog.ident = square[:, IDENT:IDENT + P]
        prog.block_ones = square[:, BLOCK:BLOCK + P]
        prog.window = square[:, WIN:WIN + P]
        prog.causal = square[:, CAUSAL:CAUSAL + T]
        prog.seen = square[:, SEEN:SEEN + 1]
        prog.fox = square[:, FOXSEL:FOXSEL + H]
        xT = prog.sb(ctx, "xT", [P, DK, T])
        with prog.stage("loaded") as (block, s):
            @block.sync
            def _(sp):
                sp.dma_start(square[:, :], dram["cst_square"]).then_inc(s["loaded"], 16)
                sp.wait_ge(s["loaded"], 16)

            @block.gpsimd
            def _(pool):
                pool.memset(prog.ones[:, :], 1.0)
                pool.memset(prog.zeros[:, :], 0.0)
                pool.memset(prog.eps[:, :], RMS_EPS)
                pool.memset(prog.ln_eps[:, :], LN_EPS)
        first_block(prog, xT)
        second_block(prog, xT)
        store(prog, xT, out)
        prog.finish()


INPUTS = ["x", "rel_bias", "norm_mix", "norm_ffn", "w_in", "forget_bias", "qk_gain", "cmp_pos", "cmp_w1", "cmp_w2",
          "sinks", "w_branch", "w_out", "w_gate", "w_up", "conv_w", "conv_b", "w_down", "c_2", "w_ada_2", "b_ada_2",
          "w_in_2", "q_scale_2", "k_scale_2", "sgu_ln_g_2", "sgu_ln_b_2", "w_spatial_2", "b_spatial_2",
          "w_branch_a_2", "w_branch_b_2", "w_out_2", "ln1_g_2", "ln1_b_2", "router_w_2", "router_bias_2", "w_gate_2",
          "w_up_2", "w_down_2", "ws_gate_2", "ws_up_2", "ws_down_2", "ln2_g_2", "ln2_b_2"]


def kernel(**inputs):
    import concourse.bacc as bacc
    from concourse.bass_utils import run_bass_kernel_spmd

    nc = bacc.Bacc("TRN2", target_bir_lowering=False, num_devices=1)
    arrays, dram = {}, {}
    given = {name: np.ascontiguousarray(inputs[name]) for name in INPUTS}
    given.update(shape_constants())
    for name, a in given.items():
        arrays[f"in_{name}_dram"] = a
        dram[name] = nc.dram_tensor(f"in_{name}_dram", a.shape, mybir.dt.from_np(a.dtype), kind="ExternalInput").ap()
    out = nc.dram_tensor("out_0_dram", (1, T, D), F32, kind="ExternalOutput").ap()
    build(nc, dram, out)
    return run_bass_kernel_spmd(nc, [arrays], core_ids=[0]).results[0]["out_0_dram"]
```
